# Optimizing a Trainium2 kernel written in Bass

```python
import jax
import jax.numpy as jnp
from jax import lax
import numpy as np

D_MODEL = 1024
BATCH = 1
SEQ = 256
DEPTH = 2

EPS = 1e-6
NEG_INF = -1e30
FORCE_SCORE = 1e9
HEAD_DIM = 64
ATT_SCALE = HEAD_DIM ** -0.5

NSA_HEADS = 8
NSA_KV_GROUPS = 2
NSA_HPG = NSA_HEADS // NSA_KV_GROUPS
CMP_LEN = 32
CMP_STRIDE = 16
CMP_HIDDEN = 2 * HEAD_DIM
SEL_LEN = 64
SEL_TOPN = 16
WINDOW = 512
NSA_QBLOCK = 64

SB_HEADS = 8
SB_QBLOCK = 128

NSA_Q_W = NSA_HEADS * HEAD_DIM
NSA_KV_W = NSA_KV_GROUPS * HEAD_DIM
NSA_GATE_W = 3 * NSA_HEADS
SB_W = SB_HEADS * HEAD_DIM
ATT_SPLIT_W = [NSA_Q_W] + [NSA_KV_W] * 6 + [NSA_GATE_W] + [SB_W] * 3
ATT_IN_W = sum(ATT_SPLIT_W)
ATT_OUT_W = NSA_Q_W + SB_W

HGRN_EXPAND = 128
HGRN_HEADS = D_MODEL // HGRN_EXPAND
HGRN_DK = HGRN_EXPAND
HGRN_W = HGRN_HEADS * HGRN_DK
HGRN_DV = D_MODEL // HGRN_HEADS
HGRN_CHUNK = 64
REC_IN_W = 2 * HGRN_W + 2 * HGRN_HEADS * HGRN_DV

MOE_GROUPS = 4
MOE_EPG = 8
MOE_EXPERTS = MOE_GROUPS * MOE_EPG
MOE_TOPK = 2
MOE_FF = 256

N_ATT = (DEPTH + 1) // 2
N_REC = DEPTH // 2

kernel_name = 'hybrid_nsa_stickbreak_hgrn2_hmoe'

def rms_norm(x, gain):
    xf = x.astype(jnp.float32)
    y = xf * lax.rsqrt(jnp.mean(xf * xf, axis=-1, keepdims=True) + EPS)
    return (y * gain.astype(jnp.float32)).astype(x.dtype)

def masked_softmax(scores, mask):
    p = jax.nn.softmax(jnp.where(mask, scores, NEG_INF), axis=-1)
    return jnp.where(mask, p, 0.0)

def nsa_compress(kv, pe, w1, w2):
    b, s, g, dh = kv.shape
    n_cmp = (s - CMP_LEN) // CMP_STRIDE + 1
    idx = np.arange(n_cmp)[:, None] * CMP_STRIDE + np.arange(CMP_LEN)[None, :]
    blocks = kv[:, idx] + pe[:, None, :]
    flat = jnp.swapaxes(blocks, 2, 3).reshape(b, n_cmp, g, CMP_LEN * dh)
    return jax.nn.gelu(flat @ w1) @ w2

def selection_cover(s):
    n_cmp = (s - CMP_LEN) // CMP_STRIDE + 1
    c0 = np.arange(n_cmp) * CMP_STRIDE
    s0 = np.arange(s // SEL_LEN) * SEL_LEN
    cover = (c0[:, None] < s0[None, :] + SEL_LEN) & (c0[:, None] + CMP_LEN > s0[None, :])
    return jnp.asarray(cover, jnp.float32)

def nsa_compressed_and_select(q, k_cmp, v_cmp):
    b, s, g, hpg, dh = q.shape
    n_cmp = k_cmp.shape[1]
    n_sel = s // SEL_LEN
    t = jnp.arange(s)
    cmp_end = jnp.arange(n_cmp) * CMP_STRIDE + CMP_LEN - 1
    visible = (cmp_end[None, :] <= t[:, None])[None, :, None, None, :]
    sc = jnp.einsum('bsghd,bcgd->bsghc', q, k_cmp).astype(jnp.float32) * ATT_SCALE
    p = masked_softmax(sc, visible)
    o_cmp = jnp.einsum('bsghc,bcgd->bsghd', p.astype(v_cmp.dtype), v_cmp)
    imp = jnp.einsum('bsghc,cn->bsgn', p, selection_cover(s))
    blk = jnp.arange(n_sel)[None, :]
    t_blk = (t // SEL_LEN)[:, None]
    causal = (blk <= t_blk)[:, None, :]
    forced = causal & ((blk == 0) | (blk == t_blk) | (blk == t_blk - 1))[:, None, :]
    imp = jnp.where(forced, FORCE_SCORE, jnp.where(causal, imp, NEG_INF))
    top_val, top_idx = lax.top_k(imp, min(SEL_TOPN, n_sel))
    return o_cmp, top_idx, top_val > 0.5 * NEG_INF

def nsa_selected_and_window(q, k_slc, v_slc, k_win, v_win, sel_idx, sel_ok):
    b, s, g, hpg, dh = q.shape
    n_sel = s // SEL_LEN
    n_top = sel_idx.shape[-1]
    k_blocks = k_slc.reshape(b, n_sel, SEL_LEN, g, dh).transpose(0, 3, 1, 2, 4)
    v_blocks = v_slc.reshape(b, n_sel, SEL_LEN, g, dh).transpose(0, 3, 1, 2, 4)
    pad = ((0, 0), (WINDOW, 0), (0, 0), (0, 0))
    k_pad = jnp.pad(k_win, pad)
    v_pad = jnp.pad(v_win, pad)
    b_ix = jnp.arange(b)[:, None, None, None]
    g_ix = jnp.arange(g)[None, None, :, None]
    q_offs = jnp.arange(NSA_QBLOCK)
    w_offs = jnp.arange(WINDOW + NSA_QBLOCK) - WINDOW
    l_offs = jnp.arange(SEL_LEN)

    def one_block(q0):
        t = q0 + q_offs
        qb = lax.dynamic_slice_in_dim(q, q0, NSA_QBLOCK, axis=1)
        ib = lax.dynamic_slice_in_dim(sel_idx, q0, NSA_QBLOCK, axis=1)
        okb = lax.dynamic_slice_in_dim(sel_ok, q0, NSA_QBLOCK, axis=1)
        ks = k_blocks[b_ix, g_ix, ib].reshape(b, NSA_QBLOCK, g, n_top * SEL_LEN, dh)
        vs = v_blocks[b_ix, g_ix, ib].reshape(b, NSA_QBLOCK, g, n_top * SEL_LEN, dh)
        kpos = ib[..., None] * SEL_LEN + l_offs
        m_s = ((kpos <= t[None, :, None, None, None]) & okb[..., None]).reshape(b, NSA_QBLOCK, g, n_top * SEL_LEN)
        sc_s = jnp.einsum('bqghd,bqgkd->bqghk', qb, ks).astype(jnp.float32) * ATT_SCALE
        p_s = masked_softmax(sc_s, m_s[:, :, :, None, :])
        o_s = jnp.einsum('bqghk,bqgkd->bqghd', p_s.astype(vs.dtype), vs)
        kw = lax.dynamic_slice_in_dim(k_pad, q0, WINDOW + NSA_QBLOCK, axis=1)
        vw = lax.dynamic_slice_in_dim(v_pad, q0, WINDOW + NSA_QBLOCK, axis=1)
        kpos_w = q0 + w_offs
        m_w = (kpos_w[None, :] <= t[:, None]) & (kpos_w[None, :] > t[:, None] - WINDOW) & (kpos_w[None, :] >= 0)
        sc_w = jnp.einsum('bqghd,bkgd->bqghk', qb, kw).astype(jnp.float32) * ATT_SCALE
        p_w = masked_softmax(sc_w, m_w[None, :, None, None, :])
        o_w = jnp.einsum('bqghk,bkgd->bqghd', p_w.astype(vw.dtype), vw)
        return o_s, o_w

    o_s, o_w = lax.map(one_block, jnp.arange(0, s, NSA_QBLOCK))
    merge = lambda o: jnp.moveaxis(o, 0, 1).reshape(b, s, g, hpg, dh)
    return merge(o_s), merge(o_w)

def stick_breaking_attention(q, k, v):
    b, s, h, dh = q.shape
    kpos = jnp.arange(s)

    def one_block(q0):
        qb = lax.dynamic_slice_in_dim(q, q0, SB_QBLOCK, axis=1)
        t = q0 + jnp.arange(SB_QBLOCK)
        before = kpos[None, :] < t[:, None]
        z = jnp.einsum('bqhd,bkhd->bhqk', qb, k).astype(jnp.float32) * ATT_SCALE
        log_beta = jax.nn.log_sigmoid(z)
        log_keep = jnp.where(before, jax.nn.log_sigmoid(-z), 0.0)
        later = lax.cumsum(log_keep, axis=3, reverse=True) - log_keep
        a = jnp.where(before, jnp.exp(log_beta + later), 0.0)
        return jnp.einsum('bhqk,bkhd->bqhd', a.astype(v.dtype), v)

    o = lax.map(one_block, jnp.arange(0, s, SB_QBLOCK))
    return jnp.moveaxis(o, 0, 1).reshape(b, s, h * dh)

def nsa_stickbreak_mixer(h, w_in, w_out, pe_k, w1_k, w2_k, pe_v, w1_v, w2_v):
    b, s, _ = h.shape
    g, hpg = NSA_KV_GROUPS, NSA_HPG
    parts = jnp.split(h @ w_in, list(np.cumsum(ATT_SPLIT_W)[:-1]), axis=-1)
    q_a, k_c, v_c, k_s, v_s, k_w, v_w, gate, q_b, k_b, v_b = parts
    q_a = q_a.reshape(b, s, g, hpg, HEAD_DIM)
    kvr = lambda a: a.reshape(b, s, g, HEAD_DIM)
    k_c, v_c, k_s, v_s, k_w, v_w = (kvr(a) for a in (k_c, v_c, k_s, v_s, k_w, v_w))
    gate = jax.nn.sigmoid(gate.astype(jnp.float32)).reshape(b, s, 3, g, hpg, 1)
    o_cmp, sel_idx, sel_ok = nsa_compressed_and_select(
        q_a, nsa_compress(k_c, pe_k, w1_k, w2_k), nsa_compress(v_c, pe_v, w1_v, w2_v))
    o_sel, o_win = nsa_selected_and_window(q_a, k_s, v_s, k_w, v_w, sel_idx, sel_ok)
    o_a = gate[:, :, 0] * o_cmp + gate[:, :, 1] * o_sel + gate[:, :, 2] * o_win
    sbr = lambda a: a.reshape(b, s, SB_HEADS, HEAD_DIM)
    o_b = stick_breaking_attention(sbr(q_b), sbr(k_b), sbr(v_b))
    o = jnp.concatenate([o_a.reshape(b, s, NSA_Q_W).astype(h.dtype), o_b.astype(h.dtype)], axis=-1)
    return (o @ w_out).astype(h.dtype)

def hgrn2_recurrence(q, f_logit, v, lb):
    b, s, h, dk = q.shape
    dv = v.shape[-1]
    n_ch = s // HGRN_CHUNK
    q = q.astype(jnp.float32) * (dk ** -0.5)
    v = v.astype(jnp.float32)
    log_f = jnp.logaddexp(jnp.log(lb), jnp.log1p(-lb) + jax.nn.log_sigmoid(f_logit.astype(jnp.float32)))
    k = -jnp.expm1(log_f)
    chunk = lambda a: a.reshape(b, n_ch, HGRN_CHUNK, h, a.shape[-1])
    q, k, v, log_f = chunk(q), chunk(k), chunk(v), chunk(log_f)
    cum = jnp.cumsum(log_f, axis=2)
    ref = cum[:, :, HGRN_CHUNK // 2:HGRN_CHUNK // 2 + 1]
    last = cum[:, :, -1:]
    a = jnp.einsum('bnthd,bnshd->bnhts', q * jnp.exp(cum - ref), k * jnp.exp(ref - cum))
    tri = jnp.asarray(np.tril(np.ones((HGRN_CHUNK, HGRN_CHUNK), dtype=bool)))
    o_intra = jnp.einsum('bnhts,bnshv->bnthv', jnp.where(tri, a, 0.0), v)
    q_in = jnp.moveaxis(q * jnp.exp(cum), 1, 0)
    k_out = jnp.moveaxis(k * jnp.exp(last - cum), 1, 0)
    v_c = jnp.moveaxis(v, 1, 0)
    decay = jnp.moveaxis(jnp.exp(last[:, :, 0]), 1, 0)

    def step(state, xs):
        qc, kc, vc, dc = xs
        o = jnp.einsum('bthd,bhdv->bthv', qc, state)
        state = state * dc[..., None] + jnp.einsum('bshd,bshv->bhdv', kc, vc)
        return state, o

    s0 = jnp.zeros((b, h, dk, dv), jnp.float32)
    _, o_inter = lax.scan(step, s0, (q_in, k_out, v_c, decay))
    o = o_intra + jnp.moveaxis(o_inter, 0, 1)
    return o.reshape(b, s, h, dv)

def hgrn2_mixer(h, w_in, lower_bound, g_norm, w_out):
    b, s, _ = h.shape
    q, f_logit, i, gate = jnp.split(h @ w_in, [HGRN_W, 2 * HGRN_W, 2 * HGRN_W + HGRN_HEADS * HGRN_DV], axis=-1)
    hd = lambda a, d: a.reshape(b, s, HGRN_HEADS, d)
    o = hgrn2_recurrence(hd(q, HGRN_DK), hd(f_logit, HGRN_DK), hd(i, HGRN_DV),
                         lower_bound.reshape(HGRN_HEADS, HGRN_DK))
    o = rms_norm(o, g_norm).reshape(b, s, HGRN_HEADS * HGRN_DV)
    o = o * jax.nn.silu(gate.astype(jnp.float32))
    return (o.astype(h.dtype) @ w_out).astype(h.dtype)

def hier_moe(x, w_grp, b_grp, w_exp, b_exp, w_gate, w_up, w_down):
    b, s, _ = x.shape
    p_grp = jax.nn.softmax((x @ w_grp).astype(jnp.float32) + b_grp, axis=-1)
    g_val, g_idx = lax.top_k(p_grp, 1)
    e_logit = ((x @ w_exp).astype(jnp.float32) + b_exp).reshape(b, s, MOE_GROUPS, MOE_EPG)
    e_logit = jnp.take_along_axis(e_logit, g_idx[..., None], axis=2)[:, :, 0]
    e_val, e_idx = lax.top_k(jax.nn.softmax(e_logit, axis=-1), MOE_TOPK)
    weight = g_val * e_val / jnp.sum(e_val, axis=-1, keepdims=True)
    expert_id = g_idx * MOE_EPG + e_idx
    combine = jnp.sum(jax.nn.one_hot(expert_id, MOE_EXPERTS, dtype=jnp.float32) * weight[..., None], axis=2)

    def per_sequence(args):
        xs, cs = args
        hid = jax.nn.silu(jnp.einsum('sd,edf->sef', xs, w_gate)) * jnp.einsum('sd,edf->sef', xs, w_up)
        return jnp.einsum('sef,efd->sd', hid * cs[..., None], w_down)

    return lax.map(per_sequence, (x, combine.astype(x.dtype))).astype(x.dtype)

def setup_inputs(seed: int = 0) -> dict:
    key = jax.random.key(seed)
    k = jax.random.split(key, 24)

    def dense(kk, shape, fan_in):
        return jax.random.normal(kk, shape, jnp.float32) * (fan_in ** -0.5)

    def gain(kk, shape):
        return 1.0 + 0.02 * jax.random.normal(kk, shape, jnp.float32)

    def small(kk, shape, scale):
        return scale * jax.random.normal(kk, shape, jnp.float32)

    return {
        'x': jax.random.normal(k[0], (BATCH, SEQ, D_MODEL), jnp.float32),
        'norm_mix': gain(k[1], (DEPTH, D_MODEL)),
        'norm_ffn': gain(k[2], (DEPTH, D_MODEL)),
        'att_w_in': dense(k[3], (N_ATT, D_MODEL, ATT_IN_W), D_MODEL),
        'att_w_out': dense(k[4], (N_ATT, ATT_OUT_W, D_MODEL), ATT_OUT_W),
        'cmp_pe_k': small(k[5], (N_ATT, CMP_LEN, HEAD_DIM), 0.02),
        'cmp_w1_k': dense(k[6], (N_ATT, CMP_LEN * HEAD_DIM, CMP_HIDDEN), CMP_LEN * HEAD_DIM),
        'cmp_w2_k': dense(k[7], (N_ATT, CMP_HIDDEN, HEAD_DIM), CMP_HIDDEN),
        'cmp_pe_v': small(k[8], (N_ATT, CMP_LEN, HEAD_DIM), 0.02),
        'cmp_w1_v': dense(k[9], (N_ATT, CMP_LEN * HEAD_DIM, CMP_HIDDEN), CMP_LEN * HEAD_DIM),
        'cmp_w2_v': dense(k[10], (N_ATT, CMP_HIDDEN, HEAD_DIM), CMP_HIDDEN),
        'rec_w_in': dense(k[11], (N_REC, D_MODEL, REC_IN_W), D_MODEL),
        'rec_lb_logits': small(k[12], (DEPTH, HGRN_W), 0.1),
        'rec_gnorm': gain(k[13], (N_REC, HGRN_DV)),
        'rec_w_out': dense(k[14], (N_REC, HGRN_HEADS * HGRN_DV, D_MODEL), HGRN_HEADS * HGRN_DV),
        'moe_w_grp': dense(k[15], (DEPTH, D_MODEL, MOE_GROUPS), D_MODEL),
        'moe_b_grp': small(k[16], (DEPTH, MOE_GROUPS), 0.01),
        'moe_w_exp': dense(k[17], (DEPTH, D_MODEL, MOE_EXPERTS), D_MODEL),
        'moe_b_exp': small(k[18], (DEPTH, MOE_EXPERTS), 0.01),
        'moe_w_gate': dense(k[19], (DEPTH, MOE_EXPERTS, D_MODEL, MOE_FF), D_MODEL),
        'moe_w_up': dense(k[20], (DEPTH, MOE_EXPERTS, D_MODEL, MOE_FF), D_MODEL),
        'moe_w_down': dense(k[21], (DEPTH, MOE_EXPERTS, MOE_FF, D_MODEL), MOE_FF),
        'final_norm': gain(k[22], (D_MODEL,)),
    }

def reference(x, norm_mix, norm_ffn, att_w_in, att_w_out, cmp_pe_k, cmp_w1_k, cmp_w2_k,
              cmp_pe_v, cmp_w1_v, cmp_w2_v, rec_w_in, rec_lb_logits, rec_gnorm, rec_w_out,
              moe_w_grp, moe_b_grp, moe_w_exp, moe_b_exp, moe_w_gate, moe_w_up, moe_w_down,
              final_norm):
    gamma = jnp.cumsum(jax.nn.softmax(rec_lb_logits.astype(jnp.float32), axis=0), axis=0)
    lower_bounds = gamma - gamma[0]
    h = x
    for layer in range(DEPTH):
        j = layer // 2
        hn = rms_norm(h, norm_mix[layer])
        if layer % 2 == 0:
            mix = nsa_stickbreak_mixer(hn, att_w_in[j], att_w_out[j], cmp_pe_k[j], cmp_w1_k[j], cmp_w2_k[j],
                                       cmp_pe_v[j], cmp_w1_v[j], cmp_w2_v[j])
        else:
            mix = hgrn2_mixer(hn, rec_w_in[j], lower_bounds[layer], rec_gnorm[j], rec_w_out[j])
        h = h + mix
        h = h + hier_moe(rms_norm(h, norm_ffn[layer]), moe_w_grp[layer], moe_b_grp[layer], moe_w_exp[layer],
                         moe_b_exp[layer], moe_w_gate[layer], moe_w_up[layer], moe_w_down[layer])
    return rms_norm(h, final_norm)


_drawn_inputs = setup_inputs


def setup_inputs(seed=0):
    import zlib

    import numpy as np

    out = dict(_drawn_inputs(seed))
    spreads = {}
    factors = {'cmp_pe_k': 8.0,
     'cmp_pe_v': 3.072,
     'rec_gnorm': 3.379,
     'moe_b_grp': 2.868,
     'moe_b_exp': 3.361,
     'final_norm': 2.829}
    for name, (base, spread) in spreads.items():
        noise = np.random.default_rng([zlib.crc32(name.encode()), seed]).standard_normal(out[name].shape)
        drawn = base * np.exp(spread * noise) if base else spread * noise
        out[name] = jnp.asarray(drawn.astype(out[name].dtype))
    for name, factor in factors.items():
        out[name] = (out[name] * factor).astype(out[name].dtype)
    return out
```

```python
from contextlib import ExitStack

import concourse.bass as bass
from concourse import mybir

F32 = mybir.dt.float32
I32 = mybir.dt.int32
ALU = mybir.AluOpType
ACT = mybir.ActivationFunctionType
AX = mybir.AxisListType

P = 128
T = 256
TT = T // P
D = 1024
KD = D // P
NL = 2
EPS = 1e-6
NEG = -1e30

DH = 64
NSA_H, NSA_G = 8, 2
HPG = NSA_H // NSA_G
SB_H = 8
CMP_LEN, CMP_STRIDE = 32, 16
NC = (T - CMP_LEN) // CMP_STRIDE + 1
LP = CMP_LEN // 2
GELU_A, GELU_B = 0.7978845608028654, 0.044715

RH, RK, RV, CH = 8, 128, 128, 64
NCH = T // CH

GR, EPG = 4, 8
NE = GR * EPG
FF = 256
KF = FF // P
QE = 4
CAP = P // QE
NQ = NE // QE
PASS_MAX = T // CAP

NU = 6
UW = 4096
UNITS_PER_QUAD = KD // 2 + KF
assert UNITS_PER_QUAD == NU

C_KC, C_VC, C_KS, C_VS, C_KW, C_VW, C_GATE, C_QB = 512, 640, 768, 896, 1024, 1152, 1280, 1304
C_KB, C_VB = C_QB + 512, C_QB + 1024
U_Q, U_KV, U_WG, U_CMP, U_QB, U_KB, U_VB, U_WO = range(8)
ATT_UNITS = 9
REC_UNITS = 10
BASE_MOE = [ATT_UNITS, ATT_UNITS + NQ * NU + REC_UNITS]
BASE_REC = ATT_UNITS + NQ * NU


class Chain:

    def __init__(self, eng, semaphore, base=0):
        self.eng, self.semaphore, self.base, self.n = eng, semaphore, base, 0

    def __call__(self, ins):
        self.n += 1
        ins.then_inc(self.semaphore, 1)
        self.eng.wait_ge(self.semaphore, self.base + self.n)


class Arena:

    def __init__(self, tensor):
        self.tensor, self.at = tensor, 0

    def __call__(self, *shape):
        n = 1
        for s in shape:
            n *= s
        ap = self.tensor[:, self.at:self.at + n]
        self.at += n
        assert self.at <= self.tensor.shape[1], self.at
        if len(shape) == 2:
            return ap.rearrange("p (a b) -> p a b", a=shape[0])
        if len(shape) == 3:
            return ap.rearrange("p (a b c) -> p a b c", a=shape[0], b=shape[1])
        if len(shape) == 4:
            return ap.rearrange("p (a b c d) -> p a b c d", a=shape[0], b=shape[1], c=shape[2])
        return ap


def spread(ap, axis, n):
    a = ap.unsqueeze(axis)
    shape = list(a.shape)
    shape[axis] = n
    return a.broadcast_to(shape)


def hybrid_trunk(nc, x, norm_mix, norm_ffn, att_w_in, att_w_out, cmp_pe_k, cmp_w1_k, cmp_w2_k, cmp_pe_v,
                 cmp_w1_v, cmp_w2_v, rec_w_in, rec_lb_logits, rec_gnorm, rec_w_out, moe_w_grp, moe_b_grp,
                 moe_w_exp, moe_b_exp, moe_w_gate, moe_w_up, moe_w_down, final_norm, out):
    ctx = ExitStack()
    with ctx:
        def sb(name, shape, dt=F32):
            return ctx.enter_context(nc.sbuf_tensor(name, shape, dt))

        class Signals(dict):
            def __missing__(self, name):
                self[name] = ctx.enter_context(nc.semaphore(name))
                return self[name]

        s = Signals()

        SB_BANKS = (4, 5, 0, 1)

        expert_rows = [nc.dram_tensor(f"expert_rows{l}", [2 * T, D], F32, kind="Internal").ap()
                       for l in range(NL)]

        ring = sb("ring", [P, NU, UW])
        h = sb("h", [P, TT, D])
        xg = sb("xg", [P, TT, D])
        xT = sb("xT", [P, KD, T])
        gain = sb("gain", [P, D])
        ident = sb("ident", [P, P])
        ones = sb("ones", [P, P])
        earlier = sb("earlier", [P, P])
        iota_slot = sb("iota_slot", [P, CAP])
        iota_exp = sb("iota_exp", [P, NE])
        token_row = sb("token_row", [P, TT])
        slot_expert = sb("slot_expert", [P, QE])
        iota_i = sb("iota_i", [P, NE], I32)
        token_i = sb("token_i", [P, TT], I32)
        norm_sum = sb("norm_sum", [P, 2 * NL + 1, TT])
        norm_rstd = sb("norm_rstd", [P, 2 * NL + 1, TT])
        eps_col = sb("eps_col", [P, 1])
        w_route = sb("w_route", [P, KD, GR + NE])
        b_route = sb("b_route", [P, GR + NE])
        logit = sb("logit", [P, TT, GR + NE])
        route_t = sb("route_t", [P, 4, TT, NE])
        route_s = sb("route_s", [P, 16, TT])
        chosen = sb("chosen", [P, 2, TT, NE])
        member = sb("member", [P, TT, NE])
        slot_of = sb("slot_of", [P, TT, NE])
        row_of = sb("row_of", [P, TT, NE])
        weight = sb("weight", [P, 2, TT])
        passes_f = sb("passes_f", [P, PASS_MAX])
        passes = [sb(f"passes{l}", [1, 1], I32) for l in range(NL)]
        lb_rows = sb("lb_rows", [P, P])[:, :]
        gnorm = sb("gnorm", [P, RV])[:, :]
        arena_t = sb("arena", [P, 19600])

        psum = ctx.enter_context(nc.psum_tensor("psum", [P, 8, 512], F32))

        def bank(b):
            return psum[:, b, :]

        a = Arena(arena_t)
        qT = a(4, T)
        kv2 = a(2, NSA_G + 1, T)
        ksw = a(2, T)
        vsw = a(TT, 280)
        qbT = a(4, T)
        kbT = a(4, T)
        vb = a(TT, SB_H * DH)
        scores = a(2, HPG, T)
        probsT = a(2, TT, 512)
        oT = a(8, T)
        w2 = a(2, DH)
        pe_rows = a(2, P)
        causal = a(2, P)
        cmp_bias = a(2)
        cmp_x = a(2, 2 * NC)
        cmp_g = a(2, 2 * NC)
        cmp_h = a(2, 2 * NC)
        hv4 = a(NSA_G, 4, 32)
        kcT = a(NC)
        vc4 = a(NSA_G, DH)
        cmask = a(TT, NC)
        cvis = a(TT, NC)
        cs = a(TT, NSA_H, NC)
        cp = a(TT, NSA_H, 32)
        pcT = a(NSA_G, T)
        gates = a(TT, 3 * NSA_H)
        cstat = a(4, TT * NSA_H)
        stat = a(2, 4, HPG)
        ztmp = a(3, 384)
        zt = a(3, 384)
        before_query = a(P)
        za = a(2, 384)
        later_own = a(P)
        later_all = a(P)
        square = qbT.rearrange("p h t -> p (h t)")
        att_end = a.at

        a = Arena(arena_t)
        rA, rB, rC, rD, rQ, r1, r2, r3 = (a(RH, T) for _ in range(8))
        rv = a(TT, D)
        rg = xg
        reset = gain[:, :]
        last_state = a(RH * RV)
        states = [xT[:, 0:4, :].rearrange("p k t -> p (k t)"), xT[:, 4:8, :].rearrange("p k t -> p (k t)"),
                  last_state]
        decay = a(RH, NCH)
        lb = a(2 * RH)
        lbt = a(4, RH)
        ostat = a(3, TT * RH)
        rec_end = a.at
        koR = rC.rearrange("p h t -> p (h t)").rearrange("p (t d) -> p t d", t=TT)
        aM = rA
        o_rows = r1.rearrange("p h t -> p (h t)").rearrange("p (t d) -> p t d", t=TT)
        e_gate = r2.rearrange("p h t -> p (h t)").rearrange("p (t d) -> p t d", t=TT)
        recT = rB
        square_rec = rQ.rearrange("p h t -> p (h t)")[:, 0:D]

        a = Arena(arena_t)
        slots = a(TT, QE, CAP)
        gatheredT = a(KD, P)
        egate = a(FF)
        hid_t = a(FF)
        hid = a(FF)
        hidT = a(KF, P)
        y_rows = a(D)
        y_pair = a(2, TT, D)
        idx_t = a(8)
        square_moe = a(D)
        moe_end = a.at
        idx_i = sb("idx_i", [P, 1], I32)

        block = ctx.enter_context(nc.Block())

        def slot_use(u, n=0):
            return u % NU, u // NU + 1 + n

        def load_unit(sp, u, parts, n=0, more=False):
            if u >= NU:
                sp.wait_ge(s["unit_used"], (u - NU + 1) + (NU * n if more else 0))
            slot = u % NU
            for i, (dst, src) in enumerate(parts):
                arrived = s[f"unit{slot}_loaded"] if i < 2 else s["cmp_w1_rest"]
                if i == 1 and u >= 1:
                    sp.wait_ge(s[f"unit{(u - 1) % NU}_loaded"], 32 * ((u - 1) // NU + 1 + n))
                sp.dma_start(dst(ring[:, slot, :]), src).then_inc(arrived, 16)

        def cols(w, c0, n):
            v = w.rearrange("(p k) n -> p k n", k=KD)[:, :, c0:c0 + n]
            half = KD // 2
            return [(lambda r, i=i: r[:, 0:KD * n].rearrange("p (k n) -> p k n", k=KD)[:, i * half:(i + 1) * half, :],
                     v[:, i * half:(i + 1) * half, :]) for i in range(2)]

        def out_cols(w, c0):
            v = w.rearrange("(j p) n -> p j n", p=P)[:, :, c0:c0 + 512]
            return [(lambda r, i=i: r.rearrange("p (j n) -> p j n", n=512)[:, 4 * i:4 * i + 4, :],
                     v[:, 4 * i:4 * i + 4, :]) for i in range(2)]

        def quad_units(l, q):
            wg = moe_w_gate[l].rearrange("(q e) (p c r) f -> q c p e (r f)", e=QE, p=P, c=KD // 2)
            wu = moe_w_up[l].rearrange("(q e) (p c r) f -> q c p e (r f)", e=QE, p=P, c=KD // 2)
            wd = moe_w_down[l].rearrange("(q e) (p j) n -> q j p e n", e=QE, j=KF)
            for c in range(KD // 2):
                yield [(lambda r, i=i: r.rearrange("p (w e f) -> p w e f", w=2, e=QE)[:, i], w[q][c])
                       for i, w in enumerate((wg, wu))]
            for j in range(KF):
                v = wd[q][j]
                yield [(lambda r, i=i: r.rearrange("p (e n) -> p e n", e=QE)[:, 2 * i:2 * i + 2],
                        v[:, 2 * i:2 * i + 2]) for i in range(2)]

        @block.sync
        def _(sp):
            for t in range(TT):
                sp.dma_start(h[:, t, :], x[0, t * P:(t + 1) * P, :]).then_inc(s["x_loaded"], 16)
            att, w_out = att_w_in[0], att_w_out[0]
            plan = [cols(att, 0, 512), cols(att, C_KC, 512), cols(att, C_KW, 280),
                    [(lambda r, i=i, odd=odd: r.rearrange("p (w j n) -> p w j n", w=2, n=P)[odd * DH:(odd + 1) * DH, i],
                      w[0].rearrange("(j odd d) n -> odd d j n", odd=2, d=DH)[odd])
                     for i, w in enumerate((cmp_w1_k, cmp_w1_v)) for odd in range(2)],
                    cols(att, C_QB, 512), cols(att, C_KB, 512), cols(att, C_VB, 512),
                    out_cols(w_out, 0), out_cols(w_out, 512)]
            assert len(plan) == ATT_UNITS
            for u, parts in enumerate(plan):
                load_unit(sp, u, parts)

            rec, w_out = rec_w_in[0], rec_w_out[0]
            plan_rec = [cols(rec, c, 512) for c in (1024, 1536, 0, 512, 2048, 2560, 3072, 3584)]
            plan_rec += [out_cols(w_out, 0), out_cols(w_out, 512)]
            assert len(plan_rec) == REC_UNITS

            before = 0
            for l in range(NL):
                if l:
                    for i, parts in enumerate(plan_rec):
                        load_unit(sp, BASE_REC + i, parts, before, True)
                with sp.Fori(0, NQ) as q:
                    for i, parts in enumerate(quad_units(l, q)):
                        load_unit(sp, BASE_MOE[l] + i, parts, q + before, True)
                sp.wait_ge(s["passes_ready"], l + 1)
                more = sp.value_load(passes[l][0:1, 0:1], min_val=0, max_val=PASS_MAX - 1)
                with sp.If(more > 0):
                    with sp.Fori(0, more) as r:
                        with sp.Fori(0, NQ) as q:
                            for i, parts in enumerate(quad_units(l, q)):
                                load_unit(sp, BASE_MOE[l] + i, parts, q + NQ * (r + 1) + before, True)
                before = before + NQ * more
            for t in range(TT):
                sp.wait_ge(s["xg_done"], 2 * 2 * NL + t + 1)
                sp.dma_start(out[0, t * P:(t + 1) * P, :], xg[:, t, :]).then_inc(s["out_done"], 16)
            sp.wait_ge(s["out_done"], 16 * TT)

        @block.gpsimd
        def _(pool):
            link = Chain(pool, s["pool_chain"])

            def gain_load(v):
                src = [norm_mix[0], norm_ffn[0], norm_mix[1], norm_ffn[1], final_norm][v]
                if v:
                    pool.wait_ge(s["xg_done"], TT * v)
                pool.dma_start(gain[:, :], src.partition_broadcast(P)).then_inc(s["gain_loaded"], 16)

            def route_load(l):
                if l:
                    pool.wait_ge(s["route_used"], l)
                pool.dma_start(w_route[:, :, 0:GR], moe_w_grp[l].rearrange("(p k) n -> p k n", k=KD))\
                    .then_inc(s["route_loaded"], 16)
                pool.dma_start(w_route[:, :, GR:], moe_w_exp[l].rearrange("(p k) n -> p k n", k=KD))\
                    .then_inc(s["route_loaded"], 16)
                pool.dma_start(b_route[:, 0:GR], moe_b_grp[l].partition_broadcast(P))\
                    .then_inc(s["route_loaded"], 16)
                pool.dma_start(b_route[:, GR:], moe_b_exp[l].partition_broadcast(P))\
                    .then_inc(s["route_loaded"], 16)

            link(pool.memset(ident[:, :], 0.0))
            pool.affine_select(out=ident[:, :], in_=ident[:, :], compare_op=ALU.not_equal, fill=1.0, base=0,
                               pattern=[[-1, P]], channel_multiplier=1).then_inc(s["ident_done"], 1)
            pool.memset(eps_col[:, :], EPS).then_inc(s["eps_done"], 1)
            pool.memset(kv2[:, :, NSA_G, :], 0.0).then_inc(s["kv2_zero"], 1)
            route_load(0)

            for l in range(NL):
                pool.sem_inc(s[f"rows_free{l}"], 1)
                pool.sem_inc(s[f"y_rows{l}"], 2)

            link(pool.memset(causal[:, :, :], 0.0))
            link(pool.affine_select(out=causal[:, 1, :], in_=causal[:, 1, :], compare_op=ALU.is_ge, fill=NEG,
                                    base=0, pattern=[[-1, P]], channel_multiplier=1))
            link(pool.memset(cmask[:, :, :], 0.0))
            link(pool.memset(cvis[:, :, :], 1.0))
            for dst, fill in ((cmask, NEG), (cvis, 0.0)):
                link(pool.affine_select(out=dst[:, :, :], in_=dst[:, :, :], compare_op=ALU.is_ge, fill=fill,
                                        base=1 - CMP_LEN, pattern=[[P, TT], [-CMP_STRIDE, NC]],
                                        channel_multiplier=1))
            link(pool.memset(later_all[:, :], -1.0))
            link(pool.affine_select(out=later_own[:, :], in_=later_all[:, :], compare_op=ALU.is_ge, fill=0.0,
                                    base=0, pattern=[[-1, P]], channel_multiplier=1))
            link(pool.memset(cp[:, :, :, :], 0.0))
            link(pool.memset(hv4[:, :, :, :], 0.0))
            link(pool.memset(ones[:, :], 1.0))
            link(pool.affine_select(out=earlier[:, :], in_=ones[:, :], compare_op=ALU.is_gt, fill=0.0, base=0,
                                    pattern=[[1, P]], channel_multiplier=-1))
            link(pool.iota(iota_i[:, :], pattern=[[1, NE]], base=0, channel_multiplier=0))
            link(pool.tensor_copy(iota_exp[:, :], iota_i[:, :]))
            link(pool.tensor_copy(iota_slot[:, :], iota_i[:, 0:CAP]))
            link(pool.iota(token_i[:, :], pattern=[[P, TT]], base=1, channel_multiplier=1))
            link(pool.tensor_copy(token_row[:, :], token_i[:, :]))
            link(pool.memset(slot_expert[:, :], 1.0))
            link(pool.affine_select(out=slot_expert[:, :], in_=slot_expert[:, :], compare_op=ALU.is_ge, fill=0.0,
                                    base=0, pattern=[[-CAP, QE]], channel_multiplier=1))
            link(pool.affine_select(out=slot_expert[:, :], in_=slot_expert[:, :], compare_op=ALU.is_ge, fill=0.0,
                                    base=CAP - 1, pattern=[[CAP, QE]], channel_multiplier=-1))
            link(pool.memset(before_query, 0.0))
            pool.affine_select(out=before_query, in_=before_query, compare_op=ALU.is_gt, fill=NEG, base=0,
                               pattern=[[1, P]], channel_multiplier=-1).then_inc(s["const_done"], 1)

            def scatter(l, n):
                pool.wait_ge(s[f"y_rows{l}"], 2 * n + 4)
                pool.wait_ge(s[f"row_index{l}"], n + 1)
                pool.sem_inc(s["scatters_begun"], 1)
                pool.indirect_dma_start(out=expert_rows[l],
                                        out_offset=bass.IndirectOffsetOnAxis(ap=idx_i[:, 0:1], axis=0),
                                        in_=y_rows, in_offset=None, bounds_check=2 * T - 1, oob_is_err=False)\
                    .then_inc(s[f"rows_out{l}"], 16)
                pool.wait_ge(s[f"rows_out{l}"], 16 * n + 16)
                pool.sem_inc(s[f"rows_free{l}"], 1)

            def experts(l):
                with pool.Fori(0, NQ) as q:
                    scatter(l, q)
                pool.wait_ge(s["passes_ready"], l + 1)
                more = pool.value_load(passes[l][0:1, 0:1], min_val=0, max_val=PASS_MAX - 1)
                with pool.If(more > 0):
                    with pool.Fori(0, more) as r:
                        with pool.Fori(0, NQ) as q:
                            scatter(l, q + NQ * (r + 1))

            gain_load(1)
            gain_load(2)
            experts(0)

            rlink = Chain(pool, s["pool_rec_chain"])
            pool.wait_ge(s["xg_done"], 3 * TT)
            rlink(pool.memset(reset, 1.0))
            pool.memset(reset.rearrange("p (c i) -> p c i", i=CH)[:, :, 0:1], 0.0).then_inc(s["rec_const"], 1)
            route_load(1)
            for hh in range(2):
                sl = slice(4 * hh, 4 * hh + 4)
                cum = rB[:, sl, :].rearrange("p h (c i) -> p (h c) i", i=CH)
                pool.wait_ge(s["rec_cum"], hh + 1)
                pool.tensor_tensor(rD[:, sl, :].rearrange("p h (c i) -> p (h c) i", i=CH),
                                   cum[:, :, CH - 1:CH].broadcast_to([P, 4 * NCH, CH]), cum, ALU.subtract)\
                    .then_inc(s["rec_left"], 1)
            gain_load(3)
            for hh in range(2):
                sl = slice(4 * hh, 4 * hh + 4)
                pool.wait_ge(s["rec_exps"], 4 * hh + 4)
                pool.tensor_tensor(rD[:, sl, :], rD[:, sl, :], rA[:, sl, :], ALU.mult)\
                    .then_inc(s["rec_kout"], 1)
                pool.tensor_tensor(r2[:, sl, :], r2[:, sl, :], rA[:, sl, :], ALU.mult)\
                    .then_inc(s["rec_kin"], 1)
            pool.wait_ge(s["rec_kout"], 2)
            pool.wait_ge(s["rec_kin"], 2)
            pool.wait_ge(s["rec_kout_read"], 1)
            aMv = aM.rearrange("p h t -> p (h t)").rearrange("p (g t) -> p g t", t=P)
            pool.memset(aMv[0:CH, :, CH:P], 0.0).then_inc(s["rec_zero"], 1)
            pool.memset(aMv[CH:P, :, 0:CH], 0.0).then_inc(s["rec_zero"], 1)
            pool.wait_ge(s["rec_zero"], 2)
            for b in range(4):
                pool.wait_ge(s["rec_a_copied"], 2 * b + 2)
                v = aMv[:, 4 * b:4 * b + 4, :]
                pool.affine_select(out=v, in_=v, compare_op=ALU.is_ge, fill=0.0, base=0,
                                   pattern=[[0, 4], [1, P]], channel_multiplier=-1)\
                    .then_inc(s["rec_a_masked"], 1)
            gain_load(4)
            experts(1)

        H_NEEDED = [None, (2, 4), (5, 6), (8, 10), (11, 12)]

        @block.scalar
        def _(act):
            link = Chain(act, s["act_chain"])

            def norm(v, t, buf):
                if v == 0:
                    act.wait_ge(s["x_loaded"], 32)
                    act.wait_ge(s["eps_done"], 1)
                else:
                    act.wait_ge(s["h_done"], H_NEEDED[v][t])
                link(act.activation(buf, h[:, t, :], ACT.Square, accum_out=norm_sum[:, v, t:t + 1]))
                link(act.activation(norm_sum[:, v, t:t + 1], norm_sum[:, v, t:t + 1], ACT.Ln,
                                    bias=eps_col[:, 0:1], scale=1.0 / D))
                act.activation(norm_rstd[:, v, t:t + 1], norm_sum[:, v, t:t + 1], ACT.Exp, scale=-0.5)\
                    .then_inc(s["norm_rstd"], 1)

            def xT_half(v, t):
                act.wait_ge(s["xT_psum"], 4 * v + 2 * t + 1)
                act.activation(xT[:, 0:4, t * P:(t + 1) * P],
                               bank(2 * t).rearrange("p (k t) -> p k t", k=4), ACT.Copy)\
                    .then_inc(s["xT_done"], 1)

            act.preload_act_table_set("natural_log_exp_and_others")
            act.dma_start(gain[:, :], norm_mix[0].partition_broadcast(P)).then_inc(s["gain_first"], 16)
            for i, pe in enumerate((cmp_pe_k, cmp_pe_v)):
                act.dma_start(pe_rows[0:LP, i, :], pe[0].rearrange("(j two) d -> j (two d)", two=2))\
                    .then_inc(s["cmp_small"], 16)
            for i, w in enumerate((cmp_w2_k, cmp_w2_v)):
                act.dma_start(w2[:, i, :], w[0]).then_inc(s["cmp_small"], 16)
            act.dma_start(lb_rows[0:2 * RH, :], rec_lb_logits.rearrange("l (h p) -> (l h) p", p=RK))\
                .then_inc(s["rec_small"], 16)
            act.dma_start(gnorm[:, :], rec_gnorm[0].partition_broadcast(P)).then_inc(s["rec_small"], 16)
            for t in range(TT):
                norm(0, t, square)
            for t in range(TT):
                xT_half(0, t)

            def proj(n):
                act.wait_ge(s["proj_psum"], n + 1)
                src = bank(n % 2)
                if n == 0:
                    act.activation(qT[:, 0:2, :], src.rearrange("p (a t) -> p a t", a=2), ACT.Copy,
                                   scale=DH ** -0.5).then_inc(s["proj_even"], 1)
                elif n == 2:
                    last = None
                    for kv in range(2):
                        for g in range(NSA_G):
                            part = bank(0)[g * DH:(g + 1) * DH, kv * T:(kv + 1) * T]
                            act.activation(kv2[0:DH, kv, g, :], part, ACT.Copy).then_inc(s["kv2_done"], 1)
                            last = act.activation(kv2[DH:P, kv, g, 0:T - 1], part[:, 1:T], ACT.Copy)
                            if (kv, g) != (1, 1):
                                last.then_inc(s["kv2_done"], 1)
                    last.then_inc(s["proj_even"], 1)
                elif n == 4:
                    act.activation(vsw[:, 0, :], src[:, 0:280], ACT.Copy).then_inc(s["proj_even"], 1)
                elif n == 6:
                    act.activation(qbT[:, 0:2, :], src.rearrange("p (a t) -> p a t", a=2), ACT.Copy,
                                   scale=DH ** -0.5).then_inc(s["proj_even"], 1)
                elif n == 8:
                    act.activation(kbT[:, 0:2, :], src.rearrange("p (a t) -> p a t", a=2), ACT.Copy)\
                        .then_inc(s["proj_even"], 1)
                elif n == 10:
                    act.activation(vb[:, 0, :], src, ACT.Copy).then_inc(s["proj_even"], 1)

            proj(0)
            proj(2)
            act.wait_ge(s["cmp_inner"], 1)
            act.activation(cmp_g, cmp_g, ACT.Exp, scale=-2.0 * GELU_A).then_inc(s["cmp_exp"], 1)
            proj(4)
            act.wait_ge(s["cmp_kv"], 1)
            act.activation(kcT[0:DH, :], bank(5)[0:DH, 0:NC], ACT.Copy).then_inc(s["cmp_kv_done"], 1)
            act.activation(kcT[DH:P, :], bank(5)[0:DH, NC:2 * NC], ACT.Copy).then_inc(s["cmp_kv_done"], 1)
            act.activation(vc4, bank(5)[:, 64:192].rearrange("p (g d) -> p g d", g=2), ACT.Copy)\
                .then_inc(s["cmp_kv_done"], 1)
            act.wait_ge(s["proj_even"], 3)
            act.wait_ge(s["proj_odd"], 3)
            act.activation(gates, vsw[:, :, C_GATE - C_KW:280], ACT.Exp, scale=-1.0)\
                .then_inc(s["gate_exp"], 1)
            act.wait_ge(s["cmp_shifted"], 1)
            act.activation(cs, cs, ACT.Exp).then_inc(s["cmp_probs"], 1)

            def exps(u):
                nk = P * (u // 4 + 1)
                act.wait_ge(s["nsa_max"], u + 1)
                for i in range(HPG):
                    v = scores[:, u % 2, i, 0:nk]
                    act.activation(v, v, ACT.Exp, bias=stat[:, u % 2, 0, i:i + 1],
                                   accum_out=stat[:, u % 2, 1, i:i + 1]).then_inc(s["nsa_exp"], 1)

            exps(0)
            for u in range(8):
                if u + 1 < 8:
                    exps(u + 1)
                if 6 + u in (6, 8, 10):
                    proj(6 + u)
                if u == 0:
                    act.wait_ge(s["cmp_pT"], 1)
                    act.activation(pcT, bank(5).rearrange("p (g t) -> p g t", g=2), ACT.Copy)\
                        .then_inc(s["cmp_pT_done"], 1)
                act.wait_ge(s["nsa_pT"], u + 1)
                if u >= 2:
                    act.wait_ge(s["nsa_pv"], u - 1)
                act.activation(probsT[:, u % 2, 0, :], bank(2), ACT.Copy).then_inc(s["nsa_pT_even"], 1)

            def exp_ln(hd):
                act.wait_ge(s["sb_z"], hd + 1)
                if hd >= 3:
                    act.wait_ge(s["sb_t"], hd - 2)
                v = ztmp[:, hd % 3, :]
                link(act.activation(v, bank(SB_BANKS[hd % 4])[:, 0:384], ACT.Abs))
                link(act.activation(v, v, ACT.Exp, scale=-1.0))
                act.activation(v, v, ACT.Ln, bias=1.0).then_inc(s["sb_ln"], 1)

            exp_ln(0)
            act.wait_ge(s["nsa_pv"], 8)
            for g in range(NSA_G):
                act.activation(oT[:, 2 * g:2 * g + 2, :], bank(6 + g).rearrange("p (a t) -> p a t", a=2), ACT.Copy)\
                    .then_inc(s["oT_done"], 1)
            for hd in range(SB_H):
                if hd + 1 < SB_H:
                    exp_ln(hd + 1)
                act.wait_ge(s["sb_e"], hd + 1)
                if hd >= 2:
                    act.wait_ge(s["sb_pv"], hd - 1)
                act.activation(za[:, hd % 2, :], bank(SB_BANKS[hd % 4])[:, 0:384], ACT.Exp).then_inc(s["sb_a"], 1)

            def route(l):
                act.wait_ge(s["route_diff"], l + 1)
                for t in range(TT):
                    act.activation(route_t[:, 3, t, 0:GR], logit[:, t, 0:GR], ACT.Exp,
                                   bias=route_s[:, 0, t:t + 1], accum_out=route_s[:, 1, t:t + 1])\
                        .then_inc(s["route_exp"], 1)
                act.activation(route_s[:, 5, :], route_s[:, 4, :], ACT.Exp).then_inc(s["route_exp"], 1)

            def quad(l, n):
                act.wait_ge(s[f"gathered{l}"], 2 * n + 1)
                act.activation(gatheredT[:, 0:4, :], bank(0).rearrange("p (k c) -> p k c", k=4), ACT.Copy)\
                    .then_inc(s[f"gatheredT{l}"], 1)
                act.wait_ge(s[f"gate_up{l}"], n + 1)
                act.activation(egate, bank(3)[:, 0:FF], ACT.Exp, scale=-1.0).then_inc(s[f"egate{l}"], 1)
                act.wait_ge(s[f"hid_psum{l}"], n + 1)
                act.activation(hidT, bank(4)[:, 0:FF].rearrange("p (j c) -> p j c", j=KF), ACT.Copy)\
                    .then_inc(s[f"hidT{l}"], 1)
                act.wait_ge(s[f"down{l}"], n + 1)
                act.wait_ge(s[f"rows_free{l}"], n + 1)
                act.activation(y_rows[:, 0:512], bank(5), ACT.Copy).then_inc(s[f"y_rows{l}"], 1)

            def experts(l):
                route(l)
                with act.Fori(0, NQ) as q:
                    quad(l, q)
                act.wait_ge(s["passes_ready"], l + 1)
                more = act.value_load(passes[l][0:1, 0:1], min_val=0, max_val=PASS_MAX - 1)
                with act.If(more > 0):
                    with act.Fori(0, more) as r:
                        with act.Fori(0, NQ) as q:
                            quad(l, q + NQ * (r + 1))
                act.wait_ge(s[f"rows_free{l}"], NQ + 1 + NQ * more)
                for t in range(TT):
                    for k in range(2):
                        act.dma_start(y_pair[:, k, t, :], expert_rows[l][k * T + t * P:k * T + (t + 1) * P, :])\
                            .then_inc(s[f"rows_in{t}"], 16)

            def norm_and_xT(v):
                for t in range(TT):
                    norm(v, t, square_moe)
                    xT_half(v, t)

            norm_and_xT(1)
            experts(0)

            norm_and_xT(2)
            act.wait_ge(s["lb_diff"], 1)
            act.activation(lbt[:, 0:2, :], lbt[:, 0:2, :], ACT.Exp).then_inc(s["lb_exp"], 1)
            for m in range(4):
                act.wait_ge(s["rec_psum"], m + 1)
                act.activation(rA[:, 2 * m:2 * m + 2, :], bank(m).rearrange("p (a t) -> p a t", a=2), ACT.Exp)\
                    .then_inc(s["rec_f"], 1)
            for hh in range(2):
                sl = slice(4 * hh, 4 * hh + 4)
                act.wait_ge(s["rec_key"], hh + 1)
                act.activation(rC[:, sl, :], rA[:, sl, :], ACT.Ln, bias=1.0, scale=-1.0)\
                    .then_inc(s["rec_logf"], 1)
            for hh in range(2):
                sl = slice(4 * hh, 4 * hh + 4)
                act.wait_ge(s["rec_cum"], hh + 1)
                act.activation(r3[:, sl, :], rB[:, sl, :], ACT.Exp).then_inc(s["rec_exps"], 1)
                act.wait_ge(s["rec_rel"], hh + 1)
                act.activation(r1[:, sl, :], rC[:, sl, :], ACT.Exp).then_inc(s["rec_exps"], 1)
                act.activation(r2[:, sl, :], rC[:, sl, :], ACT.Exp, scale=-1.0).then_inc(s["rec_exps"], 1)
                act.wait_ge(s["rec_left"], hh + 1)
                act.activation(rD[:, sl, :], rD[:, sl, :], ACT.Exp).then_inc(s["rec_exps"], 1)
            for m in range(8, 12):
                act.wait_ge(s["rec_psum"], m + 1)
                act.activation(rv[:, (m - 8) % 2, (m - 8) // 2 * 512:(m - 8) // 2 * 512 + 512], bank(m % 4),
                               ACT.Copy).then_inc(s["rec_v"], 1)
            for b in (0, 2):
                act.wait_ge(s["ko_psum"], b + 1)
                act.activation(koR[:, b // 2, (b % 2) * 512:(b % 2) * 512 + 512], bank(b), ACT.Copy)\
                    .then_inc(s["ko_done"], 1)
            aMv = aM.rearrange("p h t -> p (h t)").rearrange("p (g t) -> p g t", t=P)
            act.wait_ge(s["rec_zero"], 2)
            for b in range(4):
                act.wait_ge(s["a_psum"], b + 1)
                for lo in (0, CH):
                    act.activation(aMv[lo:lo + CH, 4 * b:4 * b + 4, lo:lo + CH],
                                   bank(4 + b)[lo:lo + CH, :].rearrange("p (g t) -> p g t", g=4)[:, :, lo:lo + CH],
                                   ACT.Copy).then_inc(s["rec_a_copied"], 1)
            act.wait_ge(s["rec_kin_used"], 1)
            for m in range(12, 16):
                act.wait_ge(s["rec_gate"], m - 11)
                i = m - 12
                c = slice(i // 2 * 512, i // 2 * 512 + 512)
                act.activation(e_gate[:, i % 2, c], rg[:, i % 2, c], ACT.Exp, scale=-1.0)\
                    .then_inc(s["rec_gate_exp"], 1)
            for t in range(TT):
                act.wait_ge(s["o_psum"], t + 1)
                o_ps = psum[:, 4 + 2 * t:6 + 2 * t, :].rearrange("p b n -> p (b n)")
                act.activation(square_rec, o_ps, ACT.Square).then_inc(s["o_square"], 1)
                act.wait_ge(s["o_sum"], t + 1)
                v = ostat[:, 0, t * RH:(t + 1) * RH]
                link(act.activation(v, v, ACT.Ln, bias=eps_col[:, 0:1], scale=1.0 / RV))
                act.activation(ostat[:, 1, t * RH:(t + 1) * RH], v, ACT.Exp, scale=-0.5)\
                    .then_inc(s["o_rstd"], 1)
            for b in (0, 2):
                act.wait_ge(s["recT_psum"], b + 1)
                act.activation(recT[:, 4 * (b % 2):4 * (b % 2) + 4, (b // 2) * P:(b // 2 + 1) * P],
                               bank(b).rearrange("p (k t) -> p k t", k=4), ACT.Copy).then_inc(s["recT_done"], 1)

            norm_and_xT(3)
            experts(1)
            for t in range(TT):
                norm(4, t, square_moe)

        @block.vector
        def _(dve):
            link = Chain(dve, s["dve_chain"])

            def norm(v, t):
                dve.wait_ge(s["norm_rstd"], TT * v + t + 1)
                if v == 0:
                    dve.wait_ge(s["gain_first"], 16)
                else:
                    dve.wait_ge(s["gain_loaded"], 16 * v)
                dve.scalar_tensor_tensor(out=xg[:, t, :], in0=h[:, t, :], scalar=norm_rstd[:, v, t:t + 1],
                                         in1=gain[:, :], op0=ALU.mult, op1=ALU.mult)\
                    .then_inc(s["xg_done"], 1)

            def xT_half(v, t):
                dve.wait_ge(s["xT_psum"], 4 * v + 2 * t + 2)
                dve.tensor_copy(xT[:, 4:8, t * P:(t + 1) * P],
                                bank(2 * t + 1).rearrange("p (k t) -> p k t", k=4)).then_inc(s["xT_done"], 1)

            for t in range(TT):
                norm(0, t)
            for t in range(TT):
                xT_half(0, t)

            def proj(n):
                dve.wait_ge(s["proj_psum"], n + 1)
                src = bank(n % 2)
                pair = src.rearrange("p (a t) -> p a t", a=2)
                if n in (1, 7):
                    dst = (qT if n == 1 else qbT)[:, 2:4, :]
                    ins = dve.tensor_scalar(dst, pair, DH ** -0.5, None, ALU.mult)
                elif n == 3:
                    ins = dve.tensor_copy(ksw, pair)
                elif n == 5:
                    ins = dve.tensor_copy(vsw[:, 1, :], src[:, 0:280])
                elif n == 9:
                    ins = dve.tensor_copy(kbT[:, 2:4, :], pair)
                else:
                    ins = dve.tensor_copy(vb[:, 1, :], src)
                ins.then_inc(s["proj_odd"], 1)

            dve.wait_ge(s["pe_psum"], 1)
            dve.wait_ge(s["kv2_zero"], 1)
            dve.tensor_copy(kv2[:, :, NSA_G, 0:CMP_LEN:2], bank(5)[:, 0:2 * LP].rearrange("p (a j) -> p a j", a=2))\
                .then_inc(s["pe_done"], 1)
            proj(1)
            proj(3)
            dve.wait_ge(s["cmp_hidden"], 1)
            hidden = bank(4)[:, 0:P].rearrange("p (a n) -> p a n", a=2)
            link(dve.tensor_copy(cmp_bias, hidden[:, :, NSA_G * NC]))
            for kv in range(2):
                link(dve.tensor_scalar(cmp_x[:, kv, :], hidden[:, kv, 0:NSA_G * NC],
                                       cmp_bias[:, kv:kv + 1], None, ALU.add))
            link(dve.tensor_tensor(cmp_g, cmp_x, cmp_x, ALU.mult))
            link(dve.tensor_scalar(cmp_g, cmp_g, GELU_B, 1.0, ALU.mult, ALU.add))
            dve.tensor_tensor(cmp_g, cmp_g, cmp_x, ALU.mult).then_inc(s["cmp_inner"], 1)
            dve.wait_ge(s["cmp_exp"], 1)
            link(dve.tensor_scalar(cmp_g, cmp_g, 1.0, None, ALU.add))
            link(dve.reciprocal(cmp_g, cmp_g))
            dve.wait_ge(s["const_done"], 1)
            dve.tensor_tensor(cmp_h, cmp_x, cmp_g, ALU.mult).then_inc(s["cmp_h_done"], 1)
            dve.wait_ge(s["cmp_h_done"], 1)
            for g in range(NSA_G):
                dve.tensor_copy(hv4[:, g, :, 0:NC], spread(cmp_h[:, 1, g * NC:(g + 1) * NC], 1, 4))\
                    .then_inc(s["cmp_h_done"], 1)
            proj(5)
            dve.wait_ge(s["gate_exp"], 1)
            link(dve.tensor_scalar(gates, gates, 1.0, None, ALU.add))
            link(dve.reciprocal(gates, gates))
            dve.wait_ge(s["cmp_scores"], 1)
            for t in range(TT):
                for g in range(NSA_G):
                    c = t * HPG * NC
                    link(dve.tensor_tensor(cs[:, t, g * HPG:(g + 1) * HPG], bank(4 + g)[:, c:c + HPG * NC]
                                           .rearrange("p (h c) -> p h c", h=HPG),
                                           spread(cmask[:, t, :], 1, HPG), ALU.add))
            flat = cs.rearrange("p t h c -> p (t h) c")
            link(dve.tensor_reduce(cstat[:, 0, :], flat, AX.X, ALU.max))
            dve.tensor_tensor(flat, flat, spread(cstat[:, 0, :], 2, NC), ALU.subtract)\
                .then_inc(s["cmp_shifted"], 1)

            def mask(u):
                t, nk = u // 4, P * (u // 4 + 1)
                dve.wait_ge(s["nsa_scores"], u + 1)
                if u >= 2:
                    dve.wait_ge(s["nsa_pT"], u - 1)
                src = (psum[:, 4:6, :].rearrange("p b n -> p (b n)")[:, 0:HPG * nk]
                       .rearrange("p (i k) -> p i k", i=HPG))
                if t == 0:
                    m = spread(causal[:, 1, :], 1, HPG)
                else:
                    m = spread(causal.rearrange("p a k -> p (a k)"), 1, HPG)
                v = scores[:, u % 2, :, 0:nk]
                dve.tensor_tensor(v, src, m, ALU.add).then_inc(s["nsa_masked"], 1)
                dve.wait_ge(s["nsa_masked"], u + 1)
                dve.tensor_reduce(stat[:, u % 2, 0, :], v, AX.X, ALU.max, negate=True)\
                    .then_inc(s["nsa_max"], 1)

            def scale(u):
                t, br, g, nk = u // 4, u // 2 % 2, u % 2, P * (u // 4 + 1)
                dve.wait_ge(s["nsa_exp"], HPG * (u + 1))
                link(dve.reciprocal(stat[:, u % 2, 2, :], stat[:, u % 2, 1, :]))
                c = (br + 1) * NSA_H + g * HPG
                link(dve.tensor_tensor(stat[:, u % 2, 3, :], stat[:, u % 2, 2, :], gates[:, t, c:c + HPG], ALU.mult))
                v = scores[:, u % 2, :, 0:nk]
                dve.tensor_tensor(v, v, spread(stat[:, u % 2, 3, :], 2, nk), ALU.mult)\
                    .then_inc(s["nsa_scaled"], 1)

            mask(0)
            dve.wait_ge(s["cmp_probs"], 1)
            link(dve.tensor_reduce(cstat[:, 1, :], flat, AX.X, ALU.add))
            link(dve.reciprocal(cstat[:, 2, :], cstat[:, 1, :]))
            link(dve.tensor_tensor(cstat[:, 3, :].rearrange("p (t h) -> p t h", t=TT),
                                   cstat[:, 2, :].rearrange("p (t h) -> p t h", t=TT),
                                   gates[:, :, 0:NSA_H], ALU.mult))
            link(dve.tensor_tensor(flat, flat, spread(cstat[:, 3, :], 2, NC), ALU.mult))
            for t in range(TT):
                dve.tensor_tensor(cp[:, t, :, 0:NC], cs[:, t], spread(cvis[:, t, :], 1, NSA_H), ALU.mult)\
                    .then_inc(s["cmp_p_done"], 1)
            for u in range(8):
                if u + 1 < 8:
                    mask(u + 1)
                scale(u)
                if 6 + u in (7, 9, 11):
                    proj(6 + u)
                if u >= 4:
                    dve.wait_ge(s["nsa_pT"], u + 1)
                    if u >= 6:
                        dve.wait_ge(s["nsa_pv"], u - 1)
                    dve.tensor_copy(probsT[:, u % 2, 1, :], bank(3)).then_inc(s["nsa_pT_odd"], 1)

            for hd in range(SB_H):
                dve.wait_ge(s["sb_ln"], hd + 1)
                if hd >= 3:
                    dve.wait_ge(s["sb_e"], hd - 2)
                dve.scalar_tensor_tensor(out=zt[:, hd % 3, :], in0=bank(SB_BANKS[hd % 4])[:, 0:384], scalar=0.0,
                                         in1=ztmp[:, hd % 3, :], op0=ALU.max, op1=ALU.add)\
                    .then_inc(s["sb_t"], 1)
            dve.wait_ge(s["sb_pv"], SB_H)
            for b in range(2):
                dve.tensor_copy(oT[:, 4 + 2 * b:6 + 2 * b, :], bank(2 + b).rearrange("p (a t) -> p a t", a=2))\
                    .then_inc(s["oT_done"], 1)

            def add_mix(l, banks):
                for i, b in enumerate(banks):
                    t, n = divmod(i, 2)
                    dve.wait_ge(s["mix_psum"], 4 * l + i + 1)
                    dve.tensor_tensor(h[:, t, n * 512:(n + 1) * 512], bank(b), h[:, t, n * 512:(n + 1) * 512],
                                      ALU.add).then_inc(s["h_done"], 1)
                    if n == 1:
                        norm(2 * l + 1, t)
                        xT_half(2 * l + 1, t)

            def route(l):
                dve.wait_ge(s["route_psum"], l + 1)
                dve.wait_ge(s["route_loaded"], 64 * (l + 1))
                for t in range(TT):
                    ins = dve.tensor_tensor(logit[:, t, :], bank(4 + t)[:, 0:GR + NE], b_route[:, :], ALU.add)
                    ins.then_inc(s["route_logit"], 1)
                dve.wait_ge(s["route_logit"], TT * (l + 1))
                lg, le = logit[:, :, 0:GR], logit[:, :, GR:]
                t0, t1, t2 = route_t[:, 0], route_t[:, 1], route_t[:, 2]
                link(dve.tensor_reduce(route_s[:, 0, :], lg, AX.X, ALU.max, negate=True))
                link(dve.tensor_tensor(t0[:, :, 0:GR], lg, spread(route_s[:, 0, :], 2, GR), ALU.add))
                link(dve.tensor_scalar(t0[:, :, 0:GR], t0[:, :, 0:GR], 0.0, 1e6, ALU.is_lt, ALU.mult))
                link(dve.tensor_tensor(t0[:, :, 0:GR], t0[:, :, 0:GR], spread(iota_exp[:, 0:GR], 1, TT), ALU.add))
                link(dve.tensor_reduce(route_s[:, 2, :], t0[:, :, 0:GR], AX.X, ALU.min))
                link(dve.tensor_tensor(t1[:, :, 0:GR], spread(iota_exp[:, 0:GR], 1, TT),
                                       spread(route_s[:, 2, :], 2, GR), ALU.is_equal))
                link(dve.tensor_scalar(t1[:, :, 0:GR], t1[:, :, 0:GR], -1.0, -NEG, ALU.add, ALU.mult))
                for t in range(TT):
                    link(dve.tensor_tensor(t0[:, t, :].rearrange("p (g e) -> p g e", g=GR),
                                           le[:, t, :].rearrange("p (g e) -> p g e", g=GR),
                                           spread(t1[:, t, 0:GR], 2, EPG), ALU.add))
                for k in range(2):
                    link(dve.tensor_reduce(route_s[:, 6 + k, :], t0, AX.X, ALU.max))
                    link(dve.tensor_tensor(t1, t0, spread(route_s[:, 6 + k, :], 2, NE), ALU.is_lt))
                    link(dve.tensor_scalar(t1, t1, 1e6, None, ALU.mult))
                    link(dve.tensor_tensor(t1, t1, spread(iota_exp[:, :], 1, TT), ALU.add))
                    link(dve.tensor_reduce(route_s[:, 3, :], t1, AX.X, ALU.min))
                    link(dve.tensor_tensor(chosen[:, k], spread(iota_exp[:, :], 1, TT),
                                           spread(route_s[:, 3, :], 2, NE), ALU.is_equal))
                    if k == 0:
                        link(dve.tensor_scalar(t2, chosen[:, 0], 3.0 * NEG, None, ALU.mult))
                        link(dve.tensor_tensor(t0, t0, t2, ALU.add))
                dve.tensor_tensor(route_s[:, 4, :], route_s[:, 7, :], route_s[:, 6, :], ALU.subtract)\
                    .then_inc(s["route_diff"], 1)
                dve.tensor_tensor(member[:, :, :], chosen[:, 0], chosen[:, 1], ALU.add)\
                    .then_inc(s["member_done"], 1)
                link(dve.tensor_scalar(row_of[:, :, :], chosen[:, 1], float(T), None, ALU.mult))
                dve.tensor_tensor(row_of[:, :, :], row_of[:, :, :], spread(token_row[:, :], 2, NE), ALU.add)\
                    .then_inc(s["row_of_done"], 1)
                dve.wait_ge(s["slot_psum"], l + 1)
                dve.wait_ge(s["member_done"], l + 1)
                link(dve.tensor_scalar(t2, bank(6)[:, 0:TT * NE].rearrange("p (t e) -> p t e", t=TT), 1.0, None,
                                       ALU.add))
                link(dve.tensor_tensor(slot_of[:, :, :], t2, member[:, :, :], ALU.mult))
                link(dve.tensor_scalar(slot_of[:, :, :], slot_of[:, :, :], -1.0, None, ALU.add))
                link(dve.tensor_reduce(route_s[:, 8, 0:1], bank(6)[:, 64:64 + NE], AX.X, ALU.max))
                for i in range(PASS_MAX - 1):
                    link(dve.tensor_scalar(passes_f[:, i:i + 1], route_s[:, 8, 0:1], float(CAP * (i + 1)), None,
                                           ALU.is_gt))
                link(dve.tensor_reduce(route_s[:, 9, 0:1], passes_f[:, 0:PASS_MAX - 1], AX.X, ALU.add))
                dve.tensor_copy(passes[l][:, :], route_s[0:1, 9, 0:1]).then_inc(s["passes_ready"], 1)
                dve.wait_ge(s["route_exp"], 3 * (l + 1))
                link(dve.tensor_scalar(route_s[:, 10, :], route_s[:, 5, :], 1.0, None, ALU.add))
                link(dve.tensor_tensor(route_s[:, 11, :], route_s[:, 10, :], route_s[:, 1, :], ALU.mult))
                link(dve.reciprocal(weight[:, 0, :], route_s[:, 11, :]))
                dve.tensor_tensor(weight[:, 1, :], weight[:, 0, :], route_s[:, 5, :], ALU.mult)\
                    .then_inc(s["route_used"], 1)

            QUAD_LINKS = 8

            def quad(l, n, q):
                qlink = Chain(dve, s[f"dve_quad{l}"], QUAD_LINKS * n)
                dve.tensor_tensor(slots, iota_slot[:, :].unsqueeze(1).unsqueeze(1).broadcast_to([P, TT, QE, CAP]),
                                  slot_of[:, :, bass.ds(QE * q, QE)].unsqueeze(3)
                                  .broadcast_to([P, TT, QE, CAP]), ALU.is_equal).then_inc(s[f"slots{l}"], 1)
                dve.wait_ge(s[f"gathered{l}"], 2 * n + 2)
                dve.tensor_copy(gatheredT[:, 4:8, :], bank(1).rearrange("p (k c) -> p k c", k=4))\
                    .then_inc(s[f"gatheredT{l}"], 1)
                dve.wait_ge(s[f"index_psum{l}"], n + 1)
                qlink(dve.tensor_tensor(idx_t[:, 0:QE], bank(2)[:, 0:QE], slot_expert[:, :], ALU.mult))
                qlink(dve.tensor_reduce(idx_t[:, 4:5], idx_t[:, 0:QE], AX.X, ALU.add))
                qlink(dve.tensor_scalar(idx_t[:, 5:6], idx_t[:, 4:5], 0.0, 1e6, ALU.is_equal, ALU.mult))
                qlink(dve.tensor_scalar(idx_t[:, 6:7], idx_t[:, 4:5], -1.0, None, ALU.add))
                dve.wait_ge(s[f"egate{l}"], n + 1)
                qlink(dve.tensor_scalar(egate, egate, 1.0, None, ALU.add))
                qlink(dve.reciprocal(egate, egate))
                qlink(dve.tensor_tensor(hid_t, bank(3)[:, 0:FF], egate, ALU.mult))
                qlink(dve.tensor_tensor(hid, bank(3)[:, FF:2 * FF], hid_t, ALU.mult))
                assert qlink.n == QUAD_LINKS
                dve.wait_ge(s[f"rows_free{l}"], n + 1)
                dve.tensor_tensor(idx_i[:, :], idx_t[:, 5:6], idx_t[:, 6:7], ALU.add)\
                    .then_inc(s[f"row_index{l}"], 1)
                dve.wait_ge(s[f"down{l}"], n + 1)
                dve.tensor_copy(y_rows[:, 512:D], bank(6)).then_inc(s[f"y_rows{l}"], 1)

            def experts(l):
                route(l)
                dve.wait_ge(s["route_used"], l + 1)
                with dve.Fori(0, NQ) as q:
                    quad(l, q, q)
                more = dve.value_load(passes[l][0:1, 0:1], min_val=0, max_val=PASS_MAX - 1)
                with dve.If(more > 0):
                    with dve.Fori(0, more) as r:
                        dve.tensor_scalar(slot_of[:, :, :], slot_of[:, :, :], -float(CAP), None, ALU.add)\
                            .then_inc(s[f"next_round{l}"], 1)
                        with dve.Fori(0, NQ) as q:
                            dve.wait_ge(s[f"next_round{l}"], r + 1)
                            quad(l, q + NQ * (r + 1), q)
                for t in range(TT):
                    dve.wait_ge(s[f"rows_in{t}"], 32 * (l + 1))
                    link(dve.scalar_tensor_tensor(out=h[:, t, :], in0=y_pair[:, 0, t, :],
                                                  scalar=weight[:, 0, t:t + 1], in1=h[:, t, :],
                                                  op0=ALU.mult, op1=ALU.add))
                    dve.scalar_tensor_tensor(out=h[:, t, :], in0=y_pair[:, 1, t, :],
                                             scalar=weight[:, 1, t:t + 1], in1=h[:, t, :],
                                             op0=ALU.mult, op1=ALU.add).then_inc(s["h_done"], 1)
                    norm(2 * l + 2, t)
                    if l == 0:
                        xT_half(2, t)

            add_mix(0, (0, 1, 4, 5))
            experts(0)

            dve.wait_ge(s["lb_psum"], 1)
            link(dve.tensor_copy(lb, bank(4)[:, 0:2 * RH]))
            link(dve.tensor_tensor(lbt[:, 2, :], lb[:, 0:RH], lb[:, RH:], ALU.max))
            link(dve.tensor_tensor(lbt[:, 0, :], lb[:, 0:RH], lbt[:, 2, :], ALU.subtract))
            dve.tensor_tensor(lbt[:, 1, :], lb[:, RH:], lbt[:, 2, :], ALU.subtract).then_inc(s["lb_diff"], 1)
            dve.wait_ge(s["lb_exp"], 1)
            link(dve.tensor_tensor(lbt[:, 2, :], lbt[:, 0, :], lbt[:, 1, :], ALU.add))
            link(dve.reciprocal(lbt[:, 3, :], lbt[:, 2, :]))
            link(dve.tensor_tensor(lbt[:, 0, :], lbt[:, 0, :], lbt[:, 3, :], ALU.mult))
            for hh in range(2):
                sl = slice(4 * hh, 4 * hh + 4)
                dve.wait_ge(s["rec_f"], 2 * hh + 2)
                link(dve.tensor_scalar(rA[:, sl, :], rA[:, sl, :], 1.0, None, ALU.add))
                link(dve.reciprocal(rA[:, sl, :], rA[:, sl, :]))
                dve.tensor_tensor(rA[:, sl, :], rA[:, sl, :], spread(lbt[:, 0, sl], 2, T), ALU.mult)\
                    .then_inc(s["rec_key"], 1)
            dve.wait_ge(s["rec_const"], 1)
            for hh in range(2):
                sl = slice(4 * hh, 4 * hh + 4)
                flat_cum = rB[:, sl, :].rearrange("p h t -> p (h t)")
                dve.wait_ge(s["rec_logf"], hh + 1)
                dve.tensor_tensor_scan(flat_cum, reset, rC[:, sl, :].rearrange("p h t -> p (h t)"), 0.0,
                                       ALU.mult, ALU.add).then_inc(s["rec_cum"], 1)
                dve.wait_ge(s["rec_cum"], hh + 1)
                cum = flat_cum.rearrange("p (g i) -> p g i", i=CH)
                dve.tensor_tensor(rC[:, sl, :].rearrange("p h (c i) -> p (h c) i", i=CH), cum,
                                  cum[:, :, CH // 2:CH // 2 + 1].broadcast_to([P, 4 * NCH, CH]), ALU.subtract)\
                    .then_inc(s["rec_rel"], 1)
            for m in range(4, 8):
                dve.wait_ge(s["rec_psum"], m + 1)
                dve.tensor_scalar(rQ[:, 2 * (m - 4):2 * (m - 4) + 2, :], bank(m).rearrange("p (a t) -> p a t", a=2),
                                  RK ** -0.5, None, ALU.mult).then_inc(s["rec_q"], 1)
            dve.wait_ge(s["rec_q"], 4)
            for hh in range(2):
                sl = slice(4 * hh, 4 * hh + 4)
                dve.wait_ge(s["rec_exps"], 4 * hh + 4)
                link(dve.tensor_copy(decay[:, sl, :], r3[:, sl, :].rearrange("p h (c i) -> p h c i", i=CH)[:, :, :, CH - 1]))
                dve.tensor_tensor(r1[:, sl, :], r1[:, sl, :], rQ[:, sl, :], ALU.mult).then_inc(s["rec_qin"], 1)
                dve.tensor_tensor(r3[:, sl, :], r3[:, sl, :], rQ[:, sl, :], ALU.mult).then_inc(s["rec_qin"], 1)
            for m in range(12, 16):
                i = m - 12
                dve.wait_ge(s["rec_psum"], m + 1)
                dve.tensor_copy(rg[:, i % 2, i // 2 * 512:i // 2 * 512 + 512], bank(m % 4 + 4))\
                    .then_inc(s["rec_gate"], 1)
            for b in (1, 3):
                dve.wait_ge(s["ko_psum"], b + 1)
                dve.tensor_copy(koR[:, b // 2, (b % 2) * 512:(b % 2) * 512 + 512], bank(b))\
                    .then_inc(s["ko_done"], 1)
            for c in range(NCH - 1):
                dve.wait_ge(s["state_psum"], c + 1)
                kv = psum[:, 2 * (c % 2):2 * (c % 2) + 2, :].rearrange("p b n -> p (b n)")
                if c == 0:
                    dve.tensor_copy(states[0], kv).then_inc(s["state_done"], RH)
                else:
                    for hd in range(RH):
                        d = slice(hd * RV, (hd + 1) * RV)
                        dve.scalar_tensor_tensor(out=states[c][:, d], in0=states[c - 1][:, d],
                                                 scalar=decay[:, hd, c:c + 1], in1=kv[:, d],
                                                 op0=ALU.mult, op1=ALU.add).then_inc(s["state_done"], 1)
                dve.wait_ge(s["state_done"], RH * (c + 1))
            for t in range(TT):
                dve.wait_ge(s["rec_gate_exp"], 4)
                link(dve.tensor_scalar(e_gate[:, t, :], e_gate[:, t, :], 1.0, None, ALU.add))
                link(dve.reciprocal(e_gate[:, t, :], e_gate[:, t, :]))
                link(dve.tensor_tensor(rg[:, t, :], rg[:, t, :], e_gate[:, t, :], ALU.mult))
                g3 = rg[:, t, :].rearrange("p (h d) -> p h d", h=RH)
                link(dve.tensor_tensor(g3, g3, spread(gnorm, 1, RH), ALU.mult))
            dve.wait_ge(s["a_used"], 1)
            for t in range(TT):
                dve.wait_ge(s["o_square"], t + 1)
                dve.tensor_reduce(ostat[:, 0, t * RH:(t + 1) * RH], square_rec.rearrange("p (h d) -> p h d", h=RH),
                                  AX.X, ALU.add).then_inc(s["o_sum"], 1)
                dve.wait_ge(s["o_rstd"], t + 1)
                o_ps = psum[:, 4 + 2 * t:6 + 2 * t, :].rearrange("p b n -> p (b n)").rearrange("p (h d) -> p h d", h=RH)
                o3 = o_rows[:, t, :].rearrange("p (h d) -> p h d", h=RH)
                link(dve.tensor_tensor(o3, o_ps, spread(ostat[:, 1, t * RH:(t + 1) * RH], 2, RV), ALU.mult))
                dve.tensor_tensor(o_rows[:, t, :], o_rows[:, t, :], rg[:, t, :], ALU.mult)\
                    .then_inc(s["o_done"], 1)
            for b in (1, 3):
                dve.wait_ge(s["recT_psum"], b + 1)
                dve.tensor_copy(recT[:, 4 * (b % 2):4 * (b % 2) + 4, (b // 2) * P:(b // 2 + 1) * P],
                                bank(b).rearrange("p (k t) -> p k t", k=4)).then_inc(s["recT_done"], 1)
            add_mix(1, (4, 5, 6, 7))
            experts(1)

        @block.tensor
        def _(pe):
            def unit(u, n=None):
                slot, use = u % NU, u // NU + 1
                pe.wait_ge(s[f"unit{slot}_loaded"], 32 * use if n is None else 32 * use + 32 * n)
                return ring[:, slot, :]

            def transposes(v, t):
                for half in range(2):
                    pe.wait_ge(s["xg_done"], TT * v + t + 1)
                    for k in range(4):
                        last = pe.transpose(bank(2 * t + half)[:, k * P:(k + 1) * P], xg[:, t, 4 * half + k::KD],
                                            ident[:, :])
                    last.then_inc(s["xT_psum"], 1)

            pe.wait_ge(s["ident_done"], 1)
            for t in range(TT):
                transposes(0, t)
            pe.wait_ge(s["cmp_small"], 64)
            for i in range(2):
                last = pe.transpose(bank(5)[:, i * LP:(i + 1) * LP], pe_rows[0:LP, i, :], ident[0:LP, 0:LP])
            last.then_inc(s["pe_psum"], 1)
            pe.wait_ge(s["xT_done"], 4)

            def w_cols(r, n):
                return r[:, 0:KD * n].rearrange("p (k n) -> p k n", k=KD)

            def tile_T(dst, lhs):
                for k in range(KD):
                    last = pe.matmul(dst, lhs(k), xT[:, k, :], start=(k == 0), stop=(k == KD - 1))
                return last

            def tile_rows(dst, t, rhs):
                for k in range(KD):
                    last = pe.matmul(dst, xT[:, k, t * P:(t + 1) * P], rhs(k), start=(k == 0), stop=(k == KD - 1))
                return last

            def proj(n):
                if n >= 2:
                    pe.wait_ge(s["proj_odd" if n % 2 else "proj_even"], (n - 2) // 2 + 1)
                b = bank(n % 2)
                if n in (0, 1):
                    w = w_cols(unit(U_Q), 512)
                    for i in range(2):
                        for k in range(KD):
                            for g in range(NSA_G):
                                c = (g * HPG + 2 * n + i) * DH
                                last = pe.matmul(b[g * DH:(g + 1) * DH, i * T:(i + 1) * T], w[:, k, c:c + DH],
                                                 xT[:, k, :], start=(k == 0), stop=(k == KD - 1))
                    if n == 1:
                        last.then_inc(s["q_unit_done"], 1)
                elif n == 2:
                    w = w_cols(unit(U_KV), 512)
                    for i in range(2):
                        last = tile_T(b[:, i * T:(i + 1) * T], lambda k: w[:, k, i * P:(i + 1) * P])
                elif n == 3:
                    w, w_w = w_cols(unit(U_KV), 512), w_cols(unit(U_WG), 280)
                    tile_T(b[:, 0:T], lambda k: w[:, k, 2 * P:3 * P])
                    last = tile_T(b[:, T:2 * T], lambda k: w_w[:, k, 0:P])
                elif n in (4, 5):
                    w, w_w = w_cols(unit(U_KV), 512), w_cols(unit(U_WG), 280)
                    tile_rows(b[:, 0:P], n - 4, lambda k: w[:, k, 3 * P:4 * P])
                    last = tile_rows(b[:, P:280], n - 4, lambda k: w_w[:, k, P:280])
                elif n in (6, 7, 8, 9):
                    w = w_cols(unit(U_QB if n < 8 else U_KB), 512)
                    for i in range(2):
                        j = 2 * (n % 2) + i
                        last = tile_T(b[:, i * T:(i + 1) * T], lambda k: w[:, k, j * P:(j + 1) * P])
                else:
                    w = w_cols(unit(U_VB), 512)
                    last = tile_rows(b, n - 10, lambda k: w[:, k, :])
                if n != 1:
                    last.then_inc(s["proj_psum"], 1)

            def free_units(k):
                pe.drain().then_inc(s["unit_used"], k)

            proj(0)
            proj(1)
            pe.wait_ge(s["q_unit_done"], 1)
            pe.nop().then_inc(s["proj_psum"], 1)
            free_units(1)
            proj(2)
            proj(3)
            w1 = unit(U_CMP).rearrange("p (w j n) -> p w j n", w=2, n=P)
            pe.wait_ge(s["cmp_w1_rest"], 32)
            pe.wait_ge(s["kv2_done"], 7)
            pe.wait_ge(s["proj_even"], 2)
            pe.wait_ge(s["pe_done"], 1)
            for kv in range(2):
                for j in range(LP):
                    last = pe.matmul(bank(4)[:, 64 * kv:64 * kv + (NSA_G + 1) * NC]
                                     .rearrange("p (g c) -> p g c", g=NSA_G + 1),
                                     w1[:, kv, j, :],
                                     kv2[:, kv, :, 2 * j:2 * j + CMP_STRIDE * (NC - 1) + 1:CMP_STRIDE],
                                     start=(j == 0), stop=(j == LP - 1))
            last.then_inc(s["cmp_hidden"], 1)
            proj(4)
            pe.wait_ge(s["cmp_h_done"], 3)
            pe.matmul(bank(5)[0:DH, 0:2 * NC], w2[:, 0, :], cmp_h[:, 0, :], start=True, stop=True)
            for g in range(NSA_G):
                last = pe.matmul(bank(5)[:, 64 + g * DH:64 + (g + 1) * DH],
                                 hv4[:, g, :, :].rearrange("p a c -> p (a c)"), w2[:, 1, :], start=True, stop=True)
            last.then_inc(s["cmp_kv"], 1)
            proj(5)
            free_units(3)
            pe.wait_ge(s["cmp_kv_done"], 3)
            pe.wait_ge(s["proj_odd"], 1)

            def q_of(hd, t):
                g, i = divmod(hd, HPG)
                return qT[g * DH:(g + 1) * DH, i, t * P:(t + 1) * P]

            for t in range(TT):
                for hd in range(NSA_H):
                    g = hd // HPG
                    c = (t * HPG + hd % HPG) * NC
                    last = pe.matmul(bank(4 + g)[:, c:c + NC], q_of(hd, t), kcT[g * DH:(g + 1) * DH, :],
                                     start=True, stop=True)
            last.then_inc(s["cmp_scores"], 1)

            def nsa_scores(u):
                t, br, g, nk = u // 4, u // 2 % 2, u % 2, P * (u // 4 + 1)
                if u == 0:
                    pe.wait_ge(s["cmp_shifted"], 1)
                    pe.wait_ge(s["proj_odd"], 2)
                else:
                    pe.wait_ge(s["nsa_masked"], u)
                dst = psum[:, 4:6, :].rearrange("p b n -> p (b n)")
                for i in range(HPG):
                    last = pe.matmul(dst[:, i * nk:(i + 1) * nk], q_of(g * HPG + i, t),
                                     ksw[g * DH:(g + 1) * DH, br, 0:nk], start=True, stop=True)
                last.then_inc(s["nsa_scores"], 1)

            def nsa_T(u):
                pe.wait_ge(s["nsa_scaled"], u + 1)
                if u >= 1:
                    pe.wait_ge(s["nsa_pT_even"], u)
                if u >= 5:
                    pe.wait_ge(s["nsa_pT_odd"], u - 4)
                for kb in range(u // 4 + 1):
                    for i in range(HPG):
                        last = pe.transpose(bank(2 + kb)[:, i * P:(i + 1) * P],
                                            scores[:, u % 2, i, kb * P:(kb + 1) * P], ident[:, :])
                last.then_inc(s["nsa_pT"], 1)

            def nsa_pv(u):
                t, br, g = u // 4, u // 2 % 2, u % 2
                pe.wait_ge(s["nsa_pT_even"], u + 1)
                if u >= 4:
                    pe.wait_ge(s["nsa_pT_odd"], u - 3)
                acc = bank(6 + g).rearrange("p (a t) -> p a t", a=2)
                for kb in range(t + 1):
                    for par in range(2):
                        heads = probsT[:, u % 2, kb, :].rearrange("p (a two q) -> p a two q", two=2, q=P)
                        last = pe.matmul(acc[par * DH:(par + 1) * DH, :, t * P:(t + 1) * P],
                                         vsw[:, kb, br * P + g * DH:br * P + (g + 1) * DH], heads[:, :, par, :],
                                         start=False, stop=True, skip_group_check=True)
                last.then_inc(s["nsa_pv"], 1)

            nsa_scores(0)
            for u in range(8):
                if u + 1 < 8:
                    nsa_scores(u + 1)
                if u == 1:
                    pe.wait_ge(s["cmp_pT_done"], 1)
                    for i in range(HPG):
                        for g in range(NSA_G):
                            last = pe.matmul(bank(6 + g)[i % 2 * DH:(i % 2 + 1) * DH, i // 2 * T:(i // 2 + 1) * T],
                                             vc4[i * 32:(i + 1) * 32, g, :], pcT[i * 32:(i + 1) * 32, g, :],
                                             start=(i < 2), stop=True, skip_group_check=True)
                        if i % 2:
                            last.then_inc(s["cmp_pv"], 1)
                            pe.wait_ge(s["cmp_pv"], i // 2 + 1)
                if u >= 1:
                    nsa_pv(u - 1)
                if 6 + u < 12:
                    proj(6 + u)
                    if 6 + u in (7, 9, 11):
                        free_units(1)
                if u == 0:
                    pe.wait_ge(s["cmp_p_done"], 2)
                    for g in range(NSA_G):
                        for t in range(TT):
                            last = pe.transpose(bank(5)[:, g * T + t * P:g * T + (t + 1) * P],
                                                cp[:, t, g * HPG:(g + 1) * HPG, :].rearrange("p h c -> p (h c)"),
                                                ident[:, :])
                    last.then_inc(s["cmp_pT"], 1)
                nsa_T(u)
            nsa_pv(7)

            def sb_z(hd):
                p0, j = hd % 2 * DH, hd // 2
                if hd == 0:
                    pe.wait_ge(s["nsa_masked"], 8)
                    pe.wait_ge(s["proj_odd"], 6)
                    pe.wait_ge(s["proj_even"], 6)
                if hd >= 4:
                    pe.wait_ge(s["sb_a"], hd - 3)
                z = bank(SB_BANKS[hd % 4])
                pe.matmul(z[:, 0:T], kbT[p0:p0 + DH, j, 0:P], qbT[p0:p0 + DH, j, :], start=True, stop=True,
                          skip_group_check=True)
                pe.matmul(z[:, T:T + P], kbT[p0:p0 + DH, j, P:T], qbT[p0:p0 + DH, j, P:T], start=False, stop=True,
                          skip_group_check=True).then_inc(s["sb_z_raw"], 1)
                pe.wait_ge(s["sb_z_raw"], hd + 1)
                pe.matmul(z[:, 0:P], ident[:, :], before_query, start=False, stop=True, skip_group_check=True)
                pe.matmul(z[:, T:T + P], ident[:, :], before_query, start=False, stop=True, skip_group_check=True)\
                    .then_inc(s["sb_z"], 1)

            def sb_e(hd):
                pe.wait_ge(s["sb_t"], hd + 1)
                z, t = bank(SB_BANKS[hd % 4]), zt[:, hd % 3, :]
                pe.matmul(z[:, 0:T], later_own, t[:, 0:T], start=False, stop=True, skip_group_check=True)
                pe.matmul(z[:, P:T], later_all, t[:, T:T + P], start=False, stop=True, skip_group_check=True)
                pe.matmul(z[:, T:T + P], later_own, t[:, T:T + P], start=False, stop=True, skip_group_check=True)\
                    .then_inc(s["sb_e"], 1)

            def sb_pv(hd):
                pe.wait_ge(s["sb_a"], hd + 1)
                if hd == 0:
                    pe.wait_ge(s["nsa_pT_even"], 8)
                    pe.wait_ge(s["nsa_pT_odd"], 4)
                p0, j = hd % 2 * DH, hd // 2
                acc = bank(2 + j // 2)[p0:p0 + DH, j % 2 * T:(j % 2 + 1) * T]
                w, p = vb[:, :, hd * DH:(hd + 1) * DH], za[:, hd % 2, :]
                pe.matmul(acc, w[:, 0, :], p[:, 0:T], start=(hd % 4 < 2), stop=True, skip_group_check=True)
                pe.matmul(acc[:, P:T], w[:, 1, :], p[:, T:T + P], start=False, stop=True, skip_group_check=True)\
                    .then_inc(s["sb_pv"], 1)

            sb_z(0)
            sb_z(1)
            for hd in range(SB_H):
                if hd + 2 < SB_H:
                    sb_z(hd + 2)
                sb_e(hd)
                if hd >= 1:
                    sb_pv(hd - 1)
            sb_pv(SB_H - 1)

            def mix(l, lhs, units, banks, n=None):
                for i, b in enumerate(banks):
                    t, c = divmod(i, 2)
                    w = unit(units + c, n).rearrange("p (j n) -> p j n", n=512)
                    for j in range(8):
                        last = pe.matmul(bank(b), lhs[:, j, t * P:(t + 1) * P], w[:, j, :],
                                         start=(j == 0), stop=(j == 7))
                    last.then_inc(s["mix_psum"], 1)
                    if i == 2:
                        transposes(2 * l + 1, 0)
                free_units(2)
                transposes(2 * l + 1, 1)

            pe.wait_ge(s["oT_done"], 4)
            pe.wait_ge(s["sb_a"], SB_H)
            mix(0, oT, U_WO, (0, 1, 4, 5))

            def route(l):
                pe.wait_ge(s["xT_done"], 4 * (2 * l + 1) + 4)
                pe.wait_ge(s["route_loaded"], 64 * (l + 1))
                for t in range(TT):
                    last = tile_rows(bank(4 + t)[:, 0:GR + NE], t, lambda k: w_route[:, k, :])
                last.then_inc(s["route_psum"], 1)
                pe.wait_ge(s["member_done"], l + 1)
                pe.matmul(bank(6)[:, 0:NE], earlier[:, :], member[:, 0, :], start=True, stop=True)
                pe.matmul(bank(6)[:, NE:2 * NE], ones[:, :], member[:, 0, :], start=True, stop=False)
                pe.matmul(bank(6)[:, NE:2 * NE], earlier[:, :], member[:, 1, :], start=False, stop=True)
                pe.matmul(bank(6)[:, 2 * NE:3 * NE], ones[:, :], member[:, 0, :], start=True, stop=False)
                pe.matmul(bank(6)[:, 2 * NE:3 * NE], ones[:, :], member[:, 1, :], start=False, stop=True)\
                    .then_inc(s["slot_psum"], 1)

            def quad(l, n, q, before):
                rounds = n + before
                pe.wait_ge(s[f"slots{l}"], n + 1)
                for k in range(KD):
                    for t in range(TT):
                        last = pe.matmul(bank(k // 4)[:, k % 4 * P:(k % 4 + 1) * P], xg[:, t, k::KD],
                                         slots[:, t].rearrange("p e c -> p (e c)"), start=(t == 0), stop=(t == TT - 1))
                    if k % 4 == 3:
                        last.then_inc(s[f"gathered{l}"], 1)
                for t in range(TT):
                    last = pe.matmul(bank(2)[:, 0:QE], slots[:, t].rearrange("p e c -> p (e c)"),
                                     row_of[:, t, bass.ds(QE * q, QE)], start=(t == 0), stop=(t == TT - 1))
                last.then_inc(s[f"index_psum{l}"], 1)
                pe.wait_ge(s[f"gatheredT{l}"], 2 * n + 2)
                for c in range(KD // 2):
                    w = unit(BASE_MOE[l] + c, rounds).rearrange("p (w e r f) -> p w e r f", w=2, e=QE, r=2)
                    for r in range(2):
                        k = 2 * c + r
                        for e in range(QE):
                            last = pe.matmul(bank(3)[e * CAP:(e + 1) * CAP, :].rearrange("p (w f) -> p w f", w=2),
                                             gatheredT[:, k, e * CAP:(e + 1) * CAP], w[:, :, e, r, :],
                                             start=(k == 0), stop=(k == KD - 1))
                    if c < KD // 2 - 1:
                        last.then_inc(s["unit_used"], 1)
                last.then_inc(s[f"gate_up{l}"], 1)
                pe.wait_ge(s[f"gate_up{l}"], n + 1)
                pe.sem_inc(s["unit_used"], 1)
                pe.wait_ge(s[f"dve_quad{l}"], 8 * n + 8)
                for j in range(KF):
                    last = pe.transpose(bank(4)[:, j * P:(j + 1) * P], hid[:, j::KF], ident[:, :])
                last.then_inc(s[f"hid_psum{l}"], 1)
                pe.wait_ge(s[f"hidT{l}"], n + 1)
                pe.wait_ge(s[f"y_rows{l}"], 2 * n + 2)
                for j in range(KF):
                    w = unit(BASE_MOE[l] + KD // 2 + j, rounds).rearrange("p (e n) -> p e n", e=QE)
                    for c in range(2):
                        for e in range(QE):
                            last = pe.matmul(bank(5 + c)[e * CAP:(e + 1) * CAP, :],
                                             hidT[:, j, e * CAP:(e + 1) * CAP], w[:, e, c * 512:(c + 1) * 512],
                                             start=(j == 0), stop=(j == KF - 1))
                    if j == 0:
                        last.then_inc(s["unit_used"], 1)
                last.then_inc(s[f"down{l}"], 1)
                pe.wait_ge(s[f"down{l}"], n + 1)
                pe.sem_inc(s["unit_used"], 1)

            def experts(l, before):
                route(l)
                with pe.Fori(0, NQ) as q:
                    quad(l, q, q, before)
                pe.wait_ge(s["passes_ready"], l + 1)
                more = pe.value_load(passes[l][0:1, 0:1], min_val=0, max_val=PASS_MAX - 1)
                with pe.If(more > 0):
                    with pe.Fori(0, more) as r:
                        with pe.Fori(0, NQ) as q:
                            quad(l, q + NQ * (r + 1), q, before)
                return NQ * more

            before = experts(0, 0)

            for t in range(TT):
                transposes(2, t)
            pe.wait_ge(s["rec_small"], 32)
            pe.transpose(bank(4)[:, 0:2 * RH], lb_rows[0:2 * RH, :], ident[0:2 * RH, 0:2 * RH])\
                .then_inc(s["lb_psum"], 1)
            pe.wait_ge(s["xT_done"], 12)

            def rec_unit(i):
                return w_cols(unit(BASE_REC + i, before), 512)

            for m in range(8):
                w = rec_unit(m // 2)
                if m == 4:
                    pe.wait_ge(s["lb_diff"], 1)
                for i in range(2):
                    j = 2 * (m % 2) + i
                    last = tile_T(bank(m)[:, i * T:(i + 1) * T], lambda k: w[:, k, j * P:(j + 1) * P])
                last.then_inc(s["rec_psum"], 1)
                if m % 2:
                    free_units(1)
            for m in range(8, 16):
                i, t = (m - 8) // 2, m % 2
                w = rec_unit(4 + i)
                if m == 8:
                    pe.wait_ge(s["rec_f"], 4)
                if m == 12:
                    pe.wait_ge(s["rec_q"], 4)
                last = tile_rows(bank(m % 4 + (4 if m >= 12 else 0)), t, lambda k: w[:, k, :])
                last.then_inc(s["rec_psum"], 1)
                if m % 2:
                    free_units(1)

            pe.wait_ge(s["rec_kout"], 2)
            pe.wait_ge(s["rec_v"], 4)
            for b in range(4):
                t, half = b // 2, b % 2
                for i in range(4):
                    last = pe.transpose(bank(b)[:, i * P:(i + 1) * P], rD[:, 4 * half + i, t * P:(t + 1) * P],
                                        ident[:, :])
                last.then_inc(s["ko_psum"], 1)
            pe.wait_ge(s["rec_kin"], 2)
            pe.nop().then_inc(s["rec_kout_read"], 1)
            pe.wait_ge(s["rec_qin"], 4)
            pe.wait_ge(s["rec_gate"], 4)
            for b in range(4):
                t, half = b // 2, b % 2
                for i in range(4):
                    hd = 4 * half + i
                    last = pe.matmul(bank(4 + b)[:, i * P:(i + 1) * P], r2[:, hd, t * P:(t + 1) * P],
                                     r1[:, hd, t * P:(t + 1) * P], start=True, stop=True)
                last.then_inc(s["a_psum"], 1)

            def state(c):
                if c == 2:
                    pe.wait_ge(s["state_done"], RH)
                p0, t = c % 2 * CH, c // 2
                kv = psum[:, 2 * (c % 2):2 * (c % 2) + 2, :].rearrange("p b n -> p (b n)")
                for hd in range(RH):
                    d = slice(hd * P, (hd + 1) * P)
                    last = pe.matmul(kv[:, d], koR[p0:p0 + CH, t, d], rv[p0:p0 + CH, t, d], start=True, stop=True)
                last.then_inc(s["state_psum"], 1)

            pe.wait_ge(s["a_psum"], 4)
            pe.nop().then_inc(s["rec_kin_used"], 1)
            pe.wait_ge(s["ko_done"], 4)
            for c in range(NCH - 1):
                state(c)
            aMv = aM.rearrange("p h t -> p (h t)").rearrange("p (g t) -> p g t", t=P)
            for t in range(TT):
                pe.wait_ge(s["rec_a_masked"], 4)
                acc = psum[:, 4 + 2 * t:6 + 2 * t, :].rearrange("p b n -> p (b n)")
                for hd in range(RH):
                    d = slice(hd * P, (hd + 1) * P)
                    pe.matmul(acc[:, d], aMv[:, t * RH + hd, :], rv[:, t, d], start=(hd % 4 == 0), stop=False,
                              skip_group_check=True)
                for c in (2 * t, 2 * t + 1):
                    if c == 0:
                        continue
                    pe.wait_ge(s["state_done"], RH * c)
                    for hd in range(RH):
                        d = slice(hd * P, (hd + 1) * P)
                        last = pe.matmul(acc[c % 2 * CH:(c % 2 + 1) * CH, d], r3[:, hd, c * CH:(c + 1) * CH],
                                         states[c - 1][:, d], start=False, stop=True, skip_group_check=True)
                last.then_inc(s["o_psum"], 1)
            pe.wait_ge(s["o_psum"], TT)
            pe.nop().then_inc(s["a_used"], 1)
            for b in range(4):
                t, half = b // 2, b % 2
                pe.wait_ge(s["o_done"], t + 1)
                for i in range(4):
                    d = (4 * half + i) * P
                    last = pe.transpose(bank(b)[:, i * P:(i + 1) * P], o_rows[:, t, d:d + P], ident[:, :])
                last.then_inc(s["recT_psum"], 1)
            pe.wait_ge(s["recT_done"], 4)
            mix(1, recT, BASE_REC + 8, (4, 5, 6, 7), before)
            experts(1, before)

        assert max(att_end, rec_end, moe_end) <= arena_t.shape[1], (att_end, rec_end, moe_end)


_INS = ["x", "norm_mix", "norm_ffn", "att_w_in", "att_w_out", "cmp_pe_k", "cmp_w1_k", "cmp_w2_k", "cmp_pe_v",
        "cmp_w1_v", "cmp_w2_v", "rec_w_in", "rec_lb_logits", "rec_gnorm", "rec_w_out", "moe_w_grp", "moe_b_grp",
        "moe_w_exp", "moe_b_exp", "moe_w_gate", "moe_w_up", "moe_w_down", "final_norm"]


def kernel(**inputs):
    import numpy as np
    import concourse.bacc as bacc
    from concourse.bass_utils import run_bass_kernel_spmd

    nc = bacc.Bacc("TRN2", target_bir_lowering=False, num_devices=1)
    arrays, args = {}, []
    for name in _INS:
        a = np.ascontiguousarray(inputs[name])
        arrays[f"in_{name}"] = a
        args.append(nc.dram_tensor(f"in_{name}", a.shape, mybir.dt.from_np(a.dtype), kind="ExternalInput").ap())
    args.append(nc.dram_tensor("out", (1, T, D), F32, kind="ExternalOutput").ap())
    hybrid_trunk(nc, *args)
    return run_bass_kernel_spmd(nc, [arrays], core_ids=[0]).results[0]["out"]
```

```python
from contextlib import ExitStack

import concourse.bass as bass
from concourse import mybir

F32 = mybir.dt.float32
F32R = mybir.dt.float32r
I32 = mybir.dt.int32
ALU = mybir.AluOpType
ACT = mybir.ActivationFunctionType
AX = mybir.AxisListType

P = 128
T = 256
TT = T // P
D = 1024
KD = D // P
NL = 2
EPS = 1e-6
NEG = -1e30

DH = 64
NSA_H, NSA_G = 8, 2
HPG = NSA_H // NSA_G
SB_H = 8
CMP_LEN, CMP_STRIDE = 32, 16
NC = (T - CMP_LEN) // CMP_STRIDE + 1
LP = CMP_LEN // 2
GELU_A, GELU_B = 0.7978845608028654, 0.044715

RH, RK, RV, CH = 8, 128, 128, 64
NCH = T // CH

GR, EPG = 4, 8
NE = GR * EPG
FF = 256
KF = FF // P
QE = 4
CAP = P // QE
NQ = NE // QE
PASS_MAX = T // CAP

NU = 6
UW = 4096
SPARE = 4
UNITS_PER_QUAD = KD // 2 + KF
assert UNITS_PER_QUAD == NU and SPARE == KD // 2

C_KC, C_VC, C_KS, C_VS, C_KW, C_VW, C_GATE, C_QB = 512, 640, 768, 896, 1024, 1152, 1280, 1304
C_KB, C_VB = C_QB + 512, C_QB + 1024
U_Q, U_KV, U_WG, U_CMP, U_QB, U_KB, U_VB, U_WO = range(8)
ATT_UNITS = 9
REC_UNITS = 10
RING_UNITS_MOE = NQ * NU - SPARE
BASE_REC = ATT_UNITS + RING_UNITS_MOE
BASE_MOE = [ATT_UNITS, BASE_REC + REC_UNITS]
BASE_LOOP = [b + 2 * NU - SPARE for b in BASE_MOE]


def ring_plan():
    n_units = BASE_MOE[1] + RING_UNITS_MOE
    slot, needed, loads = [], [], []
    last_use, count = [-1] * NU, [0] * NU
    for u in range(n_units):
        mixer = u < ATT_UNITS or BASE_REC <= u < BASE_MOE[1]
        if u in BASE_MOE:
            last_use[HI_SLOT] = u - 1
        pick = min((i for i in range(NU) if not (mixer and i == HI_SLOT)),
                   key=lambda i: (last_use[i], i == HI_SLOT, i))
        slot.append(pick)
        needed.append(last_use[pick] + 1)
        count[pick] += 1
        loads.append(count[pick])
        last_use[pick] = u
    for b in BASE_LOOP:
        for u in range(b, b + NU * (NQ - 3)):
            assert slot[u + NU] == slot[u] and needed[u + NU] == needed[u] + NU and loads[u + NU] == loads[u] + 1
        assert slot[b - 1] == slot[b + NU - 1]
    return slot, needed, loads


HI_SLOT = NU - 1
RING_SLOT, RING_NEEDED, RING_LOADS = ring_plan()
REC_QUARTERS = 4 * 8


class Chain:

    def __init__(self, eng, semaphore, base=0):
        self.eng, self.semaphore, self.base, self.n = eng, semaphore, base, 0

    def __call__(self, ins):
        self.n += 1
        ins.then_inc(self.semaphore, 1)
        self.eng.wait_ge(self.semaphore, self.base + self.n)


class Arena:

    def __init__(self, tensor):
        self.tensor, self.at = tensor, 0

    def __call__(self, *shape):
        n = 1
        for s in shape:
            n *= s
        ap = self.tensor[:, self.at:self.at + n]
        self.at += n
        assert self.at <= self.tensor.shape[1], self.at
        if len(shape) == 2:
            return ap.rearrange("p (a b) -> p a b", a=shape[0])
        if len(shape) == 3:
            return ap.rearrange("p (a b c) -> p a b c", a=shape[0], b=shape[1])
        if len(shape) == 4:
            return ap.rearrange("p (a b c d) -> p a b c d", a=shape[0], b=shape[1], c=shape[2])
        return ap


def spread(ap, axis, n):
    a = ap.unsqueeze(axis)
    shape = list(a.shape)
    shape[axis] = n
    return a.broadcast_to(shape)


def hybrid_trunk(nc, x, norm_mix, norm_ffn, att_w_in, att_w_out, cmp_pe_k, cmp_w1_k, cmp_w2_k, cmp_pe_v,
                 cmp_w1_v, cmp_w2_v, rec_w_in, rec_lb_logits, rec_gnorm, rec_w_out, moe_w_grp, moe_b_grp,
                 moe_w_exp, moe_b_exp, moe_w_gate, moe_w_up, moe_w_down, final_norm, out):
    ctx = ExitStack()
    with ctx:
        address = {}

        def sb(name, shape, dt=F32):
            address[name] = (nc.sbuf_base + 31) // 32 * 32
            return ctx.enter_context(nc.sbuf_tensor(name, shape, dt))

        class Signals(dict):
            def __missing__(self, name):
                self[name] = ctx.enter_context(nc.semaphore(name))
                return self[name]

        s = Signals()

        SB_BANKS = (4, 5, 0, 1)

        ring = sb("ring", [P, NU, UW])
        h = sb("h", [P, TT, D])
        xg = sb("xg", [P, TT, D])
        xT = sb("xT", [P, KD, T])
        gain = sb("gain", [P, D])
        ident = sb("ident", [P, P])
        ones = sb("ones", [P, P])
        earlier = sb("earlier", [P, P])
        iota_slot = sb("iota_slot", [P, CAP])
        iota_exp = sb("iota_exp", [P, NE])
        iota_i = sb("iota_i", [P, NE], I32)
        norm_sum = sb("norm_sum", [P, 2 * NL + 1, TT])
        norm_rstd = sb("norm_rstd", [P, 2 * NL + 1, TT])
        eps_col = sb("eps_col", [P, 1])
        w_route = sb("w_route", [P, KD, GR + NE])
        b_route = sb("b_route", [P, GR + NE])
        logit = sb("logit", [P, TT, GR + NE])
        route_t = sb("route_t", [P, 4, TT, NE])
        route_s = sb("route_s", [P, 16, TT])
        chosen = sb("chosen", [P, 2, TT, NE])
        member = sb("member", [P, TT, NE])
        slot_of = sb("slot_of", [P, TT, NE])
        share = sb("share", [P, TT, NE])
        weight = sb("weight", [P, 2, TT])
        passes_f = sb("passes_f", [P, PASS_MAX])
        passes = [sb(f"passes{l}", [1, 1], I32) for l in range(NL)]
        lb_rows = sb("lb_rows", [P, P])[:, :]
        gnorm = sb("gnorm", [P, RV])[:, :]
        arena_t = sb("arena", [P, 19600])

        psum = ctx.enter_context(nc.psum_tensor("psum", [P, 8, 512], F32))

        def bank(b):
            return psum[:, b, :]

        spare = arena_t[:, 0:SPARE * UW].rearrange("p (s w) -> p s w", s=SPARE)
        tail = SPARE * UW
        a = Arena(arena_t)
        qT = a(4, T)
        kv2 = a(2, NSA_G + 1, T)
        ksw = a(2, T)
        vsw = a(TT, 280)
        qbT = a(4, T)
        kbT = a(4, T)
        vb = a(TT, SB_H * DH)
        scores = a(2, HPG, T)
        probsT = a(2, TT, 512)
        ztmp = a(3, 384)
        zt = a(3, 384)
        za = a(2, 384)
        w2 = a(2, DH)
        pe_rows = a(2, P)
        causal = a(2, P)
        cmp_bias = a(2)
        cmp_x = a(2, 2 * NC)
        cmp_g = a(2, 2 * NC)
        cmp_h = a(2, 2 * NC)
        hv4 = a(NSA_G, 4, 32)
        vc4 = a(NSA_G, DH)
        cp = a(TT, NSA_H, 32)
        pcT = a(NSA_G, T)
        before_query = a(P)
        later_own = a(P)
        att_front = a.at
        a.at = tail
        oT = a(8, T)
        later_all = a(P)
        kcT = a(NC)
        cmask = a(TT, NC)
        cvis = a(TT, NC)
        cs = a(TT, NSA_H, NC)
        gates = a(TT, 3 * NSA_H)
        cstat = a(4, TT * NSA_H)
        stat = a(2, 4, HPG)
        square = qbT.rearrange("p h t -> p (h t)")
        att_end = a.at
        assert att_front <= tail, (att_front, tail)

        a = Arena(arena_t)
        rA, rD, rQ, r3 = (a(RH, T) for _ in range(4))
        rv = a(TT, D)
        rC, r1, r2 = (a(RH, T) for _ in range(3))
        assert a.at == tail
        rB = a(RH, T)
        reset = gain[:, :]
        last_state = a(RH * RV)
        states = [xT[:, 0:4, :].rearrange("p k t -> p (k t)"), xT[:, 4:8, :].rearrange("p k t -> p (k t)"),
                  last_state]
        decay = a(RH, NCH)
        lb = a(2 * RH)
        lbt = a(4, RH)
        ostat = a(3, TT * RH)
        rec_end = a.at
        koR = rB.rearrange("p h t -> p (h t)").rearrange("p (t d) -> p t d", t=TT)
        aM = rA
        o_rows = r1.rearrange("p h t -> p (h t)").rearrange("p (t d) -> p t d", t=TT)
        e_gate = rC.rearrange("p h t -> p (h t)").rearrange("p (t d) -> p t d", t=TT)
        recT = rB
        square_rec = r2.rearrange("p h t -> p (h t)")[:, 0:D]

        def rounded(name, shape, place, at=0):
            return nc.alloc_sbuf_tensor_at(name, shape, F32R, offset=address[place] + at)

        x_hi = rounded("x_hi", [P, KD, T], "xT")
        x_lo = rounded("x_lo", [P, TT, KD, P], "xg")
        w_hi = rounded("w_hi", [P, 2, KD, 256], "ring", 4 * UW * HI_SLOT)
        w_lo = rounded("w_lo", [P, NU, KD, 512], "ring")

        def quarter_hi(r):
            return w_hi[:, r % 4 // 2, :, r % 2 * P:(r % 2 + 1) * P]

        def quarter_lo(r):
            return w_lo[:, RING_SLOT[BASE_REC + r // 4], :, r % 4 * P:(r % 4 + 1) * P]

        def quarter(r):
            return ring[:, RING_SLOT[BASE_REC + r // 4], :]\
                .rearrange("p (k n) -> p k n", k=KD)[:, :, r % 4 * P:(r % 4 + 1) * P]

        def split_low(eng, r):
            eng.wait_ge(s["w_hi"], r + 1)
            eng.tensor_tensor(quarter_lo(r), quarter(r), quarter_hi(r).bitcast(F32), ALU.subtract)\
                .then_inc(s["w_lo_odd" if r % 2 else "w_lo_even"], 1)

        a = Arena(arena_t)
        a.at = tail
        slots = a(TT, QE, CAP)
        slots_share = a(TT, QE, CAP)
        shareT = a(TT, P)
        egate = a(FF)
        hid_t = a(FF)
        hid = a(FF)
        hidT = a(KF, P)
        a.at = tail + RH * T
        square_moe = a(D)
        moe_end = a.at
        gatheredT = xT[:, 0:4, :].rearrange("p k t -> p (k t)").rearrange("p (k c) -> p k c", k=KD)
        y_rows = xT[:, 4:8, :].rearrange("p k t -> p (k t)")

        block = ctx.enter_context(nc.Block())

        def arrival(u, n=0):
            return s[f"unit{RING_SLOT[u]}_loaded"], 32 * (RING_LOADS[u] + n)

        def load(sp, dst, parts, arrived, before):
            for i, (part, src) in enumerate(parts):
                if i == 1 and before is not None:
                    sp.wait_ge(*before)
                sp.dma_start(part(dst), src).then_inc(arrived if i < 2 else s["cmp_w1_rest"], 16)

        def load_ring(sp, u, parts, n=0, before=None):
            if RING_NEEDED[u]:
                sp.wait_ge(s["unit_used"], RING_NEEDED[u] + NU * n)
            if before is None and u >= 1:
                before = arrival(u - 1, n)
            load(sp, ring[:, RING_SLOT[u], :], parts, arrival(u, n)[0], before)

        def load_spare(sp, l, i, parts, before=None):
            load(sp, spare[:, i, :], parts, s[f"spare{i}_loaded"], before or (s[f"spare{i - 1}_loaded"], 32 * (l + 1)))

        def cols(w, c0, n):
            v = w.rearrange("(p k) n -> p k n", k=KD)[:, :, c0:c0 + n]
            half = KD // 2
            return [(lambda r, i=i: r[:, 0:KD * n].rearrange("p (k n) -> p k n", k=KD)[:, i * half:(i + 1) * half, :],
                     v[:, i * half:(i + 1) * half, :]) for i in range(2)]

        def out_cols(w, c0):
            v = w.rearrange("(j p) n -> p j n", p=P)[:, :, c0:c0 + 512]
            return [(lambda r, i=i: r.rearrange("p (j n) -> p j n", n=512)[:, 4 * i:4 * i + 4, :],
                     v[:, 4 * i:4 * i + 4, :]) for i in range(2)]

        def quad_units(l, q):
            wg = moe_w_gate[l].rearrange("(q e) (p c r) f -> q c p e (r f)", e=QE, p=P, c=KD // 2)
            wu = moe_w_up[l].rearrange("(q e) (p c r) f -> q c p e (r f)", e=QE, p=P, c=KD // 2)
            wd = moe_w_down[l].rearrange("(q e) (p j) n -> q j p e n", e=QE, j=KF)
            for c in range(KD // 2):
                yield [(lambda r, i=i: r.rearrange("p (w e f) -> p w e f", w=2, e=QE)[:, i], w[q][c])
                       for i, w in enumerate((wg, wu))]
            for j in range(KF):
                v = wd[q][j]
                yield [(lambda r, i=i: r.rearrange("p (e n) -> p e n", e=QE)[:, 2 * i:2 * i + 2],
                        v[:, 2 * i:2 * i + 2]) for i in range(2)]

        @block.sync
        def _(sp):
            for t in range(TT):
                sp.dma_start(h[:, t, :], x[0, t * P:(t + 1) * P, :]).then_inc(s["x_loaded"], 16)
            att, w_out = att_w_in[0], att_w_out[0]
            plan = [cols(att, 0, 512), cols(att, C_KC, 512), cols(att, C_KW, 280),
                    [(lambda r, i=i, odd=odd: r.rearrange("p (w j n) -> p w j n", w=2, n=P)[odd * DH:(odd + 1) * DH, i],
                      w[0].rearrange("(j odd d) n -> odd d j n", odd=2, d=DH)[odd])
                     for i, w in enumerate((cmp_w1_k, cmp_w1_v)) for odd in range(2)],
                    cols(att, C_QB, 512), cols(att, C_KB, 512), cols(att, C_VB, 512),
                    out_cols(w_out, 0), out_cols(w_out, 512)]
            assert len(plan) == ATT_UNITS
            for u, parts in enumerate(plan):
                load_ring(sp, u, parts)

            rec, w_out = rec_w_in[0], rec_w_out[0]
            plan_rec = [cols(rec, c, 512) for c in (1024, 1536, 0, 512, 2048, 2560, 3072, 3584)]
            plan_rec += [out_cols(w_out, 0), out_cols(w_out, 512)]
            assert len(plan_rec) == REC_UNITS

            before = 0
            for l in range(NL):
                if l:
                    for i, parts in enumerate(plan_rec):
                        load_ring(sp, BASE_REC + i, parts, before)
                quads = [list(quad_units(l, q)) for q in range(2)]
                base = BASE_MOE[l]
                for i in range(3):
                    load_ring(sp, base + i, quads[0][i], before)
                sp.wait_ge(*((s["a_used"], 1) if l else (s["sb_pv"], SB_H)))
                for i in range(SPARE):
                    if l and i == SPARE - 2:
                        sp.wait_ge(s["recT_psum"], 4)
                    load_spare(sp, l, i, quads[1][i], arrival(base + 2, before) if i == 0 else None)
                for i in range(3, NU):
                    load_ring(sp, base + i, quads[0][i], before,
                              (s[f"spare{SPARE - 1}_loaded"], 32 * (l + 1)) if i == 3 else None)
                for i in (4, 5):
                    load_ring(sp, base + NU + i - SPARE, quads[1][i], before)
                with sp.Fori(2, NQ) as q:
                    for i, parts in enumerate(quad_units(l, q)):
                        load_ring(sp, BASE_LOOP[l] + i, parts, q - 2 + before)
                sp.wait_ge(s["passes_ready"], l + 1)
                more = sp.value_load(passes[l][0:1, 0:1], min_val=0, max_val=PASS_MAX - 1)
                with sp.If(more > 0):
                    with sp.Fori(0, more) as r:
                        with sp.Fori(0, NQ) as q:
                            for i, parts in enumerate(quad_units(l, q)):
                                load_ring(sp, BASE_LOOP[l] + i, parts, q + NQ * (r + 1) - 2 + before)
                before = before + NQ * more
            for t in range(TT):
                sp.wait_ge(s["xg_done"], 2 * 2 * NL + t + 1)
                sp.dma_start(out[0, t * P:(t + 1) * P, :], xg[:, t, :]).then_inc(s["out_done"], 16)
            sp.wait_ge(s["out_done"], 16 * TT)

        @block.gpsimd
        def _(pool):
            link = Chain(pool, s["pool_chain"])

            def gain_load(v):
                src = [norm_mix[0], norm_ffn[0], norm_mix[1], norm_ffn[1], final_norm][v]
                if v:
                    pool.wait_ge(s["xg_done"], TT * v)
                pool.dma_start(gain[:, :], src.partition_broadcast(P)).then_inc(s["gain_loaded"], 16)

            def route_load(l):
                if l:
                    pool.wait_ge(s["route_used"], l)
                pool.dma_start(w_route[:, :, 0:GR], moe_w_grp[l].rearrange("(p k) n -> p k n", k=KD))\
                    .then_inc(s["route_loaded"], 16)
                pool.dma_start(w_route[:, :, GR:], moe_w_exp[l].rearrange("(p k) n -> p k n", k=KD))\
                    .then_inc(s["route_loaded"], 16)
                pool.dma_start(b_route[:, 0:GR], moe_b_grp[l].partition_broadcast(P))\
                    .then_inc(s["route_loaded"], 16)
                pool.dma_start(b_route[:, GR:], moe_b_exp[l].partition_broadcast(P))\
                    .then_inc(s["route_loaded"], 16)

            link(pool.memset(ident[:, :], 0.0))
            pool.affine_select(out=ident[:, :], in_=ident[:, :], compare_op=ALU.not_equal, fill=1.0, base=0,
                               pattern=[[-1, P]], channel_multiplier=1).then_inc(s["ident_done"], 1)
            pool.memset(eps_col[:, :], EPS).then_inc(s["eps_done"], 1)
            pool.memset(kv2[:, :, NSA_G, :], 0.0).then_inc(s["kv2_zero"], 1)
            route_load(0)

            link(pool.memset(causal[:, :, :], 0.0))
            link(pool.affine_select(out=causal[:, 1, :], in_=causal[:, 1, :], compare_op=ALU.is_ge, fill=NEG,
                                    base=0, pattern=[[-1, P]], channel_multiplier=1))
            link(pool.memset(cmask[:, :, :], 0.0))
            link(pool.memset(cvis[:, :, :], 1.0))
            for dst, fill in ((cmask, NEG), (cvis, 0.0)):
                link(pool.affine_select(out=dst[:, :, :], in_=dst[:, :, :], compare_op=ALU.is_ge, fill=fill,
                                        base=1 - CMP_LEN, pattern=[[P, TT], [-CMP_STRIDE, NC]],
                                        channel_multiplier=1))
            link(pool.memset(later_all[:, :], -1.0))
            link(pool.affine_select(out=later_own[:, :], in_=later_all[:, :], compare_op=ALU.is_ge, fill=0.0,
                                    base=0, pattern=[[-1, P]], channel_multiplier=1))
            link(pool.memset(cp[:, :, :, :], 0.0))
            link(pool.memset(hv4[:, :, :, :], 0.0))
            link(pool.memset(ones[:, :], 1.0))
            link(pool.affine_select(out=earlier[:, :], in_=ones[:, :], compare_op=ALU.is_gt, fill=0.0, base=0,
                                    pattern=[[1, P]], channel_multiplier=-1))
            link(pool.iota(iota_i[:, :], pattern=[[1, NE]], base=0, channel_multiplier=0))
            link(pool.tensor_copy(iota_exp[:, :], iota_i[:, :]))
            link(pool.tensor_copy(iota_slot[:, :], iota_i[:, 0:CAP]))
            link(pool.memset(before_query, 0.0))
            pool.affine_select(out=before_query, in_=before_query, compare_op=ALU.is_gt, fill=NEG, base=0,
                               pattern=[[1, P]], channel_multiplier=-1).then_inc(s["const_done"], 1)

            gain_load(1)
            gain_load(2)

            rlink = Chain(pool, s["pool_rec_chain"])
            pool.wait_ge(s["xg_done"], 3 * TT)
            rlink(pool.memset(reset, 1.0))
            pool.memset(reset.rearrange("p (c i) -> p c i", i=CH)[:, :, 0:1], 0.0).then_inc(s["rec_const"], 1)
            route_load(1)
            def left(hh):
                sl = slice(4 * hh, 4 * hh + 4)
                cum = rB[:, sl, :].rearrange("p h (c i) -> p (h c) i", i=CH)
                pool.wait_ge(s["rec_cum"], hh + 1)
                pool.tensor_tensor(rD[:, sl, :].rearrange("p h (c i) -> p (h c) i", i=CH),
                                   cum[:, :, CH - 1:CH].broadcast_to([P, 4 * NCH, CH]), cum, ALU.subtract)\
                    .then_inc(s["rec_left"], 1)

            def k_out(hh):
                sl = slice(4 * hh, 4 * hh + 4)
                pool.wait_ge(s["rec_exps"], 4 * hh + 4)
                pool.tensor_tensor(rD[:, sl, :], rD[:, sl, :], rA[:, sl, :], ALU.mult)\
                    .then_inc(s["rec_kout"], 1)

            def k_in(hh):
                sl = slice(4 * hh, 4 * hh + 4)
                pool.tensor_tensor(r2[:, sl, :], r2[:, sl, :], rA[:, sl, :], ALU.mult)\
                    .then_inc(s["rec_kin"], 1)

            split_low(pool, 1)
            split_low(pool, 3)
            for m in range(16):
                if 2 * m + 5 < REC_QUARTERS:
                    split_low(pool, 2 * m + 5)
                if m in (4, 6):
                    left(m // 2 - 2)
                if m in (7, 9):
                    k_out((m - 7) // 2)
                if m in (8, 10):
                    k_in((m - 8) // 2)
            gain_load(3)
            pool.wait_ge(s["rec_kout"], 2)
            pool.wait_ge(s["rec_kin"], 2)
            pool.wait_ge(s["rec_kout_read"], 1)
            aMv = aM.rearrange("p h t -> p (h t)").rearrange("p (g t) -> p g t", t=P)
            pool.memset(aMv[0:CH, :, CH:P], 0.0).then_inc(s["rec_zero"], 1)
            pool.memset(aMv[CH:P, :, 0:CH], 0.0).then_inc(s["rec_zero"], 1)
            pool.wait_ge(s["rec_zero"], 2)
            for b in range(4):
                pool.wait_ge(s["rec_a_copied"], 2 * b + 2)
                v = aMv[:, 4 * b:4 * b + 4, :]
                pool.affine_select(out=v, in_=v, compare_op=ALU.is_ge, fill=0.0, base=0,
                                   pattern=[[0, 4], [1, P]], channel_multiplier=-1)\
                    .then_inc(s["rec_a_masked"], 1)
            gain_load(4)

        COMBINE_BANKS = (7, 2, 0, 1)
        H_NEEDED = [None] + [(4 * v - 2, 4 * v) for v in range(1, 2 * NL + 1)]

        @block.scalar
        def _(act):
            link = Chain(act, s["act_chain"])

            def norm(v, t, buf):
                if v == 0:
                    act.wait_ge(s["x_loaded"], 32)
                    act.wait_ge(s["eps_done"], 1)
                else:
                    act.wait_ge(s["h_done"], H_NEEDED[v][t])
                link(act.activation(buf, h[:, t, :], ACT.Square, accum_out=norm_sum[:, v, t:t + 1]))
                link(act.activation(norm_sum[:, v, t:t + 1], norm_sum[:, v, t:t + 1], ACT.Ln,
                                    bias=eps_col[:, 0:1], scale=1.0 / D))
                act.activation(norm_rstd[:, v, t:t + 1], norm_sum[:, v, t:t + 1], ACT.Exp, scale=-0.5)\
                    .then_inc(s["norm_rstd"], 1)

            def xT_half(v, t):
                act.wait_ge(s["xT_psum"], 4 * v + 2 * t + 1)
                act.activation((x_hi if v == 2 else xT)[:, 0:4, t * P:(t + 1) * P],
                               bank(2 * t).rearrange("p (k t) -> p k t", k=4), ACT.Copy)\
                    .then_inc(s["xT_done"], 1)

            act.preload_act_table_set("natural_log_exp_and_others")
            act.dma_start(gain[:, :], norm_mix[0].partition_broadcast(P)).then_inc(s["gain_first"], 16)
            for i, pe in enumerate((cmp_pe_k, cmp_pe_v)):
                act.dma_start(pe_rows[0:LP, i, :], pe[0].rearrange("(j two) d -> j (two d)", two=2))\
                    .then_inc(s["cmp_small"], 16)
            for i, w in enumerate((cmp_w2_k, cmp_w2_v)):
                act.dma_start(w2[:, i, :], w[0]).then_inc(s["cmp_small"], 16)
            act.dma_start(lb_rows[0:2 * RH, :], rec_lb_logits.rearrange("l (h p) -> (l h) p", p=RK))\
                .then_inc(s["rec_small"], 16)
            act.dma_start(gnorm[:, :], rec_gnorm[0].partition_broadcast(P)).then_inc(s["rec_small"], 16)
            for t in range(TT):
                norm(0, t, square)
            for t in range(TT):
                xT_half(0, t)

            def proj(n):
                act.wait_ge(s["proj_psum"], n + 1)
                src = bank(n % 2)
                if n == 0:
                    act.activation(qT[:, 0:2, :], src.rearrange("p (a t) -> p a t", a=2), ACT.Copy,
                                   scale=DH ** -0.5).then_inc(s["proj_even"], 1)
                elif n == 2:
                    last = None
                    for kv in range(2):
                        for g in range(NSA_G):
                            part = bank(0)[g * DH:(g + 1) * DH, kv * T:(kv + 1) * T]
                            act.activation(kv2[0:DH, kv, g, :], part, ACT.Copy).then_inc(s["kv2_done"], 1)
                            last = act.activation(kv2[DH:P, kv, g, 0:T - 1], part[:, 1:T], ACT.Copy)
                            if (kv, g) != (1, 1):
                                last.then_inc(s["kv2_done"], 1)
                    last.then_inc(s["proj_even"], 1)
                elif n == 4:
                    act.activation(vsw[:, 0, :], src[:, 0:280], ACT.Copy).then_inc(s["proj_even"], 1)
                elif n == 6:
                    act.activation(qbT[:, 0:2, :], src.rearrange("p (a t) -> p a t", a=2), ACT.Copy,
                                   scale=DH ** -0.5).then_inc(s["proj_even"], 1)
                elif n == 8:
                    act.activation(kbT[:, 0:2, :], src.rearrange("p (a t) -> p a t", a=2), ACT.Copy)\
                        .then_inc(s["proj_even"], 1)
                elif n == 10:
                    act.activation(vb[:, 0, :], src, ACT.Copy).then_inc(s["proj_even"], 1)

            proj(0)
            proj(2)
            act.wait_ge(s["cmp_inner"], 1)
            act.activation(cmp_g, cmp_g, ACT.Exp, scale=-2.0 * GELU_A).then_inc(s["cmp_exp"], 1)
            proj(4)
            act.wait_ge(s["cmp_kv"], 1)
            act.activation(kcT[0:DH, :], bank(5)[0:DH, 0:NC], ACT.Copy).then_inc(s["cmp_kv_done"], 1)
            act.activation(kcT[DH:P, :], bank(5)[0:DH, NC:2 * NC], ACT.Copy).then_inc(s["cmp_kv_done"], 1)
            act.activation(vc4, bank(5)[:, 64:192].rearrange("p (g d) -> p g d", g=2), ACT.Copy)\
                .then_inc(s["cmp_kv_done"], 1)
            act.wait_ge(s["proj_even"], 3)
            act.wait_ge(s["proj_odd"], 3)
            act.activation(gates, vsw[:, :, C_GATE - C_KW:280], ACT.Exp, scale=-1.0)\
                .then_inc(s["gate_exp"], 1)
            act.wait_ge(s["cmp_shifted"], 1)
            act.activation(cs, cs, ACT.Exp).then_inc(s["cmp_probs"], 1)

            def exps(u):
                nk = P * (u // 4 + 1)
                act.wait_ge(s["nsa_max"], u + 1)
                for i in range(HPG):
                    v = scores[:, u % 2, i, 0:nk]
                    act.activation(v, v, ACT.Exp, bias=stat[:, u % 2, 0, i:i + 1],
                                   accum_out=stat[:, u % 2, 1, i:i + 1]).then_inc(s["nsa_exp"], 1)

            exps(0)
            for u in range(8):
                if u + 1 < 8:
                    exps(u + 1)
                if 6 + u in (6, 8, 10):
                    proj(6 + u)
                if u == 0:
                    act.wait_ge(s["cmp_pT"], 1)
                    act.activation(pcT, bank(5).rearrange("p (g t) -> p g t", g=2), ACT.Copy)\
                        .then_inc(s["cmp_pT_done"], 1)
                act.wait_ge(s["nsa_pT"], u + 1)
                if u >= 2:
                    act.wait_ge(s["nsa_pv"], u - 1)
                act.activation(probsT[:, u % 2, 0, :], bank(2), ACT.Copy).then_inc(s["nsa_pT_even"], 1)

            def exp_ln(hd):
                act.wait_ge(s["sb_z"], hd + 1)
                if hd >= 3:
                    act.wait_ge(s["sb_t"], hd - 2)
                v = ztmp[:, hd % 3, :]
                link(act.activation(v, bank(SB_BANKS[hd % 4])[:, 0:384], ACT.Abs))
                link(act.activation(v, v, ACT.Exp, scale=-1.0))
                act.activation(v, v, ACT.Ln, bias=1.0).then_inc(s["sb_ln"], 1)

            exp_ln(0)
            act.wait_ge(s["nsa_pv"], 8)
            for g in range(NSA_G):
                act.activation(oT[:, 2 * g:2 * g + 2, :], bank(6 + g).rearrange("p (a t) -> p a t", a=2), ACT.Copy)\
                    .then_inc(s["oT_done"], 1)
            for hd in range(SB_H):
                if hd + 1 < SB_H:
                    exp_ln(hd + 1)
                act.wait_ge(s["sb_e"], hd + 1)
                if hd >= 2:
                    act.wait_ge(s["sb_pv"], hd - 1)
                act.activation(za[:, hd % 2, :], bank(SB_BANKS[hd % 4])[:, 0:384], ACT.Exp).then_inc(s["sb_a"], 1)

            def route(l):
                act.wait_ge(s["route_diff"], l + 1)
                for t in range(TT):
                    act.activation(route_t[:, 3, t, 0:GR], logit[:, t, 0:GR], ACT.Exp,
                                   bias=route_s[:, 0, t:t + 1], accum_out=route_s[:, 1, t:t + 1])\
                        .then_inc(s["route_exp"], 1)
                act.activation(route_s[:, 5, :], route_s[:, 4, :], ACT.Exp).then_inc(s["route_exp"], 1)

            def quad(l, n):
                act.wait_ge(s[f"gathered{l}"], 2 * n + 1)
                act.activation(gatheredT[:, 0:4, :], bank(0).rearrange("p (k c) -> p k c", k=4), ACT.Copy)\
                    .then_inc(s[f"gatheredT{l}"], 1)
                act.wait_ge(s[f"gate_up{l}"], n + 1)
                act.activation(egate, bank(3)[:, 0:FF], ACT.Exp, scale=-1.0).then_inc(s[f"act_quad{l}"], 1)
                act.wait_ge(s[f"act_quad{l}"], 2 * n + 1)
                act.activation(egate, egate, ACT.Ln, bias=1.0).then_inc(s[f"act_quad{l}"], 1)
                act.wait_ge(s[f"act_quad{l}"], 2 * n + 2)
                act.activation(egate, egate, ACT.Exp, scale=-1.0).then_inc(s[f"egate{l}"], 1)
                act.wait_ge(s[f"hid_psum{l}"], n + 1)
                act.activation(hidT, bank(4)[:, 0:FF].rearrange("p (j c) -> p j c", j=KF), ACT.Copy)\
                    .then_inc(s[f"hidT{l}"], 1)
                act.activation(shareT, bank(4)[:, FF:2 * FF].rearrange("p (t c) -> p t c", t=TT), ACT.Copy)\
                    .then_inc(s[f"shareT{l}"], 1)
                act.wait_ge(s[f"down{l}"], n + 1)
                act.activation(y_rows[:, 0:512], bank(5), ACT.Copy).then_inc(s[f"y_rows{l}"], 1)

            def experts(l):
                route(l)
                for q in range(2):
                    quad(l, q)
                with act.Fori(2, NQ) as q:
                    quad(l, q)
                act.wait_ge(s["passes_ready"], l + 1)
                more = act.value_load(passes[l][0:1, 0:1], min_val=0, max_val=PASS_MAX - 1)
                with act.If(more > 0):
                    with act.Fori(0, more) as r:
                        with act.Fori(0, NQ) as q:
                            quad(l, q + NQ * (r + 1))
                return NQ * more

            def norm_and_xT(v):
                for t in range(TT):
                    norm(v, t, square_moe)
                    xT_half(v, t)

            norm_and_xT(1)
            before = experts(0)

            norm_and_xT(2)
            act.wait_ge(s["lb_diff"], 1)
            act.activation(lbt[:, 0:2, :], lbt[:, 0:2, :], ACT.Exp).then_inc(s["lb_exp"], 1)
            def split_high(r):
                if r == 0:
                    act.wait_ge(s["unit_used"], BASE_REC + NU * before)
                elif r >= 4:
                    act.wait_ge(s["rec_psum"], r - 3 if r < 20 else r // 2 * 2 - 2)
                if r % 4 == 0:
                    act.wait_ge(*arrival(BASE_REC + r // 4, before))
                act.activation(quarter_hi(r), quarter(r), ACT.Copy).then_inc(s["w_hi"], 1)

            def f_exp(m):
                act.activation(rA[:, 2 * m:2 * m + 2, :], bank(m).rearrange("p (a t) -> p a t", a=2), ACT.Exp)\
                    .then_inc(s["rec_f"], 1)

            def log_f(hh):
                sl = slice(4 * hh, 4 * hh + 4)
                act.wait_ge(s["rec_key"], 2 * hh + 2)
                act.activation(rC[:, sl, :], rA[:, sl, :], ACT.Ln, bias=1.0, scale=-1.0)\
                    .then_inc(s["rec_logf"], 1)

            def decay_exps(hh, first):
                sl = slice(4 * hh, 4 * hh + 4)
                if first:
                    act.wait_ge(s["rec_cum"], hh + 1)
                    act.activation(r3[:, sl, :], rB[:, sl, :], ACT.Exp).then_inc(s["rec_exps"], 1)
                    act.wait_ge(s["rec_rel"], hh + 1)
                    act.activation(r1[:, sl, :], rC[:, sl, :], ACT.Exp).then_inc(s["rec_exps"], 1)
                else:
                    act.activation(r2[:, sl, :], rC[:, sl, :], ACT.Exp, scale=-1.0).then_inc(s["rec_exps"], 1)
                    act.wait_ge(s["rec_left"], hh + 1)
                    act.activation(rD[:, sl, :], rD[:, sl, :], ACT.Exp).then_inc(s["rec_exps"], 1)

            def gate_sigmoid(i):
                v = e_gate[:, :, i * 256:(i + 1) * 256]
                link(act.activation(v, bank(4 + i).rearrange("p (t n) -> p t n", t=TT), ACT.Exp, scale=-1.0))
                link(act.activation(v, v, ACT.Ln, bias=1.0))
                act.activation(v, v, ACT.Exp, scale=-1.0).then_inc(s["rec_gate_exp"], 1)

            for r in range(4):
                split_high(r)
            for m in range(16):
                for r in (2 * m + 4, 2 * m + 5):
                    if r < REC_QUARTERS:
                        split_high(r)
                act.wait_ge(s["rec_psum"], 2 * m + 2)
                if m < 4:
                    f_exp(m)
                if m in (3, 5):
                    log_f((m - 3) // 2)
                if m in (5, 6):
                    decay_exps(0, m == 5)
                if m in (7, 8):
                    decay_exps(1, m == 7)
                if 8 <= m < 12:
                    act.activation(rv[:, :, (m - 8) * 256:(m - 7) * 256],
                                   bank(m - 8).rearrange("p (t n) -> p t n", t=TT), ACT.Copy)\
                        .then_inc(s["rec_v"], 1)
                if m >= 12:
                    if m == 12:
                        act.wait_ge(s["rec_exps"], 8)
                    gate_sigmoid(m - 12)
            act.wait_ge(s["rec_left"], 2)
            act.wait_ge(s["rec_rel"], 2)
            for b in (0, 2):
                act.wait_ge(s["ko_psum"], b + 1)
                act.activation(koR[:, b // 2, (b % 2) * 512:(b % 2) * 512 + 512], bank(b), ACT.Copy)\
                    .then_inc(s["ko_done"], 1)
            aMv = aM.rearrange("p h t -> p (h t)").rearrange("p (g t) -> p g t", t=P)
            act.wait_ge(s["rec_zero"], 2)
            for b in range(4):
                act.wait_ge(s["a_psum"], b + 1)
                for lo in (0, CH):
                    act.activation(aMv[lo:lo + CH, 4 * b:4 * b + 4, lo:lo + CH],
                                   bank(4 + b)[lo:lo + CH, :].rearrange("p (g t) -> p g t", g=4)[:, :, lo:lo + CH],
                                   ACT.Copy).then_inc(s["rec_a_copied"], 1)
            act.wait_ge(s["rec_kin_used"], 1)
            for t in range(TT):
                act.wait_ge(s["o_psum"], t + 1)
                o_ps = psum[:, 4 + 2 * t:6 + 2 * t, :].rearrange("p b n -> p (b n)")
                act.activation(square_rec, o_ps, ACT.Square).then_inc(s["o_square"], 1)
                act.wait_ge(s["o_sum"], t + 1)
                v = ostat[:, 0, t * RH:(t + 1) * RH]
                link(act.activation(v, v, ACT.Ln, bias=eps_col[:, 0:1], scale=1.0 / RV))
                act.activation(ostat[:, 1, t * RH:(t + 1) * RH], v, ACT.Exp, scale=-0.5)\
                    .then_inc(s["o_rstd"], 1)
            for b in (0, 2):
                act.wait_ge(s["recT_psum"], b + 1)
                act.activation(recT[:, 4 * (b % 2):4 * (b % 2) + 4, (b // 2) * P:(b // 2 + 1) * P],
                               bank(b).rearrange("p (k t) -> p k t", k=4), ACT.Copy).then_inc(s["recT_done"], 1)

            norm_and_xT(3)
            experts(1)
            for t in range(TT):
                norm(4, t, square_moe)

        @block.vector
        def _(dve):
            link = Chain(dve, s["dve_chain"])

            def norm(v, t):
                dve.wait_ge(s["norm_rstd"], TT * v + t + 1)
                if v == 0:
                    dve.wait_ge(s["gain_first"], 16)
                else:
                    dve.wait_ge(s["gain_loaded"], 16 * v)
                dve.scalar_tensor_tensor(out=xg[:, t, :], in0=h[:, t, :], scalar=norm_rstd[:, v, t:t + 1],
                                         in1=gain[:, :], op0=ALU.mult, op1=ALU.mult)\
                    .then_inc(s["xg_done"], 1)

            def xT_half(v, t):
                dve.wait_ge(s["xT_psum"], 4 * v + 2 * t + 2)
                dve.tensor_copy((x_hi if v == 2 else xT)[:, 4:8, t * P:(t + 1) * P],
                                bank(2 * t + 1).rearrange("p (k t) -> p k t", k=4)).then_inc(s["xT_done"], 1)
                if v == 2:
                    dve.wait_ge(s["xT_done"], 4 * v + 2 * t + 2)
                    dve.tensor_tensor(x_lo[:, t],
                                      psum[:, 2 * t:2 * t + 2, :].rearrange("p b (k c) -> p (b k) c", k=4),
                                      x_hi[:, :, t * P:(t + 1) * P].bitcast(F32), ALU.subtract).then_inc(s["x_lo_done"], 1)

            for t in range(TT):
                norm(0, t)
            for t in range(TT):
                xT_half(0, t)

            def proj(n):
                dve.wait_ge(s["proj_psum"], n + 1)
                src = bank(n % 2)
                pair = src.rearrange("p (a t) -> p a t", a=2)
                if n in (1, 7):
                    dst = (qT if n == 1 else qbT)[:, 2:4, :]
                    ins = dve.tensor_scalar(dst, pair, DH ** -0.5, None, ALU.mult)
                elif n == 3:
                    ins = dve.tensor_copy(ksw, pair)
                elif n == 5:
                    ins = dve.tensor_copy(vsw[:, 1, :], src[:, 0:280])
                elif n == 9:
                    ins = dve.tensor_copy(kbT[:, 2:4, :], pair)
                else:
                    ins = dve.tensor_copy(vb[:, 1, :], src)
                ins.then_inc(s["proj_odd"], 1)

            dve.wait_ge(s["pe_psum"], 1)
            dve.wait_ge(s["kv2_zero"], 1)
            dve.tensor_copy(kv2[:, :, NSA_G, 0:CMP_LEN:2], bank(5)[:, 0:2 * LP].rearrange("p (a j) -> p a j", a=2))\
                .then_inc(s["pe_done"], 1)
            proj(1)
            proj(3)
            dve.wait_ge(s["cmp_hidden"], 1)
            hidden = bank(4)[:, 0:P].rearrange("p (a n) -> p a n", a=2)
            link(dve.tensor_copy(cmp_bias, hidden[:, :, NSA_G * NC]))
            for kv in range(2):
                link(dve.tensor_scalar(cmp_x[:, kv, :], hidden[:, kv, 0:NSA_G * NC],
                                       cmp_bias[:, kv:kv + 1], None, ALU.add))
            link(dve.tensor_tensor(cmp_g, cmp_x, cmp_x, ALU.mult))
            link(dve.tensor_scalar(cmp_g, cmp_g, GELU_B, 1.0, ALU.mult, ALU.add))
            dve.tensor_tensor(cmp_g, cmp_g, cmp_x, ALU.mult).then_inc(s["cmp_inner"], 1)
            dve.wait_ge(s["cmp_exp"], 1)
            link(dve.tensor_scalar(cmp_g, cmp_g, 1.0, None, ALU.add))
            link(dve.reciprocal(cmp_g, cmp_g))
            dve.wait_ge(s["const_done"], 1)
            dve.tensor_tensor(cmp_h, cmp_x, cmp_g, ALU.mult).then_inc(s["cmp_h_done"], 1)
            dve.wait_ge(s["cmp_h_done"], 1)
            for g in range(NSA_G):
                dve.tensor_copy(hv4[:, g, :, 0:NC], spread(cmp_h[:, 1, g * NC:(g + 1) * NC], 1, 4))\
                    .then_inc(s["cmp_h_done"], 1)
            proj(5)
            dve.wait_ge(s["gate_exp"], 1)
            link(dve.tensor_scalar(gates, gates, 1.0, None, ALU.add))
            link(dve.reciprocal(gates, gates))
            dve.wait_ge(s["cmp_scores"], 1)
            for t in range(TT):
                for g in range(NSA_G):
                    c = t * HPG * NC
                    link(dve.tensor_tensor(cs[:, t, g * HPG:(g + 1) * HPG], bank(4 + g)[:, c:c + HPG * NC]
                                           .rearrange("p (h c) -> p h c", h=HPG),
                                           spread(cmask[:, t, :], 1, HPG), ALU.add))
            flat = cs.rearrange("p t h c -> p (t h) c")
            link(dve.tensor_reduce(cstat[:, 0, :], flat, AX.X, ALU.max))
            dve.tensor_tensor(flat, flat, spread(cstat[:, 0, :], 2, NC), ALU.subtract)\
                .then_inc(s["cmp_shifted"], 1)

            def mask(u):
                t, nk = u // 4, P * (u // 4 + 1)
                dve.wait_ge(s["nsa_scores"], u + 1)
                if u >= 2:
                    dve.wait_ge(s["nsa_pT"], u - 1)
                src = (psum[:, 4:6, :].rearrange("p b n -> p (b n)")[:, 0:HPG * nk]
                       .rearrange("p (i k) -> p i k", i=HPG))
                if t == 0:
                    m = spread(causal[:, 1, :], 1, HPG)
                else:
                    m = spread(causal.rearrange("p a k -> p (a k)"), 1, HPG)
                v = scores[:, u % 2, :, 0:nk]
                dve.tensor_tensor(v, src, m, ALU.add).then_inc(s["nsa_masked"], 1)
                dve.wait_ge(s["nsa_masked"], u + 1)
                dve.tensor_reduce(stat[:, u % 2, 0, :], v, AX.X, ALU.max, negate=True)\
                    .then_inc(s["nsa_max"], 1)

            def scale(u):
                t, br, g, nk = u // 4, u // 2 % 2, u % 2, P * (u // 4 + 1)
                dve.wait_ge(s["nsa_exp"], HPG * (u + 1))
                link(dve.reciprocal(stat[:, u % 2, 2, :], stat[:, u % 2, 1, :]))
                c = (br + 1) * NSA_H + g * HPG
                link(dve.tensor_tensor(stat[:, u % 2, 3, :], stat[:, u % 2, 2, :], gates[:, t, c:c + HPG], ALU.mult))
                v = scores[:, u % 2, :, 0:nk]
                dve.tensor_tensor(v, v, spread(stat[:, u % 2, 3, :], 2, nk), ALU.mult)\
                    .then_inc(s["nsa_scaled"], 1)

            mask(0)
            dve.wait_ge(s["cmp_probs"], 1)
            link(dve.tensor_reduce(cstat[:, 1, :], flat, AX.X, ALU.add))
            link(dve.reciprocal(cstat[:, 2, :], cstat[:, 1, :]))
            link(dve.tensor_tensor(cstat[:, 3, :].rearrange("p (t h) -> p t h", t=TT),
                                   cstat[:, 2, :].rearrange("p (t h) -> p t h", t=TT),
                                   gates[:, :, 0:NSA_H], ALU.mult))
            link(dve.tensor_tensor(flat, flat, spread(cstat[:, 3, :], 2, NC), ALU.mult))
            for t in range(TT):
                dve.tensor_tensor(cp[:, t, :, 0:NC], cs[:, t], spread(cvis[:, t, :], 1, NSA_H), ALU.mult)\
                    .then_inc(s["cmp_p_done"], 1)
            for u in range(8):
                if u + 1 < 8:
                    mask(u + 1)
                scale(u)
                if 6 + u in (7, 9, 11):
                    proj(6 + u)
                if u >= 4:
                    dve.wait_ge(s["nsa_pT"], u + 1)
                    if u >= 6:
                        dve.wait_ge(s["nsa_pv"], u - 1)
                    dve.tensor_copy(probsT[:, u % 2, 1, :], bank(3)).then_inc(s["nsa_pT_odd"], 1)

            for hd in range(SB_H):
                dve.wait_ge(s["sb_ln"], hd + 1)
                if hd >= 3:
                    dve.wait_ge(s["sb_e"], hd - 2)
                dve.scalar_tensor_tensor(out=zt[:, hd % 3, :], in0=bank(SB_BANKS[hd % 4])[:, 0:384], scalar=0.0,
                                         in1=ztmp[:, hd % 3, :], op0=ALU.max, op1=ALU.add)\
                    .then_inc(s["sb_t"], 1)
            dve.wait_ge(s["sb_pv"], SB_H)
            for b in range(2):
                dve.tensor_copy(oT[:, 4 + 2 * b:6 + 2 * b, :], bank(2 + b).rearrange("p (a t) -> p a t", a=2))\
                    .then_inc(s["oT_done"], 1)

            def add_mix(l, banks):
                for i, b in enumerate(banks):
                    t, n = divmod(i, 2)
                    dve.wait_ge(s["mix_psum"], 4 * l + i + 1)
                    dve.tensor_tensor(h[:, t, n * 512:(n + 1) * 512], bank(b), h[:, t, n * 512:(n + 1) * 512],
                                      ALU.add).then_inc(s["h_done"], 1)
                    if n == 1:
                        norm(2 * l + 1, t)
                        xT_half(2 * l + 1, t)

            def route(l):
                dve.wait_ge(s["route_psum"], l + 1)
                dve.wait_ge(s["route_loaded"], 64 * (l + 1))
                for t in range(TT):
                    ins = dve.tensor_tensor(logit[:, t, :], bank(4 + t)[:, 0:GR + NE], b_route[:, :], ALU.add)
                    ins.then_inc(s["route_logit"], 1)
                dve.wait_ge(s["route_logit"], TT * (l + 1))
                lg, le = logit[:, :, 0:GR], logit[:, :, GR:]
                t0, t1, t2 = route_t[:, 0], route_t[:, 1], route_t[:, 2]
                link(dve.tensor_reduce(route_s[:, 0, :], lg, AX.X, ALU.max, negate=True))
                link(dve.tensor_tensor(t0[:, :, 0:GR], lg, spread(route_s[:, 0, :], 2, GR), ALU.add))
                link(dve.tensor_scalar(t0[:, :, 0:GR], t0[:, :, 0:GR], 0.0, 1e6, ALU.is_lt, ALU.mult))
                link(dve.tensor_tensor(t0[:, :, 0:GR], t0[:, :, 0:GR], spread(iota_exp[:, 0:GR], 1, TT), ALU.add))
                link(dve.tensor_reduce(route_s[:, 2, :], t0[:, :, 0:GR], AX.X, ALU.min))
                link(dve.tensor_tensor(t1[:, :, 0:GR], spread(iota_exp[:, 0:GR], 1, TT),
                                       spread(route_s[:, 2, :], 2, GR), ALU.is_equal))
                link(dve.tensor_scalar(t1[:, :, 0:GR], t1[:, :, 0:GR], -1.0, -NEG, ALU.add, ALU.mult))
                for t in range(TT):
                    link(dve.tensor_tensor(t0[:, t, :].rearrange("p (g e) -> p g e", g=GR),
                                           le[:, t, :].rearrange("p (g e) -> p g e", g=GR),
                                           spread(t1[:, t, 0:GR], 2, EPG), ALU.add))
                for k in range(2):
                    link(dve.tensor_reduce(route_s[:, 6 + k, :], t0, AX.X, ALU.max))
                    link(dve.tensor_tensor(t1, t0, spread(route_s[:, 6 + k, :], 2, NE), ALU.is_lt))
                    link(dve.tensor_scalar(t1, t1, 1e6, None, ALU.mult))
                    link(dve.tensor_tensor(t1, t1, spread(iota_exp[:, :], 1, TT), ALU.add))
                    link(dve.tensor_reduce(route_s[:, 3, :], t1, AX.X, ALU.min))
                    link(dve.tensor_tensor(chosen[:, k], spread(iota_exp[:, :], 1, TT),
                                           spread(route_s[:, 3, :], 2, NE), ALU.is_equal))
                    if k == 0:
                        link(dve.tensor_scalar(t2, chosen[:, 0], 3.0 * NEG, None, ALU.mult))
                        link(dve.tensor_tensor(t0, t0, t2, ALU.add))
                dve.tensor_tensor(route_s[:, 4, :], route_s[:, 7, :], route_s[:, 6, :], ALU.subtract)\
                    .then_inc(s["route_diff"], 1)
                dve.tensor_tensor(member[:, :, :], chosen[:, 0], chosen[:, 1], ALU.add)\
                    .then_inc(s["member_done"], 1)
                dve.wait_ge(s["route_exp"], 3 * (l + 1))
                link(dve.tensor_scalar(route_s[:, 10, :], route_s[:, 5, :], 1.0, None, ALU.add))
                link(dve.tensor_tensor(route_s[:, 11, :], route_s[:, 10, :], route_s[:, 1, :], ALU.mult))
                link(dve.reciprocal(weight[:, 0, :], route_s[:, 11, :]))
                link(dve.tensor_tensor(weight[:, 1, :], weight[:, 0, :], route_s[:, 5, :], ALU.mult))
                dve.wait_ge(s["slot_psum"], l + 1)
                dve.wait_ge(s["member_done"], l + 1)
                link(dve.tensor_scalar(t2, bank(6)[:, 0:TT * NE].rearrange("p (t e) -> p t e", t=TT), 1.0, None,
                                       ALU.add))
                link(dve.tensor_tensor(slot_of[:, :, :], t2, member[:, :, :], ALU.mult))
                link(dve.tensor_scalar(slot_of[:, :, :], slot_of[:, :, :], -1.0, None, ALU.add))
                link(dve.tensor_reduce(route_s[:, 8, 0:1], bank(6)[:, 64:64 + NE], AX.X, ALU.max))

            def shares_and_rounds(l):
                link(dve.tensor_tensor(route_t[:, 1], chosen[:, 0], spread(weight[:, 0, :], 2, NE), ALU.mult))
                link(dve.tensor_tensor(share[:, :, :], chosen[:, 1], spread(weight[:, 1, :], 2, NE), ALU.mult))
                link(dve.tensor_tensor(share[:, :, :], share[:, :, :], route_t[:, 1], ALU.add))
                for i in range(PASS_MAX - 1):
                    link(dve.tensor_scalar(passes_f[:, i:i + 1], route_s[:, 8, 0:1], float(CAP * (i + 1)), None,
                                           ALU.is_gt))
                link(dve.tensor_reduce(route_s[:, 9, 0:1], passes_f[:, 0:PASS_MAX - 1], AX.X, ALU.add))
                link(dve.tensor_copy(passes[l][:, :], route_s[0:1, 9, 0:1]))
                dve.sem_inc(s["route_used"], 1)
                dve.sem_inc(s["passes_ready"], 1)

            def expert_columns(table, q):
                return table[:, :, bass.ds(QE * q, QE)].unsqueeze(3).broadcast_to([P, TT, QE, CAP])

            def add_rows(l, m, done, first=False):
                if not first:
                    dve.wait_ge(s[f"added{l}"], 4 * m)
                for i, b in enumerate(COMBINE_BANKS):
                    t, half = divmod(i, 2)
                    v = h[:, t, half * 512:(half + 1) * 512]
                    dve.wait_ge(s[f"combined{l}"], 4 * m + i + 1)
                    dve.tensor_tensor(v, bank(b), v, ALU.add).then_inc(done, 1)

            def quad(l, n, q):
                first = isinstance(n, int) and n == 0
                dve.tensor_tensor(slots, iota_slot[:, :].unsqueeze(1).unsqueeze(1).broadcast_to([P, TT, QE, CAP]),
                                  expert_columns(slot_of, q), ALU.is_equal).then_inc(s[f"slots{l}"], 1)
                if first:
                    shares_and_rounds(l)
                dve.wait_ge(s[f"gathered{l}"], 2 * n + 2)
                dve.tensor_copy(gatheredT[:, 4:8, :], bank(1).rearrange("p (k c) -> p k c", k=4))\
                    .then_inc(s[f"gatheredT{l}"], 1)
                dve.wait_ge(s[f"slots{l}"], n + 1)
                dve.tensor_tensor(slots_share, slots, expert_columns(share, q), ALU.mult)\
                    .then_inc(s[f"slots_share{l}"], 1)
                dve.wait_ge(s[f"egate{l}"], n + 1)
                dve.tensor_tensor(hid_t, bank(3)[:, 0:FF], egate, ALU.mult).then_inc(s[f"silu{l}"], 1)
                dve.wait_ge(s[f"silu{l}"], n + 1)
                dve.tensor_tensor(hid, bank(3)[:, FF:2 * FF], hid_t, ALU.mult).then_inc(s[f"hid{l}"], 1)
                if not first:
                    add_rows(l, n - 1, s[f"added{l}"], isinstance(n, int) and n == 1)
                dve.wait_ge(s[f"down{l}"], n + 1)
                dve.tensor_copy(y_rows[:, 512:D], bank(6)).then_inc(s[f"y_rows{l}"], 1)

            def experts(l):
                route(l)
                for q in range(2):
                    quad(l, q, q)
                with dve.Fori(2, NQ) as q:
                    quad(l, q, q)
                dve.wait_ge(s["passes_ready"], l + 1)
                more = dve.value_load(passes[l][0:1, 0:1], min_val=0, max_val=PASS_MAX - 1)
                with dve.If(more > 0):
                    with dve.Fori(0, more) as r:
                        dve.tensor_scalar(slot_of[:, :, :], slot_of[:, :, :], -float(CAP), None, ALU.add)\
                            .then_inc(s[f"next_round{l}"], 1)
                        with dve.Fori(0, NQ) as q:
                            dve.wait_ge(s[f"next_round{l}"], r + 1)
                            quad(l, q + NQ * (r + 1), q)
                add_rows(l, NQ * more + NQ - 1, s["h_done"])
                for t in range(TT):
                    norm(2 * l + 2, t)
                    if l == 0:
                        xT_half(2, t)

            add_mix(0, (0, 1, 4, 5))
            experts(0)

            dve.wait_ge(s["lb_psum"], 1)
            link(dve.tensor_copy(lb, bank(4)[:, 0:2 * RH]))
            link(dve.tensor_tensor(lbt[:, 2, :], lb[:, 0:RH], lb[:, RH:], ALU.max))
            link(dve.tensor_tensor(lbt[:, 0, :], lb[:, 0:RH], lbt[:, 2, :], ALU.subtract))
            dve.tensor_tensor(lbt[:, 1, :], lb[:, RH:], lbt[:, 2, :], ALU.subtract).then_inc(s["lb_diff"], 1)
            dve.wait_ge(s["lb_exp"], 1)
            link(dve.tensor_tensor(lbt[:, 2, :], lbt[:, 0, :], lbt[:, 1, :], ALU.add))
            link(dve.reciprocal(lbt[:, 3, :], lbt[:, 2, :]))
            link(dve.tensor_tensor(lbt[:, 0, :], lbt[:, 0, :], lbt[:, 3, :], ALU.mult))
            def key(m):
                v = rA[:, 2 * m:2 * m + 2, :]
                dve.wait_ge(s["rec_f"], m + 1)
                link(dve.tensor_scalar(v, v, 1.0, None, ALU.add))
                link(dve.reciprocal(v, v))
                dve.tensor_tensor(v, v, spread(lbt[:, 0, 2 * m:2 * m + 2], 2, T), ALU.mult)\
                    .then_inc(s["rec_key"], 1)

            def cumulate(hh):
                sl = slice(4 * hh, 4 * hh + 4)
                flat_cum = rB[:, sl, :].rearrange("p h t -> p (h t)")
                dve.wait_ge(s["rec_logf"], hh + 1)
                dve.tensor_tensor_scan(flat_cum, reset, rC[:, sl, :].rearrange("p h t -> p (h t)"), 0.0,
                                       ALU.mult, ALU.add).then_inc(s["rec_cum"], 1)
                dve.wait_ge(s["rec_cum"], hh + 1)
                cum = flat_cum.rearrange("p (g i) -> p g i", i=CH)
                dve.tensor_tensor(rC[:, sl, :].rearrange("p h (c i) -> p (h c) i", i=CH), cum,
                                  cum[:, :, CH // 2:CH // 2 + 1].broadcast_to([P, 4 * NCH, CH]), ALU.subtract)\
                    .then_inc(s["rec_rel"], 1)

            def queries(hh):
                sl = slice(4 * hh, 4 * hh + 4)
                dve.wait_ge(s["rec_q"], 4)
                dve.wait_ge(s["rec_exps"], 4 * hh + 4)
                link(dve.tensor_copy(decay[:, sl, :], r3[:, sl, :].rearrange("p h (c i) -> p h c i", i=CH)[:, :, :, CH - 1]))
                dve.tensor_tensor(r1[:, sl, :], r1[:, sl, :], rQ[:, sl, :], ALU.mult).then_inc(s["rec_qin"], 1)
                dve.tensor_tensor(r3[:, sl, :], r3[:, sl, :], rQ[:, sl, :], ALU.mult).then_inc(s["rec_qin"], 1)

            def gate_silu(i):
                v = e_gate[:, :, i * 256:(i + 1) * 256]
                dve.wait_ge(s["rec_gate_exp"], i + 1)
                dve.tensor_tensor(v, v, bank(4 + i).rearrange("p (t n) -> p t n", t=TT), ALU.mult)\
                    .then_inc(s["rec_gate"], 1)
                dve.wait_ge(s["rec_gate"], i + 1)
                for t in range(TT):
                    v3 = v[:, t, :].rearrange("p (h d) -> p h d", d=RV)
                    ins = dve.tensor_tensor(v3, v3, spread(gnorm, 1, 256 // RV), ALU.mult)
                    ins.then_inc(s["gate_normed"], 1)

            split_low(dve, 0)
            split_low(dve, 2)
            dve.wait_ge(s["rec_const"], 1)
            for m in range(16):
                if 2 * m + 4 < REC_QUARTERS:
                    split_low(dve, 2 * m + 4)
                if m < 4:
                    key(m)
                elif m < 8:
                    dve.wait_ge(s["rec_psum"], 2 * m + 2)
                    dve.tensor_scalar(rQ[:, 2 * (m - 4):2 * (m - 4) + 2, :],
                                      bank(m).rearrange("p (a t) -> p a t", a=2),
                                      RK ** -0.5, None, ALU.mult).then_inc(s["rec_q"], 1)
                if m in (4, 6):
                    cumulate(m // 2 - 2)
                if m in (8, 10):
                    queries((m - 8) // 2)
                if m >= 12:
                    gate_silu(m - 12)
            for b in (1, 3):
                dve.wait_ge(s["ko_psum"], b + 1)
                dve.tensor_copy(koR[:, b // 2, (b % 2) * 512:(b % 2) * 512 + 512], bank(b))\
                    .then_inc(s["ko_done"], 1)
            for c in range(NCH - 1):
                dve.wait_ge(s["state_psum"], c + 1)
                kv = psum[:, 2 * (c % 2):2 * (c % 2) + 2, :].rearrange("p b n -> p (b n)")
                if c == 0:
                    dve.tensor_copy(states[0], kv).then_inc(s["state_done"], RH)
                else:
                    for hd in range(RH):
                        d = slice(hd * RV, (hd + 1) * RV)
                        dve.scalar_tensor_tensor(out=states[c][:, d], in0=states[c - 1][:, d],
                                                 scalar=decay[:, hd, c:c + 1], in1=kv[:, d],
                                                 op0=ALU.mult, op1=ALU.add).then_inc(s["state_done"], 1)
                dve.wait_ge(s["state_done"], RH * (c + 1))
            dve.wait_ge(s["a_used"], 1)
            dve.wait_ge(s["gate_normed"], 4 * TT)
            for t in range(TT):
                dve.wait_ge(s["o_square"], t + 1)
                dve.tensor_reduce(ostat[:, 0, t * RH:(t + 1) * RH], square_rec.rearrange("p (h d) -> p h d", h=RH),
                                  AX.X, ALU.add).then_inc(s["o_sum"], 1)
                dve.wait_ge(s["o_rstd"], t + 1)
                o_ps = psum[:, 4 + 2 * t:6 + 2 * t, :].rearrange("p b n -> p (b n)").rearrange("p (h d) -> p h d", h=RH)
                o3 = o_rows[:, t, :].rearrange("p (h d) -> p h d", h=RH)
                link(dve.tensor_tensor(o3, o_ps, spread(ostat[:, 1, t * RH:(t + 1) * RH], 2, RV), ALU.mult))
                dve.tensor_tensor(o_rows[:, t, :], o_rows[:, t, :], e_gate[:, t, :], ALU.mult)\
                    .then_inc(s["o_done"], 1)
            for b in (1, 3):
                dve.wait_ge(s["recT_psum"], b + 1)
                dve.tensor_copy(recT[:, 4 * (b % 2):4 * (b % 2) + 4, (b // 2) * P:(b // 2 + 1) * P],
                                bank(b).rearrange("p (k t) -> p k t", k=4)).then_inc(s["recT_done"], 1)
            add_mix(1, (4, 5, 6, 7))
            experts(1)

        @block.tensor
        def _(pe):
            def unit(u, n=0):
                pe.wait_ge(*arrival(u, n))
                return ring[:, RING_SLOT[u], :]

            def transposes(v, t):
                for half in range(2):
                    pe.wait_ge(s["xg_done"], TT * v + t + 1)
                    for k in range(4):
                        last = pe.transpose(bank(2 * t + half)[:, k * P:(k + 1) * P], xg[:, t, 4 * half + k::KD],
                                            ident[:, :])
                    last.then_inc(s["xT_psum"], 1)

            pe.wait_ge(s["ident_done"], 1)
            for t in range(TT):
                transposes(0, t)
            pe.wait_ge(s["cmp_small"], 64)
            for i in range(2):
                last = pe.transpose(bank(5)[:, i * LP:(i + 1) * LP], pe_rows[0:LP, i, :], ident[0:LP, 0:LP])
            last.then_inc(s["pe_psum"], 1)
            pe.wait_ge(s["xT_done"], 4)

            def w_cols(r, n):
                return r[:, 0:KD * n].rearrange("p (k n) -> p k n", k=KD)

            def tile_T(dst, lhs):
                for k in range(KD):
                    last = pe.matmul(dst, lhs(k), xT[:, k, :], start=(k == 0), stop=(k == KD - 1))
                return last

            def tile_rows(dst, t, rhs):
                for k in range(KD):
                    last = pe.matmul(dst, xT[:, k, t * P:(t + 1) * P], rhs(k), start=(k == 0), stop=(k == KD - 1))
                return last

            def proj(n):
                if n >= 2:
                    pe.wait_ge(s["proj_odd" if n % 2 else "proj_even"], (n - 2) // 2 + 1)
                b = bank(n % 2)
                if n in (0, 1):
                    w = w_cols(unit(U_Q), 512)
                    for i in range(2):
                        for k in range(KD):
                            for g in range(NSA_G):
                                c = (g * HPG + 2 * n + i) * DH
                                last = pe.matmul(b[g * DH:(g + 1) * DH, i * T:(i + 1) * T], w[:, k, c:c + DH],
                                                 xT[:, k, :], start=(k == 0), stop=(k == KD - 1))
                    if n == 1:
                        last.then_inc(s["q_unit_done"], 1)
                elif n == 2:
                    w = w_cols(unit(U_KV), 512)
                    for i in range(2):
                        last = tile_T(b[:, i * T:(i + 1) * T], lambda k: w[:, k, i * P:(i + 1) * P])
                elif n == 3:
                    w, w_w = w_cols(unit(U_KV), 512), w_cols(unit(U_WG), 280)
                    tile_T(b[:, 0:T], lambda k: w[:, k, 2 * P:3 * P])
                    last = tile_T(b[:, T:2 * T], lambda k: w_w[:, k, 0:P])
                elif n in (4, 5):
                    w, w_w = w_cols(unit(U_KV), 512), w_cols(unit(U_WG), 280)
                    tile_rows(b[:, 0:P], n - 4, lambda k: w[:, k, 3 * P:4 * P])
                    last = tile_rows(b[:, P:280], n - 4, lambda k: w_w[:, k, P:280])
                elif n in (6, 7, 8, 9):
                    w = w_cols(unit(U_QB if n < 8 else U_KB), 512)
                    for i in range(2):
                        j = 2 * (n % 2) + i
                        last = tile_T(b[:, i * T:(i + 1) * T], lambda k: w[:, k, j * P:(j + 1) * P])
                else:
                    w = w_cols(unit(U_VB), 512)
                    last = tile_rows(b, n - 10, lambda k: w[:, k, :])
                if n != 1:
                    last.then_inc(s["proj_psum"], 1)

            def free_units(k):
                pe.drain().then_inc(s["unit_used"], k)

            proj(0)
            proj(1)
            pe.wait_ge(s["q_unit_done"], 1)
            pe.nop().then_inc(s["proj_psum"], 1)
            free_units(1)
            proj(2)
            proj(3)
            w1 = unit(U_CMP).rearrange("p (w j n) -> p w j n", w=2, n=P)
            pe.wait_ge(s["cmp_w1_rest"], 32)
            pe.wait_ge(s["kv2_done"], 7)
            pe.wait_ge(s["proj_even"], 2)
            pe.wait_ge(s["pe_done"], 1)
            for kv in range(2):
                for j in range(LP):
                    last = pe.matmul(bank(4)[:, 64 * kv:64 * kv + (NSA_G + 1) * NC]
                                     .rearrange("p (g c) -> p g c", g=NSA_G + 1),
                                     w1[:, kv, j, :],
                                     kv2[:, kv, :, 2 * j:2 * j + CMP_STRIDE * (NC - 1) + 1:CMP_STRIDE],
                                     start=(j == 0), stop=(j == LP - 1))
            last.then_inc(s["cmp_hidden"], 1)
            proj(4)
            pe.wait_ge(s["cmp_h_done"], 3)
            pe.matmul(bank(5)[0:DH, 0:2 * NC], w2[:, 0, :], cmp_h[:, 0, :], start=True, stop=True)
            for g in range(NSA_G):
                last = pe.matmul(bank(5)[:, 64 + g * DH:64 + (g + 1) * DH],
                                 hv4[:, g, :, :].rearrange("p a c -> p (a c)"), w2[:, 1, :], start=True, stop=True)
            last.then_inc(s["cmp_kv"], 1)
            proj(5)
            free_units(3)
            pe.wait_ge(s["cmp_kv_done"], 3)
            pe.wait_ge(s["proj_odd"], 1)

            def q_of(hd, t):
                g, i = divmod(hd, HPG)
                return qT[g * DH:(g + 1) * DH, i, t * P:(t + 1) * P]

            for t in range(TT):
                for hd in range(NSA_H):
                    g = hd // HPG
                    c = (t * HPG + hd % HPG) * NC
                    last = pe.matmul(bank(4 + g)[:, c:c + NC], q_of(hd, t), kcT[g * DH:(g + 1) * DH, :],
                                     start=True, stop=True)
            last.then_inc(s["cmp_scores"], 1)

            def nsa_scores(u):
                t, br, g, nk = u // 4, u // 2 % 2, u % 2, P * (u // 4 + 1)
                if u == 0:
                    pe.wait_ge(s["cmp_shifted"], 1)
                    pe.wait_ge(s["proj_odd"], 2)
                else:
                    pe.wait_ge(s["nsa_masked"], u)
                dst = psum[:, 4:6, :].rearrange("p b n -> p (b n)")
                for i in range(HPG):
                    last = pe.matmul(dst[:, i * nk:(i + 1) * nk], q_of(g * HPG + i, t),
                                     ksw[g * DH:(g + 1) * DH, br, 0:nk], start=True, stop=True)
                last.then_inc(s["nsa_scores"], 1)

            def nsa_T(u):
                pe.wait_ge(s["nsa_scaled"], u + 1)
                if u >= 1:
                    pe.wait_ge(s["nsa_pT_even"], u)
                if u >= 5:
                    pe.wait_ge(s["nsa_pT_odd"], u - 4)
                for kb in range(u // 4 + 1):
                    for i in range(HPG):
                        last = pe.transpose(bank(2 + kb)[:, i * P:(i + 1) * P],
                                            scores[:, u % 2, i, kb * P:(kb + 1) * P], ident[:, :])
                last.then_inc(s["nsa_pT"], 1)

            def nsa_pv(u):
                t, br, g = u // 4, u // 2 % 2, u % 2
                pe.wait_ge(s["nsa_pT_even"], u + 1)
                if u >= 4:
                    pe.wait_ge(s["nsa_pT_odd"], u - 3)
                acc = bank(6 + g).rearrange("p (a t) -> p a t", a=2)
                for kb in range(t + 1):
                    for par in range(2):
                        heads = probsT[:, u % 2, kb, :].rearrange("p (a two q) -> p a two q", two=2, q=P)
                        last = pe.matmul(acc[par * DH:(par + 1) * DH, :, t * P:(t + 1) * P],
                                         vsw[:, kb, br * P + g * DH:br * P + (g + 1) * DH], heads[:, :, par, :],
                                         start=False, stop=True, skip_group_check=True)
                last.then_inc(s["nsa_pv"], 1)

            nsa_scores(0)
            for u in range(8):
                if u + 1 < 8:
                    nsa_scores(u + 1)
                if u == 1:
                    pe.wait_ge(s["cmp_pT_done"], 1)
                    for i in range(HPG):
                        for g in range(NSA_G):
                            last = pe.matmul(bank(6 + g)[i % 2 * DH:(i % 2 + 1) * DH, i // 2 * T:(i // 2 + 1) * T],
                                             vc4[i * 32:(i + 1) * 32, g, :], pcT[i * 32:(i + 1) * 32, g, :],
                                             start=(i < 2), stop=True, skip_group_check=True)
                        if i % 2:
                            last.then_inc(s["cmp_pv"], 1)
                            pe.wait_ge(s["cmp_pv"], i // 2 + 1)
                if u >= 1:
                    nsa_pv(u - 1)
                if 6 + u < 12:
                    proj(6 + u)
                    if 6 + u in (7, 9, 11):
                        free_units(1)
                if u == 0:
                    pe.wait_ge(s["cmp_p_done"], 2)
                    for g in range(NSA_G):
                        for t in range(TT):
                            last = pe.transpose(bank(5)[:, g * T + t * P:g * T + (t + 1) * P],
                                                cp[:, t, g * HPG:(g + 1) * HPG, :].rearrange("p h c -> p (h c)"),
                                                ident[:, :])
                    last.then_inc(s["cmp_pT"], 1)
                nsa_T(u)
            nsa_pv(7)

            def sb_z(hd):
                p0, j = hd % 2 * DH, hd // 2
                if hd == 0:
                    pe.wait_ge(s["nsa_masked"], 8)
                    pe.wait_ge(s["proj_odd"], 6)
                    pe.wait_ge(s["proj_even"], 6)
                if hd >= 4:
                    pe.wait_ge(s["sb_a"], hd - 3)
                z = bank(SB_BANKS[hd % 4])
                pe.matmul(z[:, 0:T], kbT[p0:p0 + DH, j, 0:P], qbT[p0:p0 + DH, j, :], start=True, stop=True,
                          skip_group_check=True)
                pe.matmul(z[:, T:T + P], kbT[p0:p0 + DH, j, P:T], qbT[p0:p0 + DH, j, P:T], start=False, stop=True,
                          skip_group_check=True).then_inc(s["sb_z_raw"], 1)
                pe.wait_ge(s["sb_z_raw"], hd + 1)
                pe.matmul(z[:, 0:P], ident[:, :], before_query, start=False, stop=True, skip_group_check=True)
                pe.matmul(z[:, T:T + P], ident[:, :], before_query, start=False, stop=True, skip_group_check=True)\
                    .then_inc(s["sb_z"], 1)

            def sb_e(hd):
                pe.wait_ge(s["sb_t"], hd + 1)
                z, t = bank(SB_BANKS[hd % 4]), zt[:, hd % 3, :]
                pe.matmul(z[:, 0:T], later_own, t[:, 0:T], start=False, stop=True, skip_group_check=True)
                pe.matmul(z[:, P:T], later_all, t[:, T:T + P], start=False, stop=True, skip_group_check=True)
                pe.matmul(z[:, T:T + P], later_own, t[:, T:T + P], start=False, stop=True, skip_group_check=True)\
                    .then_inc(s["sb_e"], 1)

            def sb_pv(hd):
                pe.wait_ge(s["sb_a"], hd + 1)
                if hd == 0:
                    pe.wait_ge(s["nsa_pT_even"], 8)
                    pe.wait_ge(s["nsa_pT_odd"], 4)
                p0, j = hd % 2 * DH, hd // 2
                acc = bank(2 + j // 2)[p0:p0 + DH, j % 2 * T:(j % 2 + 1) * T]
                w, p = vb[:, :, hd * DH:(hd + 1) * DH], za[:, hd % 2, :]
                pe.matmul(acc, w[:, 0, :], p[:, 0:T], start=(hd % 4 < 2), stop=True, skip_group_check=True)
                pe.matmul(acc[:, P:T], w[:, 1, :], p[:, T:T + P], start=False, stop=True, skip_group_check=True)\
                    .then_inc(s["sb_pv"], 1)

            sb_z(0)
            sb_z(1)
            for hd in range(SB_H):
                if hd + 2 < SB_H:
                    sb_z(hd + 2)
                sb_e(hd)
                if hd >= 1:
                    sb_pv(hd - 1)
            sb_pv(SB_H - 1)

            def mix(l, lhs, units, banks, n=0):
                for i, b in enumerate(banks):
                    t, c = divmod(i, 2)
                    w = unit(units + c, n).rearrange("p (j n) -> p j n", n=512)
                    for j in range(8):
                        last = pe.matmul(bank(b), lhs[:, j, t * P:(t + 1) * P], w[:, j, :],
                                         start=(j == 0), stop=(j == 7))
                    last.then_inc(s["mix_psum"], 1)
                    if i == 2:
                        transposes(2 * l + 1, 0)
                free_units(2)
                transposes(2 * l + 1, 1)

            pe.wait_ge(s["oT_done"], 4)
            pe.wait_ge(s["sb_a"], SB_H)
            mix(0, oT, U_WO, (0, 1, 4, 5))

            def route(l):
                pe.wait_ge(s["xT_done"], 4 * (2 * l + 1) + 4)
                pe.wait_ge(s["route_loaded"], 64 * (l + 1))
                for t in range(TT):
                    last = tile_rows(bank(4 + t)[:, 0:GR + NE], t, lambda k: w_route[:, k, :])
                last.then_inc(s["route_psum"], 1)
                pe.wait_ge(s["member_done"], l + 1)
                pe.matmul(bank(6)[:, 0:NE], earlier[:, :], member[:, 0, :], start=True, stop=True)
                pe.matmul(bank(6)[:, NE:2 * NE], ones[:, :], member[:, 0, :], start=True, stop=False)
                pe.matmul(bank(6)[:, NE:2 * NE], earlier[:, :], member[:, 1, :], start=False, stop=True)
                pe.matmul(bank(6)[:, 2 * NE:3 * NE], ones[:, :], member[:, 0, :], start=True, stop=False)
                pe.matmul(bank(6)[:, 2 * NE:3 * NE], ones[:, :], member[:, 1, :], start=False, stop=True)\
                    .then_inc(s["slot_psum"], 1)

            def combine(l, m):
                pe.wait_ge(s[f"shareT{l}"], m + 1)
                pe.wait_ge(s[f"y_rows{l}"], 2 * m + 2)
                for i, b in enumerate(COMBINE_BANKS):
                    t, half = divmod(i, 2)
                    pe.matmul(bank(b), shareT[:, t, :], y_rows[:, half * 512:(half + 1) * 512],
                              start=True, stop=True).then_inc(s[f"combined{l}"], 1)

            def quad(l, n, before):
                static = isinstance(n, int)
                pe.wait_ge(s[f"slots{l}"], n + 1)
                if not static:
                    pe.wait_ge(s[f"added{l}"], 4 * n - 4)
                for k in range(KD):
                    for t in range(TT):
                        last = pe.matmul(bank(k // 4)[:, k % 4 * P:(k % 4 + 1) * P], xg[:, t, k::KD],
                                         slots[:, t].rearrange("p e c -> p (e c)"), start=(t == 0), stop=(t == TT - 1))
                    if k % 4 == 3:
                        last.then_inc(s[f"gathered{l}"], 1)

                def weights(i):
                    if static and n == 1 and i < SPARE:
                        pe.wait_ge(s[f"spare{i}_loaded"], 32 * (l + 1))
                        return spare[:, i, :], False
                    if static:
                        return unit(BASE_MOE[l] + i + (NU - SPARE) * n, before), True
                    return unit(BASE_LOOP[l] + i, n - 2 + before), True

                pe.wait_ge(s[f"gatheredT{l}"], 2 * n + 2)
                for c in range(KD // 2):
                    w, in_ring = weights(c)
                    w = w.rearrange("p (w e r f) -> p w e r f", w=2, e=QE, r=2)
                    for r in range(2):
                        k = 2 * c + r
                        for e in range(QE):
                            last = pe.matmul(bank(3)[e * CAP:(e + 1) * CAP, :].rearrange("p (w f) -> p w f", w=2),
                                             gatheredT[:, k, e * CAP:(e + 1) * CAP], w[:, :, e, r, :],
                                             start=(k == 0), stop=(k == KD - 1))
                    if c < KD // 2 - 1 and in_ring:
                        last.then_inc(s["unit_used"], 1)
                last.then_inc(s[f"gate_up{l}"], 1)
                if in_ring:
                    pe.wait_ge(s[f"gate_up{l}"], n + 1)
                    pe.sem_inc(s["unit_used"], 1)
                if not (static and n == 0):
                    combine(l, n - 1)
                pe.wait_ge(s[f"slots_share{l}"], n + 1)
                for t in range(TT):
                    pe.transpose(bank(4)[:, FF + t * P:FF + (t + 1) * P],
                                 slots_share[:, t].rearrange("p e c -> p (e c)"), ident[:, :])
                pe.wait_ge(s[f"hid{l}"], n + 1)
                for j in range(KF):
                    last = pe.transpose(bank(4)[:, j * P:(j + 1) * P], hid[:, j::KF], ident[:, :])
                last.then_inc(s[f"hid_psum{l}"], 1)
                pe.wait_ge(s[f"hidT{l}"], n + 1)
                for j in range(KF):
                    w, in_ring = weights(KD // 2 + j)
                    w = w.rearrange("p (e n) -> p e n", e=QE)
                    for c in range(2):
                        for e in range(QE):
                            last = pe.matmul(bank(5 + c)[e * CAP:(e + 1) * CAP, :],
                                             hidT[:, j, e * CAP:(e + 1) * CAP], w[:, e, c * 512:(c + 1) * 512],
                                             start=(j == 0), stop=(j == KF - 1))
                    if j == 0:
                        last.then_inc(s["unit_used"], 1)
                last.then_inc(s[f"down{l}"], 1)
                pe.wait_ge(s[f"down{l}"], n + 1)
                pe.sem_inc(s["unit_used"], 1)

            def experts(l, before):
                route(l)
                for q in range(2):
                    quad(l, q, before)
                with pe.Fori(2, NQ) as q:
                    quad(l, q, before)
                pe.wait_ge(s["passes_ready"], l + 1)
                more = pe.value_load(passes[l][0:1, 0:1], min_val=0, max_val=PASS_MAX - 1)
                with pe.If(more > 0):
                    with pe.Fori(0, more) as r:
                        with pe.Fori(0, NQ) as q:
                            quad(l, q + NQ * (r + 1), before)
                combine(l, NQ * more + NQ - 1)
                return NQ * more

            before = experts(0, 0)

            for t in range(TT):
                transposes(2, t)
            pe.wait_ge(s["rec_small"], 32)
            pe.transpose(bank(4)[:, 0:2 * RH], lb_rows[0:2 * RH, :], ident[0:2 * RH, 0:2 * RH])\
                .then_inc(s["lb_psum"], 1)
            pe.wait_ge(s["xT_done"], 12)

            def three(dst, lhs_hi, lhs_lo, rhs_hi, rhs_lo):
                for k in range(KD):
                    pe.matmul(dst, lhs_hi(k), rhs_hi(k), start=(k == 0), stop=False)
                    pe.matmul(dst, lhs_hi(k), rhs_lo(k), start=False, stop=False)
                    last = pe.matmul(dst, lhs_lo(k), rhs_hi(k), start=False, stop=(k == KD - 1))
                return last

            pe.wait_ge(s["x_lo_done"], TT)
            for m in range(8):
                if m == 4:
                    pe.wait_ge(s["lb_diff"], 1)
                for i in range(2):
                    r = 2 * m + i
                    pe.wait_ge(s["w_lo_odd" if i else "w_lo_even"], m + 1)
                    three(bank(m)[:, i * T:(i + 1) * T],
                          lambda k: quarter_hi(r)[:, k, :], lambda k: quarter_lo(r)[:, k, :],
                          lambda k: x_hi[:, k, :], lambda k: x_lo[:, :, k, :])\
                        .then_inc(s["rec_psum"], 1)
                if m % 2:
                    free_units(1)
            for m in range(8, 16):
                if m == 8:
                    pe.wait_ge(s["rec_f"], 4)
                if m == 12:
                    pe.wait_ge(s["rec_q"], 4)
                pe.wait_ge(s["w_lo_even"], m + 1)
                pe.wait_ge(s["w_lo_odd"], m + 1)
                high = w_hi[:, m % 2]
                low = w_lo[:, RING_SLOT[BASE_REC + m // 2], :, m % 2 * 256:(m % 2 + 1) * 256]
                for t in range(TT):
                    three(bank(m % 8)[:, t * 256:(t + 1) * 256],
                          lambda k: x_hi[:, k, t * P:(t + 1) * P], lambda k: x_lo[:, t, k, :],
                          lambda k: high[:, k, :], lambda k: low[:, k, :]).then_inc(s["rec_psum"], 1)
                if m % 2:
                    free_units(1)

            pe.wait_ge(s["rec_kout"], 2)
            pe.wait_ge(s["rec_v"], 4)
            for b in range(4):
                t, half = b // 2, b % 2
                for i in range(4):
                    last = pe.transpose(bank(b)[:, i * P:(i + 1) * P], rD[:, 4 * half + i, t * P:(t + 1) * P],
                                        ident[:, :])
                last.then_inc(s["ko_psum"], 1)
            pe.wait_ge(s["rec_kin"], 2)
            pe.nop().then_inc(s["rec_kout_read"], 1)
            pe.wait_ge(s["rec_qin"], 4)
            for b in range(4):
                t, half = b // 2, b % 2
                pe.wait_ge(s["rec_gate"], b + 1)
                for i in range(4):
                    hd = 4 * half + i
                    last = pe.matmul(bank(4 + b)[:, i * P:(i + 1) * P], r2[:, hd, t * P:(t + 1) * P],
                                     r1[:, hd, t * P:(t + 1) * P], start=True, stop=True)
                last.then_inc(s["a_psum"], 1)

            def state(c):
                if c == 2:
                    pe.wait_ge(s["state_done"], RH)
                p0, t = c % 2 * CH, c // 2
                kv = psum[:, 2 * (c % 2):2 * (c % 2) + 2, :].rearrange("p b n -> p (b n)")
                for hd in range(RH):
                    d = slice(hd * P, (hd + 1) * P)
                    last = pe.matmul(kv[:, d], koR[p0:p0 + CH, t, d], rv[p0:p0 + CH, t, d], start=True, stop=True)
                last.then_inc(s["state_psum"], 1)

            pe.wait_ge(s["a_psum"], 4)
            pe.nop().then_inc(s["rec_kin_used"], 1)
            pe.wait_ge(s["ko_done"], 4)
            for c in range(NCH - 1):
                state(c)
            aMv = aM.rearrange("p h t -> p (h t)").rearrange("p (g t) -> p g t", t=P)
            for t in range(TT):
                pe.wait_ge(s["rec_a_masked"], 4)
                acc = psum[:, 4 + 2 * t:6 + 2 * t, :].rearrange("p b n -> p (b n)")
                for hd in range(RH):
                    d = slice(hd * P, (hd + 1) * P)
                    pe.matmul(acc[:, d], aMv[:, t * RH + hd, :], rv[:, t, d], start=(hd % 4 == 0), stop=False,
                              skip_group_check=True)
                for c in (2 * t, 2 * t + 1):
                    if c == 0:
                        continue
                    pe.wait_ge(s["state_done"], RH * c)
                    for hd in range(RH):
                        d = slice(hd * P, (hd + 1) * P)
                        last = pe.matmul(acc[c % 2 * CH:(c % 2 + 1) * CH, d], r3[:, hd, c * CH:(c + 1) * CH],
                                         states[c - 1][:, d], start=False, stop=True, skip_group_check=True)
                last.then_inc(s["o_psum"], 1)
            pe.wait_ge(s["o_psum"], TT)
            pe.nop().then_inc(s["a_used"], 1)
            for b in range(4):
                t, half = b // 2, b % 2
                pe.wait_ge(s["o_done"], t + 1)
                for i in range(4):
                    d = (4 * half + i) * P
                    last = pe.transpose(bank(b)[:, i * P:(i + 1) * P], o_rows[:, t, d:d + P], ident[:, :])
                last.then_inc(s["recT_psum"], 1)
            pe.wait_ge(s["recT_done"], 4)
            mix(1, recT, BASE_REC + 8, (4, 5, 6, 7), before)
            experts(1, before)

        assert max(att_end, rec_end, moe_end) <= arena_t.shape[1], (att_end, rec_end, moe_end)


_INS = ["x", "norm_mix", "norm_ffn", "att_w_in", "att_w_out", "cmp_pe_k", "cmp_w1_k", "cmp_w2_k", "cmp_pe_v",
        "cmp_w1_v", "cmp_w2_v", "rec_w_in", "rec_lb_logits", "rec_gnorm", "rec_w_out", "moe_w_grp", "moe_b_grp",
        "moe_w_exp", "moe_b_exp", "moe_w_gate", "moe_w_up", "moe_w_down", "final_norm"]


def kernel(**inputs):
    import numpy as np
    import concourse.bacc as bacc
    from concourse.bass_utils import run_bass_kernel_spmd

    nc = bacc.Bacc("TRN2", target_bir_lowering=False, num_devices=1)
    arrays, args = {}, []
    for name in _INS:
        a = np.ascontiguousarray(inputs[name])
        arrays[f"in_{name}"] = a
        args.append(nc.dram_tensor(f"in_{name}", a.shape, mybir.dt.from_np(a.dtype), kind="ExternalInput").ap())
    args.append(nc.dram_tensor("out", (1, T, D), F32, kind="ExternalOutput").ap())
    hybrid_trunk(nc, *args)
    return run_bass_kernel_spmd(nc, [arrays], core_ids=[0]).results[0]["out"]
```

```python
from contextlib import ExitStack

import concourse.bass as bass
from concourse import mybir

F32 = mybir.dt.float32
F32R = mybir.dt.float32r
I32 = mybir.dt.int32
ALU = mybir.AluOpType
ACT = mybir.ActivationFunctionType
AX = mybir.AxisListType

P = 128
T = 256
TT = T // P
D = 1024
KD = D // P
NL = 2
EPS = 1e-6
NEG = -1e30

DH = 64
NSA_H, NSA_G = 8, 2
HPG = NSA_H // NSA_G
SB_H = 8
CMP_LEN, CMP_STRIDE = 32, 16
NC = (T - CMP_LEN) // CMP_STRIDE + 1
LP = CMP_LEN // 2
GELU_A, GELU_B = 0.7978845608028654, 0.044715

RH, RK, RV, CH = 8, 128, 128, 64
NCH = T // CH

GR, EPG = 4, 8
NE = GR * EPG
FF = 256
KF = FF // P
QE = 4
CAP = P // QE
NQ = NE // QE
PASS_MAX = T // CAP

NU = 6
UW = 4096
SPARE = 4
UNITS_PER_QUAD = KD // 2 + KF
assert UNITS_PER_QUAD == NU and SPARE == KD // 2

C_KC, C_VC, C_KS, C_VS, C_KW, C_VW, C_GATE, C_QB = 512, 640, 768, 896, 1024, 1152, 1280, 1304
C_KB, C_VB = C_QB + 512, C_QB + 1024
U_Q, U_KV, U_WG, U_CMP, U_QB, U_KB, U_VB, U_WO = range(8)
ATT_UNITS = 9
REC_UNITS = 10
RING_UNITS_MOE = NQ * NU - SPARE
BASE_REC = ATT_UNITS + RING_UNITS_MOE
BASE_MOE = [ATT_UNITS, BASE_REC + REC_UNITS]
BASE_LOOP = [b + 2 * NU - SPARE for b in BASE_MOE]


def ring_plan():
    n_units = BASE_MOE[1] + RING_UNITS_MOE
    slot, needed, loads = [], [], []
    last_use, count = [-1] * NU, [0] * NU
    for u in range(n_units):
        mixer = u < ATT_UNITS or BASE_REC <= u < BASE_MOE[1]
        if u in BASE_MOE:
            last_use[HI_SLOT] = u - 1
        pick = min((i for i in range(NU) if not (mixer and i == HI_SLOT)),
                   key=lambda i: (last_use[i], i == HI_SLOT, i))
        slot.append(pick)
        needed.append(last_use[pick] + 1)
        count[pick] += 1
        loads.append(count[pick])
        last_use[pick] = u
    for b in BASE_LOOP:
        for u in range(b, b + NU * (NQ - 3)):
            assert slot[u + NU] == slot[u] and needed[u + NU] == needed[u] + NU and loads[u + NU] == loads[u] + 1
        assert slot[b - 1] == slot[b + NU - 1]
    return slot, needed, loads


HI_SLOT = NU - 1
RING_SLOT, RING_NEEDED, RING_LOADS = ring_plan()
ATT_QUARTERS, REC_QUARTERS, MIX_QUARTERS = 4 * 3, 4 * 8, 4 * 2
WG = 280
HIGH_BEFORE = {"q": 0, "kv": 4, "wg": 8, "att": 9, "mix0": 21, "rec": 29, "mix1": 61}
LOW_POOL = {"att": 0, "mix0": 12, "rec": 20, "mix1": 36}
LOW_DVE = {"q": 0, "kv": 4, "wg": 8, "rec": 9}
assert HIGH_BEFORE["mix1"] == 9 + ATT_QUARTERS + MIX_QUARTERS + REC_QUARTERS


class Chain:

    def __init__(self, eng, semaphore, base=0):
        self.eng, self.semaphore, self.base, self.n = eng, semaphore, base, 0

    def __call__(self, ins):
        self.n += 1
        ins.then_inc(self.semaphore, 1)
        self.eng.wait_ge(self.semaphore, self.base + self.n)


class Arena:

    def __init__(self, tensor):
        self.tensor, self.at = tensor, 0

    def __call__(self, *shape):
        n = 1
        for s in shape:
            n *= s
        ap = self.tensor[:, self.at:self.at + n]
        self.at += n
        assert self.at <= self.tensor.shape[1], self.at
        if len(shape) == 2:
            return ap.rearrange("p (a b) -> p a b", a=shape[0])
        if len(shape) == 3:
            return ap.rearrange("p (a b c) -> p a b c", a=shape[0], b=shape[1])
        if len(shape) == 4:
            return ap.rearrange("p (a b c d) -> p a b c d", a=shape[0], b=shape[1], c=shape[2])
        return ap


def spread(ap, axis, n):
    a = ap.unsqueeze(axis)
    shape = list(a.shape)
    shape[axis] = n
    return a.broadcast_to(shape)


def hybrid_trunk(nc, x, norm_mix, norm_ffn, att_w_in, att_w_out, cmp_pe_k, cmp_w1_k, cmp_w2_k, cmp_pe_v,
                 cmp_w1_v, cmp_w2_v, rec_w_in, rec_lb_logits, rec_gnorm, rec_w_out, moe_w_grp, moe_b_grp,
                 moe_w_exp, moe_b_exp, moe_w_gate, moe_w_up, moe_w_down, final_norm, out):
    ctx = ExitStack()
    with ctx:
        address = {}

        def sb(name, shape, dt=F32):
            address[name] = (nc.sbuf_base + 31) // 32 * 32
            return ctx.enter_context(nc.sbuf_tensor(name, shape, dt))

        class Signals(dict):
            def __missing__(self, name):
                self[name] = ctx.enter_context(nc.semaphore(name))
                return self[name]

        s = Signals()

        SB_BANKS = (4, 5, 0, 1)

        ring = sb("ring", [P, NU, UW])
        h = sb("h", [P, TT, D])
        xg = sb("xg", [P, TT, D])
        xT = sb("xT", [P, KD, T])
        gain = sb("gain", [P, D])
        ident = sb("ident", [P, P])
        ones = sb("ones", [P, P])
        earlier = sb("earlier", [P, P])
        iota_slot = sb("iota_slot", [P, CAP])
        rank = sb("rank", [P, NE])
        iota_i = sb("iota_i", [P, NE], I32)
        norm_sum = sb("norm_sum", [P, 2 * NL + 1, TT])
        norm_part = sb("norm_part", [P, 2, TT, 4])
        norm_rstd = sb("norm_rstd", [P, 2 * NL + 1, TT])
        eps_col = sb("eps_col", [P, 1])
        w_route = sb("w_route", [P, KD, GR + NE])
        b_route = sb("b_route", [P, GR + NE])
        logit = sb("logit", [P, TT, GR + NE])
        route_t = sb("route_t", [P, 4, TT, NE])
        route_s = sb("route_s", [P, 16, TT])
        chosen = sb("chosen", [P, 2, TT, NE])
        member = sb("member", [P, TT, NE])
        slot_of = sb("slot_of", [P, TT, NE])
        share = sb("share", [P, TT, NE])
        weight = sb("weight", [P, 2, TT])
        passes_f = sb("passes_f", [P, PASS_MAX])
        passes = [sb(f"passes{l}", [1, 1], I32) for l in range(NL)]
        lb_rows = sb("lb_rows", [P, P])[:, :]
        gnorm = sb("gnorm", [P, RV])[:, :]
        arena_t = sb("arena", [P, 19600])

        psum = ctx.enter_context(nc.psum_tensor("psum", [P, 8, 512], F32))

        def bank(b):
            return psum[:, b, :]

        spare = arena_t[:, 0:SPARE * UW].rearrange("p (s w) -> p s w", s=SPARE)
        tail = SPARE * UW
        a = Arena(arena_t)
        qT = a(4, T)
        kv2 = a(2, NSA_G + 1, T)
        ksw = a(2, T)
        vsw = a(TT, 280)
        scores_at = a.at
        scores = a(2, HPG, T)
        probsT = a(2, TT, 512)
        cp = a(TT, NSA_H, 32)
        pcT = a(NSA_G, T)
        w2 = a(2, DH)
        pe_rows = a(2, P)
        causal = a(2, P)
        cmp_bias = a(2)
        cmp_x = a(2, 2 * NC)
        cmp_g = a(2, 2 * NC)
        cmp_h = a(2, 2 * NC)
        hv4 = a(NSA_G, 4, 32)
        vc4 = a(NSA_G, DH)
        assert a.at >= SPARE // 2 * UW
        qbT = a(4, T)
        kbT = a(4, T)
        vb = a(TT, SB_H * DH)
        a.at = ztmp_at = (a.at + 7) // 8 * 8
        ztmp = a(3, 384)
        zt = a(3, 384)
        za = a(2, 384)
        before_query = a(P)
        later_own = a(P)
        att_front = a.at
        a.at = tail
        a.at += 8 * T
        later_all = a(P)
        ident_r_at = a.at
        a.at += P
        before_r_at = a.at
        a.at += P
        kcT = a(NC)
        cmask = a(TT, NC)
        cvis = a(TT, NC)
        cs = a(TT, NSA_H, NC)
        gates = a(TT, 3 * NSA_H)
        cstat = a(4, TT * NSA_H)
        stat = a(2, 4, HPG)
        square = qbT.rearrange("p h t -> p (h t)")
        att_end = a.at
        assert att_front <= tail, (att_front, tail)

        a = Arena(arena_t)
        rA, rD, rQ, r3 = (a(RH, T) for _ in range(4))
        rv = a(TT, D)
        rC, r1, r2 = (a(RH, T) for _ in range(3))
        assert a.at == tail
        rB = a(RH, T)
        reset = gain[:, :]
        last_state = a(RH * RV)
        states = [xT[:, 0:4, :].rearrange("p k t -> p (k t)"), xT[:, 4:8, :].rearrange("p k t -> p (k t)"),
                  last_state]
        decay = a(RH, NCH)
        lb = a(2 * RH)
        lbt = a(4, RH)
        ostat = a(3, TT * RH)
        rec_end = a.at
        koR = rB.rearrange("p h t -> p (h t)").rearrange("p (t d) -> p t d", t=TT)
        aM = rA
        o_rows = r1.rearrange("p h t -> p (h t)").rearrange("p (t d) -> p t d", t=TT)
        e_gate = rC.rearrange("p h t -> p (h t)").rearrange("p (t d) -> p t d", t=TT)
        square_rec = r2.rearrange("p h t -> p (h t)")[:, 0:D]

        def rounded(name, shape, place, at=0):
            return nc.alloc_sbuf_tensor_at(name, shape, F32R, offset=address[place] + at)

        x_hi = rounded("x_hi", [P, KD, T], "xT")
        x_lo = rounded("x_lo", [P, TT, KD, P], "xg")
        w_hi = rounded("w_hi", [P, 2, KD, 256], "ring", 4 * UW * HI_SLOT)
        w_lo = rounded("w_lo", [P, NU, KD, 512], "ring")

        q_lo = rounded("q_lo", [P, 4, KD, P], "arena", 4 * scores_at)
        wg_hi = rounded("wg_hi", [P, KD, WG], "arena", 4 * ztmp_at)
        wg_lo = rounded("wg_lo", [P, KD, WG], "ring", 4 * UW * RING_SLOT[U_WG])
        wg = ring[:, RING_SLOT[U_WG], 0:KD * WG].rearrange("p (k n) -> p k n", k=KD)

        def q_quarter(i):
            return ring[:, RING_SLOT[U_Q], :].rearrange("p (k g n) -> p k g n", k=KD, g=NSA_G)\
                [:, :, :, i * DH:(i + 1) * DH]

        def by_group(ap):
            return ap.rearrange("p k (g d) -> p k g d", g=NSA_G)

        ident_r = rounded("ident_r", [P, P], "arena", 4 * ident_r_at)
        before_r = rounded("before_r", [P, P], "arena", 4 * before_r_at)

        mix_hi = rounded("mix_hi", [P, 8, T], "arena", 4 * tail)
        mix_lo = rounded("mix_lo", [P, 8, T], "xT")

        def quarter_hi(r):
            return w_hi[:, r % 4 // 2, :, r % 2 * P:(r % 2 + 1) * P]

        def quarter_lo(base, r):
            return w_lo[:, RING_SLOT[base + r // 4], :, r % 4 * P:(r % 4 + 1) * P]

        def quarter(base, r):
            return ring[:, RING_SLOT[base + r // 4], :]\
                .rearrange("p (k n) -> p k n", k=KD)[:, :, r % 4 * P:(r % 4 + 1) * P]

        def half_parts(base, m):
            return w_hi[:, m % 2], w_lo[:, RING_SLOT[base + m // 2], :, m % 2 * 256:(m % 2 + 1) * 256]

        def split_low(eng, base, r, stage):
            eng.wait_ge(s["w_high"], HIGH_BEFORE[stage] + r + 1)
            on_dve = stage == "kv" or stage == "rec" and r % 2 == 0
            eng.tensor_tensor(quarter_lo(base, r), quarter(base, r), quarter_hi(r).bitcast(F32), ALU.subtract)\
                .then_inc(s["w_low_dve" if on_dve else "w_low_pool"], 1)

        a = Arena(arena_t)
        a.at = tail
        slots = a(TT, QE, CAP)
        slots_share = a(TT, QE, CAP)
        shareT = a(TT, P)
        egate = a(FF)
        hid_t = a(FF)
        hid = a(FF)
        hidT = a(KF, P)
        a.at = tail + RH * T
        square_moe = a(D)
        moe_end = a.at
        gatheredT = xT[:, 0:4, :].rearrange("p k t -> p (k t)").rearrange("p (k c) -> p k c", k=KD)
        y_rows = xT[:, 4:8, :].rearrange("p k t -> p (k t)")

        block = ctx.enter_context(nc.Block())

        def arrival(u, n=0):
            return s[f"unit{RING_SLOT[u]}_loaded"], 32 * (RING_LOADS[u] + n)

        def load(sp, dst, parts, arrived):
            for i, (part, src) in enumerate(parts):
                sp.dma_start(part(dst), src).then_inc(arrived if i < 2 else s["cmp_w1_rest"], 16)

        def load_ring(sp, u, parts, n=0):
            if RING_NEEDED[u]:
                sp.wait_ge(s["unit_used"], RING_NEEDED[u] + NU * n)
            load(sp, ring[:, RING_SLOT[u], :], parts, arrival(u, n)[0])

        def load_spare(sp, i, parts):
            load(sp, spare[:, i, :], parts, s[f"spare{i}_loaded"])

        def cols(w, c0, n):
            v = w.rearrange("(p k) n -> p k n", k=KD)[:, :, c0:c0 + n]
            half = KD // 2
            return [(lambda r, i=i: r[:, 0:KD * n].rearrange("p (k n) -> p k n", k=KD)[:, i * half:(i + 1) * half, :],
                     v[:, i * half:(i + 1) * half, :]) for i in range(2)]

        def out_cols(w, c0):
            v = w.rearrange("(j p) n -> p j n", p=P)[:, :, c0:c0 + 512]
            return [(lambda r, i=i: r.rearrange("p (j n) -> p j n", n=512)[:, 4 * i:4 * i + 4, :],
                     v[:, 4 * i:4 * i + 4, :]) for i in range(2)]

        def quad_units(l, q):
            wg = moe_w_gate[l].rearrange("(q e) (p c r) f -> q c p e (r f)", e=QE, p=P, c=KD // 2)
            wu = moe_w_up[l].rearrange("(q e) (p c r) f -> q c p e (r f)", e=QE, p=P, c=KD // 2)
            wd = moe_w_down[l].rearrange("(q e) (p j) n -> q j p e n", e=QE, j=KF)
            for c in range(KD // 2):
                yield [(lambda r, i=i: r.rearrange("p (w e f) -> p w e f", w=2, e=QE)[:, i], w[q][c])
                       for i, w in enumerate((wg, wu))]
            for j in range(KF):
                v = wd[q][j]
                yield [(lambda r, i=i: r.rearrange("p (e n) -> p e n", e=QE)[:, 2 * i:2 * i + 2],
                        v[:, 2 * i:2 * i + 2]) for i in range(2)]

        @block.sync
        def _(sp):
            for t in range(TT):
                sp.dma_start(h[:, t, :], x[0, t * P:(t + 1) * P, :]).then_inc(s[f"x_loaded{t}"], 16)
            att, w_out = att_w_in[0], att_w_out[0]

            def blocks(width, *pieces):
                parts, at = [], 0
                for c0, n in pieces:
                    parts.append((lambda r, at=at, n=n: r[:, 0:KD * width].rearrange("p (k n) -> p k n", k=KD)
                                  [:, :, at:at + n], att.rearrange("(p k) n -> p k n", k=KD)[:, :, c0:c0 + n]))
                    at += n
                return parts

            plan = [cols(att, 0, 512), blocks(512, (C_KC, 3 * P), (C_KW, P)),
                    blocks(WG, (C_VS, P), (C_VW, WG - P)),
                    [(lambda r, i=i, odd=odd: r.rearrange("p (w j n) -> p w j n", w=2, n=P)[odd * DH:(odd + 1) * DH, i],
                      w[0].rearrange("(j odd d) n -> odd d j n", odd=2, d=DH)[odd])
                     for i, w in enumerate((cmp_w1_k, cmp_w1_v)) for odd in range(2)],
                    cols(att, C_QB, 512), cols(att, C_KB, 512), cols(att, C_VB, 512),
                    out_cols(w_out, 0), out_cols(w_out, 512)]
            assert len(plan) == ATT_UNITS
            for u, parts in enumerate(plan):
                load_ring(sp, u, parts)

            rec, w_out = rec_w_in[0], rec_w_out[0]
            plan_rec = [cols(rec, c, 512) for c in (1024, 1536, 0, 512, 2048, 2560, 3072, 3584)]
            plan_rec += [out_cols(w_out, 0), out_cols(w_out, 512)]
            assert len(plan_rec) == REC_UNITS

            before = 0
            for l in range(NL):
                if l:
                    for i, parts in enumerate(plan_rec):
                        load_ring(sp, BASE_REC + i, parts, before)
                quads = [list(quad_units(l, q)) for q in range(2)]
                base = BASE_MOE[l]
                for i in range(3):
                    load_ring(sp, base + i, quads[0][i], before)
                free = [(s["nsa_pv"], 8), (s["sb_pv"], SB_H)] if l == 0 else [(s["a_used"], 1), (s["recT_psum"], 4)]
                for i in range(SPARE):
                    if i % 2 == 0:
                        sp.wait_ge(*free[i // 2])
                    load_spare(sp, i, quads[1][i])
                for i in range(3, NU):
                    load_ring(sp, base + i, quads[0][i], before)
                for i in (4, 5):
                    load_ring(sp, base + NU + i - SPARE, quads[1][i], before)
                with sp.Fori(2, NQ) as q:
                    for i, parts in enumerate(quad_units(l, q)):
                        load_ring(sp, BASE_LOOP[l] + i, parts, q - 2 + before)
                sp.wait_ge(s["passes_ready"], l + 1)
                more = sp.value_load(passes[l][0:1, 0:1], min_val=0, max_val=PASS_MAX - 1)
                with sp.If(more > 0):
                    with sp.Fori(0, more) as r:
                        with sp.Fori(0, NQ) as q:
                            for i, parts in enumerate(quad_units(l, q)):
                                load_ring(sp, BASE_LOOP[l] + i, parts, q + NQ * (r + 1) - 2 + before)
                before = before + NQ * more
            for t in range(TT):
                sp.wait_ge(s["xg_done"], 2 * 2 * NL + t + 1)
                sp.dma_start(out[0, t * P:(t + 1) * P, :], xg[:, t, :]).then_inc(s["out_done"], 16)
            sp.wait_ge(s["out_done"], 16 * TT)

        @block.gpsimd
        def _(pool):
            link = Chain(pool, s["pool_chain"])

            def gain_load(v):
                src = [norm_mix[0], norm_ffn[0], norm_mix[1], norm_ffn[1], final_norm][v]
                if v:
                    pool.wait_ge(s["xg_done"], TT * v)
                pool.dma_start(gain[:, :], src.partition_broadcast(P)).then_inc(s["gain_loaded"], 16)

            def route_load(l):
                if l:
                    pool.wait_ge(s["route_used"], l)
                pool.dma_start(w_route[:, :, 0:GR], moe_w_grp[l].rearrange("(p k) n -> p k n", k=KD))\
                    .then_inc(s["route_loaded"], 16)
                pool.dma_start(w_route[:, :, GR:], moe_w_exp[l].rearrange("(p k) n -> p k n", k=KD))\
                    .then_inc(s["route_loaded"], 16)
                pool.dma_start(b_route[:, 0:GR], moe_b_grp[l].partition_broadcast(P))\
                    .then_inc(s["route_loaded"], 16)
                pool.dma_start(b_route[:, GR:], moe_b_exp[l].partition_broadcast(P))\
                    .then_inc(s["route_loaded"], 16)

            link(pool.memset(ident[:, :], 0.0))
            pool.affine_select(out=ident[:, :], in_=ident[:, :], compare_op=ALU.not_equal, fill=1.0, base=0,
                               pattern=[[-1, P]], channel_multiplier=1).then_inc(s["ident_done"], 1)
            pool.memset(eps_col[:, :], EPS).then_inc(s["eps_done"], 1)
            pool.memset(kv2[:, :, NSA_G, :], 0.0).then_inc(s["kv2_zero"], 1)

            link(pool.memset(causal[:, :, :], 0.0))
            link(pool.affine_select(out=causal[:, 1, :], in_=causal[:, 1, :], compare_op=ALU.is_ge, fill=NEG,
                                    base=0, pattern=[[-1, P]], channel_multiplier=1))
            link(pool.memset(cmask[:, :, :], 0.0))
            link(pool.memset(cvis[:, :, :], 1.0))
            for dst, fill in ((cmask, NEG), (cvis, 0.0)):
                link(pool.affine_select(out=dst[:, :, :], in_=dst[:, :, :], compare_op=ALU.is_ge, fill=fill,
                                        base=1 - CMP_LEN, pattern=[[P, TT], [-CMP_STRIDE, NC]],
                                        channel_multiplier=1))
            link(pool.memset(later_all[:, :], -1.0))
            link(pool.affine_select(out=later_own[:, :], in_=later_all[:, :], compare_op=ALU.is_ge, fill=0.0,
                                    base=0, pattern=[[-1, P]], channel_multiplier=1))
            link(pool.memset(cp[:, :, :, :], 0.0))
            link(pool.memset(hv4[:, :, :, :], 0.0))
            link(pool.memset(ones[:, :], 1.0))
            link(pool.affine_select(out=earlier[:, :], in_=ones[:, :], compare_op=ALU.is_gt, fill=0.0, base=0,
                                    pattern=[[1, P]], channel_multiplier=-1))
            link(pool.iota(iota_i[:, :], pattern=[[1, NE]], base=0, channel_multiplier=0))
            link(pool.tensor_copy(rank[:, :], iota_i[:, :]))
            link(pool.tensor_scalar(iota_slot[:, :], rank[:, 0:CAP], 1.0, None, ALU.add))
            link(pool.tensor_scalar(rank[:, :], rank[:, :], 1.0 / 64, None, ALU.mult))
            link(pool.memset(before_query, 0.0))
            link(pool.affine_select(out=before_query, in_=before_query, compare_op=ALU.is_gt, fill=NEG, base=0,
                                    pattern=[[1, P]], channel_multiplier=-1))
            link(pool.tensor_copy(before_r[:, :], before_query))
            pool.tensor_copy(ident_r[:, :], ident[:, :]).then_inc(s["const_done"], 1)

            route_load(0)
            gain_load(1)
            for r in range(ATT_QUARTERS):
                split_low(pool, U_QB, r, "att")
            for r in range(MIX_QUARTERS):
                split_low(pool, U_WO, r, "mix0")
            gain_load(2)

            rlink = Chain(pool, s["pool_rec_chain"])
            pool.wait_ge(s["xg_done"], 3 * TT)
            rlink(pool.memset(reset, 1.0))
            pool.memset(reset.rearrange("p (c i) -> p c i", i=CH)[:, :, 0:1], 0.0).then_inc(s["rec_const"], 1)
            route_load(1)
            def left(hh):
                sl = slice(4 * hh, 4 * hh + 4)
                cum = rB[:, sl, :].rearrange("p h (c i) -> p (h c) i", i=CH)
                pool.wait_ge(s["rec_cum"], hh + 1)
                pool.tensor_tensor(rD[:, sl, :].rearrange("p h (c i) -> p (h c) i", i=CH),
                                   cum[:, :, CH - 1:CH].broadcast_to([P, 4 * NCH, CH]), cum, ALU.subtract)\
                    .then_inc(s["rec_left"], 1)

            def k_out(hh):
                sl = slice(4 * hh, 4 * hh + 4)
                pool.wait_ge(s["rec_exps"], 4 * hh + 4)
                pool.tensor_tensor(rD[:, sl, :], rD[:, sl, :], rA[:, sl, :], ALU.mult)\
                    .then_inc(s["rec_kout"], 1)

            def k_in(hh):
                sl = slice(4 * hh, 4 * hh + 4)
                pool.tensor_tensor(r2[:, sl, :], r2[:, sl, :], rA[:, sl, :], ALU.mult)\
                    .then_inc(s["rec_kin"], 1)

            split_low(pool, BASE_REC, 1, "rec")
            split_low(pool, BASE_REC, 3, "rec")
            for m in range(16):
                if 2 * m + 5 < REC_QUARTERS:
                    split_low(pool, BASE_REC, 2 * m + 5, "rec")
                if m in (4, 6):
                    left(m // 2 - 2)
                if m in (7, 9):
                    k_out((m - 7) // 2)
                if m in (8, 10):
                    k_in((m - 8) // 2)
            gain_load(3)
            pool.wait_ge(s["rec_kout"], 2)
            pool.wait_ge(s["rec_kin"], 2)
            pool.wait_ge(s["w_low_pool"], LOW_POOL["mix1"])
            aMv = aM.rearrange("p h t -> p (h t)").rearrange("p (g t) -> p g t", t=P)
            pool.memset(aMv[0:CH, :, CH:P], 0.0).then_inc(s["rec_zero"], 1)
            pool.memset(aMv[CH:P, :, 0:CH], 0.0).then_inc(s["rec_zero"], 1)
            pool.wait_ge(s["rec_zero"], 2)
            for b in range(4):
                pool.wait_ge(s["rec_a_copied"], 2 * b + 2)
                v = aMv[:, 4 * b:4 * b + 4, :]
                pool.affine_select(out=v, in_=v, compare_op=ALU.is_ge, fill=0.0, base=0,
                                   pattern=[[0, 4], [1, P]], channel_multiplier=-1)\
                    .then_inc(s["rec_a_masked"], 1)
            for r in range(MIX_QUARTERS):
                split_low(pool, BASE_REC + 8, r, "mix1")
            gain_load(4)

        START, ROUTE, NORM = 16, 18, 10
        PROJ_AT = {0: 6, 2: 7, 3: 8, 4: 9, 5: 10, 6: 11}
        COMBINE_BANKS = (7, 2, 0, 1)
        H_NEEDED = [None, (7, 8), (10, 12), (19, 20), (22, 24)]

        @block.scalar
        def _(act):
            link = Chain(act, s["act_chain"])

            def norm(v, t, buf):
                if v == 0:
                    act.wait_ge(s[f"x_loaded{t}"], 16)
                    act.wait_ge(s["eps_done"], 1)
                else:
                    act.wait_ge(s["h_done"], H_NEEDED[v][t])
                link(act.activation(buf, h[:, t, :], ACT.Square, accum_out=norm_sum[:, v, t:t + 1]))
                rstd(v, t)

            def rstd(v, t):
                link(act.activation(norm_sum[:, v, t:t + 1], norm_sum[:, v, t:t + 1], ACT.Ln,
                                    bias=eps_col[:, 0:1], scale=1.0 / D))
                act.activation(norm_rstd[:, v, t:t + 1], norm_sum[:, v, t:t + 1], ACT.Exp, scale=-0.5)\
                    .then_inc(s["norm_rstd"], 1)

            def split_high(base, r, before=0):
                if r % 4 == 0:
                    act.wait_ge(*arrival(base + r // 4, before))
                act.activation(quarter_hi(r), quarter(base, r), ACT.Copy).then_inc(s["w_high"], 1)

            def split_mix(l, r, before):
                if r == 0:
                    act.wait_ge(*((s["rec_psum"], REC_QUARTERS) if l else (s["proj_psum"], 12)))
                if r >= 4:
                    act.wait_ge(s["mix_psum"], 8 * l + r // 2 * 2 - 2)
                split_high(BASE_REC + 8 if l else U_WO, r, before)

            def mix_and_norm(l, before):
                v = 2 * l + 1
                for m in range(4):
                    for r in (2 * m + 4, 2 * m + 5):
                        if r < MIX_QUARTERS:
                            split_mix(l, r, before)
                    for t in range(TT):
                        act.wait_ge(s["h_done"], 12 * l + 2 * m + t + 1)
                        link(act.activation(square_moe[:, 0:256], h[:, t, m * 256:(m + 1) * 256], ACT.Square,
                                            accum_out=norm_part[:, l, t, m:m + 1]))
                        if m == 3:
                            link(act.activation(square_moe[:, 0:4], norm_part[:, l, t, :], ACT.Copy,
                                                accum_out=norm_sum[:, v, t:t + 1]))
                            rstd(v, t)
                for t in range(TT):
                    xT_half(v, t)

            def xT_half(v, t):
                act.wait_ge(s["xT_psum"], 4 * v + 2 * t + 1)
                act.activation((x_hi if v in (0, 2) else xT)[:, 0:4, t * P:(t + 1) * P],
                               bank(2 * t).rearrange("p (k t) -> p k t", k=4), ACT.Copy)\
                    .then_inc(s["xT_front"], 1)

            act.preload_act_table_set("natural_log_exp_and_others")
            act.dma_start(gain[:, :], norm_mix[0].partition_broadcast(P)).then_inc(s["gain_first"], 16)
            for i, pe in enumerate((cmp_pe_k, cmp_pe_v)):
                act.dma_start(pe_rows[0:LP, i, :], pe[0].rearrange("(j two) d -> j (two d)", two=2))\
                    .then_inc(s["cmp_small"], 16)
            for i, w in enumerate((cmp_w2_k, cmp_w2_v)):
                act.dma_start(w2[:, i, :], w[0]).then_inc(s["cmp_small"], 16)
            act.dma_start(lb_rows[0:2 * RH, :], rec_lb_logits.rearrange("l (h p) -> (l h) p", p=RK))\
                .then_inc(s["rec_small"], 16)
            act.dma_start(gnorm[:, :], rec_gnorm[0].partition_broadcast(P)).then_inc(s["rec_small"], 16)
            for t in range(TT):
                norm(0, t, square)
            for t in range(TT):
                xT_half(0, t)

            def proj(n):
                act.wait_ge(s["proj_psum"], n + 1)
                src = bank(n % 2)
                if n == 0:
                    act.activation(qT[:, 0:2, :], src.rearrange("p (a t) -> p a t", a=2), ACT.Copy,
                                   scale=DH ** -0.5).then_inc(s["proj_even"], 1)
                elif n == 2:
                    last = None
                    for kv in range(2):
                        for g in range(NSA_G):
                            part = bank(0)[g * DH:(g + 1) * DH, kv * T:(kv + 1) * T]
                            act.activation(kv2[0:DH, kv, g, :], part, ACT.Copy).then_inc(s["kv2_done"], 1)
                            last = act.activation(kv2[DH:P, kv, g, 0:T - 1], part[:, 1:T], ACT.Copy)
                            if (kv, g) != (1, 1):
                                last.then_inc(s["kv2_done"], 1)
                    last.then_inc(s["proj_even"], 1)
                elif n == 4:
                    act.activation(vsw[:, 0, :], src[:, 0:280], ACT.Copy).then_inc(s["proj_even"], 1)
                elif n == 6:
                    act.activation(qbT[:, 0:2, :], src.rearrange("p (a t) -> p a t", a=2), ACT.Copy,
                                   scale=DH ** -0.5).then_inc(s["proj_even"], 1)
                elif n == 8:
                    act.activation(kbT[:, 0:2, :], src.rearrange("p (a t) -> p a t", a=2), ACT.Copy)\
                        .then_inc(s["proj_even"], 1)
                elif n == 10:
                    act.activation(vb[:, :, 0:256], src.rearrange("p (t n) -> p t n", t=TT), ACT.Copy)\
                        .then_inc(s["proj_even"], 1)

            def split_first(r):
                if r < 4:
                    if r == 0:
                        act.wait_ge(*arrival(U_Q))
                    act.activation(by_group(quarter_hi(r)), q_quarter(r), ACT.Copy).then_inc(s["w_high"], 1)
                else:
                    if r % 2 == 0:
                        act.wait_ge(s["proj_psum"], r // 2 - 1)
                    split_high(U_KV, r - 4)

            for r in range(6):
                split_first(r)
            proj(0)
            for r in (6, 7):
                split_first(r)
            act.wait_ge(*arrival(U_WG))
            act.activation(wg_hi[:, :, :], wg, ACT.Copy).then_inc(s["w_high"], 1)
            proj(2)
            act.wait_ge(s["cmp_inner"], 1)
            act.activation(cmp_g, cmp_g, ACT.Exp, scale=-2.0 * GELU_A).then_inc(s["cmp_exp"], 1)
            proj(4)
            act.wait_ge(s["cmp_kv"], 1)
            act.activation(kcT[0:DH, :], bank(5)[0:DH, 0:NC], ACT.Copy).then_inc(s["cmp_kv_done"], 1)
            act.activation(kcT[DH:P, :], bank(5)[0:DH, NC:2 * NC], ACT.Copy).then_inc(s["cmp_kv_done"], 1)
            act.activation(vc4, bank(5)[:, 64:192].rearrange("p (g d) -> p g d", g=2), ACT.Copy)\
                .then_inc(s["cmp_kv_done"], 1)
            act.wait_ge(s["proj_even"], 3)
            act.wait_ge(s["proj_odd"], 3)
            act.activation(gates, vsw[:, :, C_GATE - C_KW:280], ACT.Exp, scale=-1.0)\
                .then_inc(s["gate_exp"], 1)
            for r in range(4):
                if r % 2 == 0:
                    act.wait_ge(s["proj_psum"], 3 + r // 2)
                split_high(U_QB, r)
            act.wait_ge(s["cmp_shifted"], 1)
            act.activation(cs, cs, ACT.Exp).then_inc(s["cmp_probs"], 1)

            def exps(u):
                nk = P * (u // 4 + 1)
                act.wait_ge(s["nsa_max"], u + 1)
                for i in range(HPG):
                    v = scores[:, u % 2, i, 0:nk]
                    act.activation(v, v, ACT.Exp, bias=stat[:, u % 2, 0, i:i + 1],
                                   accum_out=stat[:, u % 2, 1, i:i + 1]).then_inc(s["nsa_exp"], 1)

            exps(0)
            for u in range(8):
                if u + 1 < 8:
                    exps(u + 1)
                n = PROJ_AT.get(u)
                if n in (6, 8, 10):
                    proj(n)
                if n in (6, 7, 8, 9):
                    act.wait_ge(s["proj_psum"], n + 1)
                    for r in (2 * n - 8, 2 * n - 7):
                        split_high(U_QB, r)
                if u == 0:
                    act.wait_ge(s["cmp_pT"], 1)
                    act.activation(pcT, bank(5).rearrange("p (g t) -> p g t", g=2), ACT.Copy)\
                        .then_inc(s["cmp_pT_done"], 1)
                act.wait_ge(s["nsa_pT"], u + 1)
                if u >= 2:
                    act.wait_ge(s["nsa_pv"], u - 1)
                act.activation(probsT[:, u % 2, 0, :], bank(2), ACT.Copy).then_inc(s["nsa_pT_even"], 1)

            def exp_ln(hd):
                act.wait_ge(s["sb_z"], hd + 1)
                if hd >= 3:
                    act.wait_ge(s["sb_t"], hd - 2)
                v = ztmp[:, hd % 3, :]
                link(act.activation(v, bank(SB_BANKS[hd % 4])[:, 0:384], ACT.Abs))
                link(act.activation(v, v, ACT.Exp, scale=-1.0))
                act.activation(v, v, ACT.Ln, bias=1.0).then_inc(s["sb_ln"], 1)

            exp_ln(0)
            act.wait_ge(s["nsa_pv"], 8)
            for g in range(NSA_G):
                act.activation(mix_hi[:, 2 * g:2 * g + 2, :], bank(6 + g).rearrange("p (a t) -> p a t", a=2),
                               ACT.Copy).then_inc(s["oT_high"], 1)
            for hd in range(SB_H):
                if hd + 1 < SB_H:
                    exp_ln(hd + 1)
                if hd < 4:
                    split_mix(0, hd, 0)
                act.wait_ge(s["sb_e"], hd + 1)
                if hd >= 2:
                    act.wait_ge(s["sb_pv"], hd - 1)
                act.activation(za[:, hd % 2, :], bank(SB_BANKS[hd % 4])[:, 0:384], ACT.Exp).then_inc(s["sb_a"], 1)

            def route(l):
                act.wait_ge(s["route_diff"], l + 1)
                for t in range(TT):
                    act.activation(route_t[:, 3, t, 0:GR], logit[:, t, 0:GR], ACT.Exp,
                                   bias=route_s[:, 0, t:t + 1], accum_out=route_s[:, 1, t:t + 1])\
                        .then_inc(s["route_exp"], 1)
                act.activation(route_s[:, 5, :], route_s[:, 4, :], ACT.Exp).then_inc(s["route_exp"], 1)

            def quad(l, n):
                act.wait_ge(s[f"gathered{l}"], 2 * n + 1)
                act.activation(gatheredT[:, 0:4, :], bank(0).rearrange("p (k c) -> p k c", k=4), ACT.Copy)\
                    .then_inc(s[f"gatheredT{l}"], 1)
                act.wait_ge(s[f"gate_up{l}"], n + 1)
                act.activation(egate, bank(3)[:, 0:FF], ACT.Exp, scale=-1.0).then_inc(s[f"egate{l}"], 1)
                act.wait_ge(s[f"egate{l}"], 3 * n + 1)
                act.activation(egate, egate, ACT.Ln, bias=1.0).then_inc(s[f"egate{l}"], 1)
                act.wait_ge(s[f"egate{l}"], 3 * n + 2)
                act.activation(egate, egate, ACT.Exp, scale=-1.0).then_inc(s[f"egate{l}"], 1)
                act.wait_ge(s[f"hid_psum{l}"], n + 1)
                act.activation(hidT, bank(4)[:, 0:FF].rearrange("p (j c) -> p j c", j=KF), ACT.Copy)\
                    .then_inc(s[f"hidT{l}"], 1)
                act.activation(shareT, bank(4)[:, FF:2 * FF].rearrange("p (t c) -> p t c", t=TT), ACT.Copy)\
                    .then_inc(s[f"shareT{l}"], 1)
                act.wait_ge(s[f"down{l}"], n + 1)
                act.activation(y_rows[:, 0:512], bank(5), ACT.Copy).then_inc(s[f"y_rows{l}"], 1)

            def experts(l):
                route(l)
                for q in range(2):
                    quad(l, q)
                with act.Fori(2, NQ) as q:
                    quad(l, q)
                act.wait_ge(s["passes_ready"], l + 1)
                more = act.value_load(passes[l][0:1, 0:1], min_val=0, max_val=PASS_MAX - 1)
                with act.If(more > 0):
                    with act.Fori(0, more) as r:
                        with act.Fori(0, NQ) as q:
                            quad(l, q + NQ * (r + 1))
                return NQ * more

            mix_and_norm(0, 0)
            before = experts(0)

            def split_rec(r):
                if r == 0:
                    act.wait_ge(s["unit_used"], BASE_REC + NU * before)
                elif r >= 4:
                    act.wait_ge(s["rec_psum"], r - 3 if r < 20 else r // 2 * 2 - 2)
                split_high(BASE_REC, r, before)

            for t in range(TT):
                norm(2, t, square_moe)
            for t in range(TT):
                split_rec(t)
                xT_half(2, t)
            for r in (2, 3):
                split_rec(r)
            act.wait_ge(s["lb_diff"], 1)
            act.activation(lbt[:, 0:2, :], lbt[:, 0:2, :], ACT.Exp).then_inc(s["lb_exp"], 1)
            def f_exp(m):
                act.activation(rA[:, 2 * m:2 * m + 2, :], bank(4 + m).rearrange("p (a t) -> p a t", a=2), ACT.Exp)\
                    .then_inc(s["rec_f"], 1)

            def log_f(hh):
                sl = slice(4 * hh, 4 * hh + 4)
                act.wait_ge(s["rec_key"], 2 * hh + 2)
                act.activation(rC[:, sl, :], rA[:, sl, :], ACT.Ln, bias=1.0, scale=-1.0)\
                    .then_inc(s["rec_logf"], 1)

            def decay_exps(hh, first):
                sl = slice(4 * hh, 4 * hh + 4)
                if first:
                    act.wait_ge(s["rec_cum"], hh + 1)
                    act.activation(r3[:, sl, :], rB[:, sl, :], ACT.Exp).then_inc(s["rec_exps"], 1)
                    act.wait_ge(s["rec_rel"], hh + 1)
                    act.activation(r1[:, sl, :], rC[:, sl, :], ACT.Exp).then_inc(s["rec_exps"], 1)
                else:
                    act.activation(r2[:, sl, :], rC[:, sl, :], ACT.Exp, scale=-1.0).then_inc(s["rec_exps"], 1)
                    act.wait_ge(s["rec_left"], hh + 1)
                    act.activation(rD[:, sl, :], rD[:, sl, :], ACT.Exp).then_inc(s["rec_exps"], 1)

            def gate_sigmoid(i):
                v = e_gate[:, :, i * 256:(i + 1) * 256]
                link(act.activation(v, bank(4 + i).rearrange("p (t n) -> p t n", t=TT), ACT.Exp, scale=-1.0))
                link(act.activation(v, v, ACT.Ln, bias=1.0))
                act.activation(v, v, ACT.Exp, scale=-1.0).then_inc(s["rec_gate_exp"], 1)

            for m in range(16):
                for r in (2 * m + 4, 2 * m + 5):
                    if r < REC_QUARTERS:
                        split_rec(r)
                act.wait_ge(s["rec_psum"], 2 * m + 2)
                if m < 4:
                    f_exp(m)
                if m in (3, 5):
                    log_f((m - 3) // 2)
                if m in (5, 6):
                    decay_exps(0, m == 5)
                if m in (7, 8):
                    decay_exps(1, m == 7)
                if 8 <= m < 12:
                    act.activation(rv[:, :, (m - 8) * 256:(m - 7) * 256],
                                   bank(m - 4).rearrange("p (t n) -> p t n", t=TT), ACT.Copy)\
                        .then_inc(s["rec_v"], 1)
                if m >= 12:
                    if m == 12:
                        act.wait_ge(s["rec_exps"], 8)
                    gate_sigmoid(m - 12)
            act.wait_ge(s["rec_left"], 2)
            act.wait_ge(s["rec_rel"], 2)
            for b in (0, 2):
                act.wait_ge(s["ko_psum"], b + 1)
                act.activation(koR[:, b // 2, (b % 2) * 512:(b % 2) * 512 + 512], bank(b), ACT.Copy)\
                    .then_inc(s["ko_done"], 1)
            aMv = aM.rearrange("p h t -> p (h t)").rearrange("p (g t) -> p g t", t=P)
            act.wait_ge(s["rec_zero"], 2)
            for b in range(4):
                act.wait_ge(s["a_psum"], b + 1)
                for lo in (0, CH):
                    act.activation(aMv[lo:lo + CH, 4 * b:4 * b + 4, lo:lo + CH],
                                   bank(4 + b)[lo:lo + CH, :].rearrange("p (g t) -> p g t", g=4)[:, :, lo:lo + CH],
                                   ACT.Copy).then_inc(s["rec_a_copied"], 1)
            for r in range(4):
                split_mix(1, r, before)
            act.wait_ge(s["rec_kin_used"], 1)
            for t in range(TT):
                act.wait_ge(s["o_psum"], t + 1)
                o_ps = psum[:, 4 + 2 * t:6 + 2 * t, :].rearrange("p b n -> p (b n)")
                for hd in range(RH):
                    d = slice(hd * RV, (hd + 1) * RV)
                    act.activation(square_rec[:, d], o_ps[:, d], ACT.Square,
                                   accum_out=ostat[:, 0, t * RH + hd:t * RH + hd + 1]).then_inc(s["o_square"], 1)
                act.wait_ge(s["o_square"], RH * (t + 1))
                v = ostat[:, 0, t * RH:(t + 1) * RH]
                link(act.activation(v, v, ACT.Ln, bias=eps_col[:, 0:1], scale=1.0 / RV))
                act.activation(ostat[:, 1, t * RH:(t + 1) * RH], v, ACT.Exp, scale=-0.5)\
                    .then_inc(s["o_rstd"], 1)
            for b in range(4):
                act.wait_ge(s["recT_psum"], b + 1)
                act.activation(mix_hi[:, 4 * (b % 2):4 * (b % 2) + 4, (b // 2) * P:(b // 2 + 1) * P],
                               bank(b).rearrange("p (k t) -> p k t", k=4), ACT.Copy).then_inc(s["recT_high"], 1)

            mix_and_norm(1, before)
            experts(1)
            for t in range(TT):
                norm(4, t, square_moe)

        @block.vector
        def _(dve):
            link = Chain(dve, s["dve_chain"])

            def norm(v, t):
                dve.wait_ge(s["norm_rstd"], TT * v + t + 1)
                if v == 0:
                    dve.wait_ge(s["gain_first"], 16)
                else:
                    dve.wait_ge(s["gain_loaded"], 16 * v)
                dve.scalar_tensor_tensor(out=xg[:, t, :], in0=h[:, t, :], scalar=norm_rstd[:, v, t:t + 1],
                                         in1=gain[:, :], op0=ALU.mult, op1=ALU.mult)\
                    .then_inc(s["xg_done"], 1)

            def xT_half(v, t):
                dve.wait_ge(s["xT_psum"], 4 * v + 2 * t + 2)
                dve.tensor_copy((x_hi if v in (0, 2) else xT)[:, 4:8, t * P:(t + 1) * P],
                                bank(2 * t + 1).rearrange("p (k t) -> p k t", k=4)).then_inc(s["xT_back"], 1)

            def x_low(v, t):
                dve.wait_ge(s["xT_front"], TT * v + t + 1)
                dve.wait_ge(s["xT_back"], TT * v + t + 1)
                dve.tensor_tensor(x_lo[:, t], psum[:, 2 * t:2 * t + 2, :].rearrange("p b (k c) -> p (b k) c", k=4),
                                  x_hi[:, :, t * P:(t + 1) * P].bitcast(F32), ALU.subtract)\
                    .then_inc(s["x_lo_done"], 1)

            for t in range(TT):
                norm(0, t)
            xT_half(0, 0)
            x_low(0, 0)
            xT_half(0, 1)
            for i in range(4):
                dve.wait_ge(s["w_high"], i + 1)
                dve.tensor_tensor(by_group(q_lo[:, i]), q_quarter(i), by_group(quarter_hi(i).bitcast(F32)),
                                  ALU.subtract).then_inc(s["w_low_dve"], 1)
                if i == 0:
                    x_low(0, 1)
            for r in (0, 1):
                split_low(dve, U_KV, r, "kv")

            def proj(n):
                dve.wait_ge(s["proj_psum"], n + 1)
                src = bank(n % 2)
                pair = src.rearrange("p (a t) -> p a t", a=2)
                if n in (1, 7):
                    dst = (qT if n == 1 else qbT)[:, 2:4, :]
                    ins = dve.tensor_scalar(dst, pair, DH ** -0.5, None, ALU.mult)
                elif n == 3:
                    ins = dve.tensor_copy(ksw, pair)
                elif n == 5:
                    ins = dve.tensor_copy(vsw[:, 1, :], src[:, 0:280])
                elif n == 9:
                    ins = dve.tensor_copy(kbT[:, 2:4, :], pair)
                else:
                    ins = dve.tensor_copy(vb[:, :, 256:512], src.rearrange("p (t n) -> p t n", t=TT))
                ins.then_inc(s["proj_odd"], 1)

            proj(1)
            dve.wait_ge(s["pe_psum"], 1)
            dve.wait_ge(s["kv2_zero"], 1)
            dve.tensor_copy(kv2[:, :, NSA_G, 0:CMP_LEN:2], bank(5)[:, 0:2 * LP].rearrange("p (a j) -> p a j", a=2))\
                .then_inc(s["pe_done"], 1)
            for r in (2, 3):
                split_low(dve, U_KV, r, "kv")
            dve.wait_ge(s["w_high"], HIGH_BEFORE["wg"] + 1)
            dve.tensor_tensor(wg_lo[:, :, :], wg, wg_hi[:, :, :].bitcast(F32), ALU.subtract)\
                .then_inc(s["w_low_dve"], 1)
            proj(3)
            dve.wait_ge(s["cmp_hidden"], 1)
            hidden = bank(4)[:, 0:P].rearrange("p (a n) -> p a n", a=2)
            link(dve.tensor_copy(cmp_bias, hidden[:, :, NSA_G * NC]))
            for kv in range(2):
                link(dve.tensor_scalar(cmp_x[:, kv, :], hidden[:, kv, 0:NSA_G * NC],
                                       cmp_bias[:, kv:kv + 1], None, ALU.add))
            link(dve.tensor_tensor(cmp_g, cmp_x, cmp_x, ALU.mult))
            link(dve.tensor_scalar(cmp_g, cmp_g, GELU_B, 1.0, ALU.mult, ALU.add))
            dve.tensor_tensor(cmp_g, cmp_g, cmp_x, ALU.mult).then_inc(s["cmp_inner"], 1)
            dve.wait_ge(s["cmp_exp"], 1)
            link(dve.tensor_scalar(cmp_g, cmp_g, 1.0, None, ALU.add))
            link(dve.reciprocal(cmp_g, cmp_g))
            dve.wait_ge(s["const_done"], 1)
            dve.tensor_tensor(cmp_h, cmp_x, cmp_g, ALU.mult).then_inc(s["cmp_h_done"], 1)
            dve.wait_ge(s["cmp_h_done"], 1)
            for g in range(NSA_G):
                dve.tensor_copy(hv4[:, g, :, 0:NC], spread(cmp_h[:, 1, g * NC:(g + 1) * NC], 1, 4))\
                    .then_inc(s["cmp_h_done"], 1)
            proj(5)
            dve.wait_ge(s["gate_exp"], 1)
            link(dve.tensor_scalar(gates, gates, 1.0, None, ALU.add))
            link(dve.reciprocal(gates, gates))
            dve.wait_ge(s["cmp_scores"], 1)
            for t in range(TT):
                for g in range(NSA_G):
                    c = t * HPG * NC
                    link(dve.tensor_tensor(cs[:, t, g * HPG:(g + 1) * HPG], bank(4 + g)[:, c:c + HPG * NC]
                                           .rearrange("p (h c) -> p h c", h=HPG),
                                           spread(cmask[:, t, :], 1, HPG), ALU.add))
            flat = cs.rearrange("p t h c -> p (t h) c")
            link(dve.tensor_reduce(cstat[:, 0, :], flat, AX.X, ALU.max))
            dve.tensor_tensor(flat, flat, spread(cstat[:, 0, :], 2, NC), ALU.subtract)\
                .then_inc(s["cmp_shifted"], 1)

            def mask(u):
                t, nk = u // 4, P * (u // 4 + 1)
                dve.wait_ge(s["nsa_scores"], u + 1)
                if u >= 2:
                    dve.wait_ge(s["nsa_pT"], u - 1)
                src = (psum[:, 4:6, :].rearrange("p b n -> p (b n)")[:, 0:HPG * nk]
                       .rearrange("p (i k) -> p i k", i=HPG))
                if t == 0:
                    m = spread(causal[:, 1, :], 1, HPG)
                else:
                    m = spread(causal.rearrange("p a k -> p (a k)"), 1, HPG)
                v = scores[:, u % 2, :, 0:nk]
                dve.tensor_tensor(v, src, m, ALU.add).then_inc(s["nsa_masked"], 1)
                dve.wait_ge(s["nsa_masked"], u + 1)
                dve.tensor_reduce(stat[:, u % 2, 0, :], v, AX.X, ALU.max, negate=True)\
                    .then_inc(s["nsa_max"], 1)

            def scale(u):
                t, br, g, nk = u // 4, u // 2 % 2, u % 2, P * (u // 4 + 1)
                dve.wait_ge(s["nsa_exp"], HPG * (u + 1))
                link(dve.reciprocal(stat[:, u % 2, 2, :], stat[:, u % 2, 1, :]))
                c = (br + 1) * NSA_H + g * HPG
                link(dve.tensor_tensor(stat[:, u % 2, 3, :], stat[:, u % 2, 2, :], gates[:, t, c:c + HPG], ALU.mult))
                v = scores[:, u % 2, :, 0:nk]
                dve.tensor_tensor(v, v, spread(stat[:, u % 2, 3, :], 2, nk), ALU.mult)\
                    .then_inc(s["nsa_scaled"], 1)

            mask(0)
            dve.wait_ge(s["cmp_probs"], 1)
            link(dve.tensor_reduce(cstat[:, 1, :], flat, AX.X, ALU.add))
            link(dve.reciprocal(cstat[:, 2, :], cstat[:, 1, :]))
            link(dve.tensor_tensor(cstat[:, 3, :].rearrange("p (t h) -> p t h", t=TT),
                                   cstat[:, 2, :].rearrange("p (t h) -> p t h", t=TT),
                                   gates[:, :, 0:NSA_H], ALU.mult))
            link(dve.tensor_tensor(flat, flat, spread(cstat[:, 3, :], 2, NC), ALU.mult))
            for t in range(TT):
                dve.tensor_tensor(cp[:, t, :, 0:NC], cs[:, t], spread(cvis[:, t, :], 1, NSA_H), ALU.mult)\
                    .then_inc(s["cmp_p_done"], 1)
            for u in range(8):
                if u + 1 < 8:
                    mask(u + 1)
                scale(u)
                if PROJ_AT.get(u) in (7, 9, 11):
                    proj(PROJ_AT[u])
                if u >= 4:
                    dve.wait_ge(s["nsa_pT"], u + 1)
                    if u >= 6:
                        dve.wait_ge(s["nsa_pv"], u - 1)
                    dve.tensor_copy(probsT[:, u % 2, 1, :], bank(3)).then_inc(s["nsa_pT_odd"], 1)

            def out_low(a, b):
                dve.tensor_tensor(mix_lo[:, a:a + 2, :], bank(b).rearrange("p (a t) -> p a t", a=2),
                                  mix_hi[:, a:a + 2, :].bitcast(F32), ALU.subtract).then_inc(s["oT_low"], 1)

            def sb_out(b):
                dve.wait_ge(s["sb_pv"], 4 * b + 4)
                link(dve.tensor_copy(mix_hi[:, 4 + 2 * b:6 + 2 * b, :], bank(2 + b).rearrange("p (a t) -> p a t", a=2)))
                out_low(4 + 2 * b, 2 + b)

            for hd in range(SB_H):
                dve.wait_ge(s["sb_ln"], hd + 1)
                if hd >= 3:
                    dve.wait_ge(s["sb_e"], hd - 2)
                dve.scalar_tensor_tensor(out=zt[:, hd % 3, :], in0=bank(SB_BANKS[hd % 4])[:, 0:384], scalar=0.0,
                                         in1=ztmp[:, hd % 3, :], op0=ALU.max, op1=ALU.add)\
                    .then_inc(s["sb_t"], 1)
                if hd in (2, 3):
                    g = hd - 2
                    dve.wait_ge(s["oT_high"], g + 1)
                    dve.wait_ge(s["proj_psum"], 12)
                    out_low(2 * g, 6 + g)
                if hd == 6:
                    sb_out(0)
            sb_out(1)

            def add_mix(l, banks):
                v = 2 * l + 1
                for m in range(4):
                    for t in range(TT):
                        c = slice(m * 256, (m + 1) * 256)
                        dve.wait_ge(s["mix_psum"], 8 * l + 2 * m + t + 1)
                        dve.tensor_tensor(h[:, t, c], bank(banks[m % 2 * 2 + t])[:, 0:256],
                                          h[:, t, c], ALU.add).then_inc(s["h_done"], 1)
                        if m == 3 and t == 0:
                            norm(v, 0)
                norm(v, 1)
                for t in range(TT):
                    xT_half(v, t)

            def route(l):
                dve.wait_ge(s["route_psum"], l + 1)
                dve.wait_ge(s["route_loaded"], 64 * (l + 1))
                for t in range(TT):
                    ins = dve.tensor_tensor(logit[:, t, :], bank(4 + t)[:, 0:GR + NE], b_route[:, :], ALU.add)
                    ins.then_inc(s["route_logit"], 1)
                dve.wait_ge(s["route_logit"], TT * (l + 1))
                lg, le = logit[:, :, 0:GR], logit[:, :, GR:]
                t0, t1 = route_t[:, 0], route_t[:, 1]
                link(dve.tensor_reduce(route_s[:, 0, :], lg, AX.X, ALU.max, negate=True))
                link(dve.tensor_tensor(t0[:, :, 0:GR], lg, spread(route_s[:, 0, :], 2, GR), ALU.add))
                link(dve.scalar_tensor_tensor(out=t0[:, :, 0:GR], in0=t0[:, :, 0:GR], scalar=0.0,
                                              in1=spread(rank[:, 0:GR], 1, TT), op0=ALU.is_lt, op1=ALU.add))
                link(dve.tensor_reduce(route_s[:, 2, :], t0[:, :, 0:GR], AX.X, ALU.min))
                link(dve.tensor_tensor(t1[:, :, 0:GR], spread(rank[:, 0:GR], 1, TT),
                                       spread(route_s[:, 2, :], 2, GR), ALU.not_equal))
                for t in range(TT):
                    link(dve.scalar_tensor_tensor(out=t0[:, t, :].rearrange("p (g e) -> p g e", g=GR),
                                                  in0=spread(t1[:, t, 0:GR], 2, EPG), scalar=NEG,
                                                  in1=le[:, t, :].rearrange("p (g e) -> p g e", g=GR),
                                                  op0=ALU.mult, op1=ALU.add))
                for k in range(2):
                    link(dve.tensor_reduce(route_s[:, 6 + k, :], t0, AX.X, ALU.max))
                    link(dve.tensor_tensor(t1, t0, spread(route_s[:, 6 + k, :], 2, NE), ALU.is_lt))
                    link(dve.tensor_tensor(t1, t1, spread(rank[:, :], 1, TT), ALU.add))
                    link(dve.tensor_reduce(route_s[:, 3, :], t1, AX.X, ALU.min))
                    link(dve.tensor_tensor(chosen[:, k], spread(rank[:, :], 1, TT),
                                           spread(route_s[:, 3, :], 2, NE), ALU.is_equal))
                    if k == 0:
                        link(dve.scalar_tensor_tensor(out=t0, in0=chosen[:, 0], scalar=3.0 * NEG, in1=t0,
                                                      op0=ALU.mult, op1=ALU.add))
                dve.tensor_tensor(route_s[:, 4, :], route_s[:, 7, :], route_s[:, 6, :], ALU.subtract)\
                    .then_inc(s["route_diff"], 1)
                dve.tensor_tensor(member[:, :, :], chosen[:, 0], chosen[:, 1], ALU.add)\
                    .then_inc(s["member_done"], 1)
                dve.wait_ge(s["route_exp"], 3 * (l + 1))
                link(dve.tensor_scalar(route_s[:, 10, :], route_s[:, 5, :], 1.0, None, ALU.add))
                link(dve.tensor_tensor(route_s[:, 11, :], route_s[:, 10, :], route_s[:, 1, :], ALU.mult))
                link(dve.reciprocal(weight[:, 0, :], route_s[:, 11, :]))
                link(dve.tensor_tensor(weight[:, 1, :], weight[:, 0, :], route_s[:, 5, :], ALU.mult))
                dve.wait_ge(s["slot_psum"], l + 1)
                dve.wait_ge(s["member_done"], l + 1)
                link(dve.scalar_tensor_tensor(out=slot_of[:, :, :],
                                              in0=bank(6)[:, 0:TT * NE].rearrange("p (t e) -> p t e", t=TT),
                                              scalar=1.0, in1=member[:, :, :], op0=ALU.add, op1=ALU.mult))

            def shares_and_rounds(l):
                link(dve.tensor_tensor(route_t[:, 1], chosen[:, 0], spread(weight[:, 0, :], 2, NE), ALU.mult))
                link(dve.tensor_tensor(share[:, :, :], chosen[:, 1], spread(weight[:, 1, :], 2, NE), ALU.mult))
                link(dve.tensor_tensor(share[:, :, :], share[:, :, :], route_t[:, 1], ALU.add))
                dve.wait_ge(s["total_psum"], l + 1)
                link(dve.tensor_reduce(route_s[:, 8, 0:1], bank(7)[:, 0:NE], AX.X, ALU.max))
                for i in range(PASS_MAX - 1):
                    link(dve.tensor_scalar(passes_f[:, i:i + 1], route_s[:, 8, 0:1], float(CAP * (i + 1)), None,
                                           ALU.is_gt))
                link(dve.tensor_reduce(route_s[:, 9, 0:1], passes_f[:, 0:PASS_MAX - 1], AX.X, ALU.add))
                link(dve.tensor_copy(passes[l][:, :], route_s[0:1, 9, 0:1]))
                dve.sem_inc(s["route_used"], 1)
                dve.sem_inc(s["passes_ready"], 1)

            def expert_columns(table, q):
                return table[:, :, bass.ds(QE * q, QE)].unsqueeze(3).broadcast_to([P, TT, QE, CAP])

            def add_rows(l, m, done, first=False):
                if not first:
                    dve.wait_ge(s[f"added{l}"], 4 * m)
                for i, b in enumerate(COMBINE_BANKS):
                    t, half = divmod(i, 2)
                    v = h[:, t, half * 512:(half + 1) * 512]
                    dve.wait_ge(s[f"combined{l}"], 4 * m + i + 1)
                    dve.tensor_tensor(v, bank(b), v, ALU.add).then_inc(done, 1)

            def quad(l, n, q):
                first = isinstance(n, int) and n == 0
                dve.tensor_tensor(slots, iota_slot[:, :].unsqueeze(1).unsqueeze(1).broadcast_to([P, TT, QE, CAP]),
                                  expert_columns(slot_of, q), ALU.is_equal).then_inc(s[f"slots{l}"], 1)
                if first:
                    shares_and_rounds(l)
                dve.wait_ge(s[f"gathered{l}"], 2 * n + 2)
                dve.tensor_copy(gatheredT[:, 4:8, :], bank(1).rearrange("p (k c) -> p k c", k=4))\
                    .then_inc(s[f"gatheredT{l}"], 1)
                dve.wait_ge(s[f"slots{l}"], n + 1)
                dve.tensor_tensor(slots_share, slots, expert_columns(share, q), ALU.mult)\
                    .then_inc(s[f"slots_share{l}"], 1)
                dve.wait_ge(s[f"egate{l}"], 3 * n + 3)
                dve.tensor_tensor(hid_t, bank(3)[:, 0:FF], egate, ALU.mult).then_inc(s[f"hid{l}"], 1)
                dve.wait_ge(s[f"hid{l}"], 2 * n + 1)
                dve.tensor_tensor(hid, bank(3)[:, FF:2 * FF], hid_t, ALU.mult).then_inc(s[f"hid{l}"], 1)
                if not first:
                    add_rows(l, n - 1, s[f"added{l}"], isinstance(n, int) and n == 1)
                dve.wait_ge(s[f"down{l}"], n + 1)
                dve.tensor_copy(y_rows[:, 512:D], bank(6)).then_inc(s[f"y_rows{l}"], 1)

            def experts(l):
                route(l)
                for q in range(2):
                    quad(l, q, q)
                with dve.Fori(2, NQ) as q:
                    quad(l, q, q)
                dve.wait_ge(s["passes_ready"], l + 1)
                more = dve.value_load(passes[l][0:1, 0:1], min_val=0, max_val=PASS_MAX - 1)
                with dve.If(more > 0):
                    with dve.Fori(0, more) as r:
                        dve.tensor_scalar(slot_of[:, :, :], slot_of[:, :, :], -float(CAP), None, ALU.add)\
                            .then_inc(s[f"next_round{l}"], 1)
                        with dve.Fori(0, NQ) as q:
                            dve.wait_ge(s[f"next_round{l}"], r + 1)
                            quad(l, q + NQ * (r + 1), q)
                add_rows(l, NQ * more + NQ - 1, s["h_done"])
                for t in range(TT):
                    norm(2 * l + 2, t)
                if l == 0:
                    xT_half(2, 0)
                    split_low(dve, BASE_REC, 0, "rec")
                    xT_half(2, 1)
                    for t in range(TT):
                        x_low(2, t)
                    split_low(dve, BASE_REC, 2, "rec")

            add_mix(0, (0, 1, 4, 5))
            experts(0)

            dve.wait_ge(s["lb_psum"], 1)
            link(dve.tensor_copy(lb, bank(7)[:, 0:2 * RH]))
            link(dve.tensor_tensor(lbt[:, 2, :], lb[:, 0:RH], lb[:, RH:], ALU.max))
            link(dve.tensor_tensor(lbt[:, 0, :], lb[:, 0:RH], lbt[:, 2, :], ALU.subtract))
            dve.tensor_tensor(lbt[:, 1, :], lb[:, RH:], lbt[:, 2, :], ALU.subtract).then_inc(s["lb_diff"], 1)
            dve.wait_ge(s["lb_exp"], 1)
            link(dve.tensor_tensor(lbt[:, 2, :], lbt[:, 0, :], lbt[:, 1, :], ALU.add))
            link(dve.reciprocal(lbt[:, 3, :], lbt[:, 2, :]))
            link(dve.tensor_tensor(lbt[:, 0, :], lbt[:, 0, :], lbt[:, 3, :], ALU.mult))
            def key(m):
                v = rA[:, 2 * m:2 * m + 2, :]
                dve.wait_ge(s["rec_f"], m + 1)
                link(dve.tensor_scalar(v, v, 1.0, None, ALU.add))
                link(dve.reciprocal(v, v))
                dve.tensor_tensor(v, v, spread(lbt[:, 0, 2 * m:2 * m + 2], 2, T), ALU.mult)\
                    .then_inc(s["rec_key"], 1)

            def cumulate(hh):
                sl = slice(4 * hh, 4 * hh + 4)
                flat_cum = rB[:, sl, :].rearrange("p h t -> p (h t)")
                dve.wait_ge(s["rec_logf"], hh + 1)
                dve.tensor_tensor_scan(flat_cum, reset, rC[:, sl, :].rearrange("p h t -> p (h t)"), 0.0,
                                       ALU.mult, ALU.add).then_inc(s["rec_cum"], 1)
                dve.wait_ge(s["rec_cum"], hh + 1)
                cum = flat_cum.rearrange("p (g i) -> p g i", i=CH)
                dve.tensor_tensor(rC[:, sl, :].rearrange("p h (c i) -> p (h c) i", i=CH), cum,
                                  cum[:, :, CH // 2:CH // 2 + 1].broadcast_to([P, 4 * NCH, CH]), ALU.subtract)\
                    .then_inc(s["rec_rel"], 1)

            def queries(hh):
                sl = slice(4 * hh, 4 * hh + 4)
                dve.wait_ge(s["rec_q"], 4)
                dve.wait_ge(s["rec_exps"], 4 * hh + 4)
                link(dve.tensor_copy(decay[:, sl, :], r3[:, sl, :].rearrange("p h (c i) -> p h c i", i=CH)[:, :, :, CH - 1]))
                dve.tensor_tensor(r1[:, sl, :], r1[:, sl, :], rQ[:, sl, :], ALU.mult).then_inc(s["rec_qin"], 1)
                dve.tensor_tensor(r3[:, sl, :], r3[:, sl, :], rQ[:, sl, :], ALU.mult).then_inc(s["rec_qin"], 1)

            def gate_silu(i):
                v = e_gate[:, :, i * 256:(i + 1) * 256]
                dve.wait_ge(s["rec_gate_exp"], i + 1)
                dve.tensor_tensor(v, v, bank(4 + i).rearrange("p (t n) -> p t n", t=TT), ALU.mult)\
                    .then_inc(s["rec_gate"], 1)
                dve.wait_ge(s["rec_gate"], i + 1)
                for t in range(TT):
                    v3 = v[:, t, :].rearrange("p (h d) -> p h d", d=RV)
                    link(dve.tensor_tensor(v3, v3, spread(gnorm, 1, 256 // RV), ALU.mult))

            dve.wait_ge(s["rec_const"], 1)
            for m in range(16):
                if 2 * m + 4 < REC_QUARTERS:
                    split_low(dve, BASE_REC, 2 * m + 4, "rec")
                if m < 4:
                    key(m)
                elif m < 8:
                    dve.wait_ge(s["rec_psum"], 2 * m + 2)
                    dve.tensor_scalar(rQ[:, 2 * (m - 4):2 * (m - 4) + 2, :],
                                      bank(m - 4).rearrange("p (a t) -> p a t", a=2),
                                      RK ** -0.5, None, ALU.mult).then_inc(s["rec_q"], 1)
                if m in (4, 6):
                    cumulate(m // 2 - 2)
                if m in (8, 10):
                    queries((m - 8) // 2)
                if m >= 12:
                    gate_silu(m - 12)
            for b in (1, 3):
                dve.wait_ge(s["ko_psum"], b + 1)
                dve.tensor_copy(koR[:, b // 2, (b % 2) * 512:(b % 2) * 512 + 512], bank(b))\
                    .then_inc(s["ko_done"], 1)
            for c in range(NCH - 1):
                dve.wait_ge(s["state_psum"], c + 1)
                kv = psum[:, 2 * (c % 2):2 * (c % 2) + 2, :].rearrange("p b n -> p (b n)")
                if c == 0:
                    dve.tensor_copy(states[0], kv).then_inc(s["state_done"], RH)
                else:
                    for hd in range(RH):
                        d = slice(hd * RV, (hd + 1) * RV)
                        dve.scalar_tensor_tensor(out=states[c][:, d], in0=states[c - 1][:, d],
                                                 scalar=decay[:, hd, c:c + 1], in1=kv[:, d],
                                                 op0=ALU.mult, op1=ALU.add).then_inc(s["state_done"], 1)
                dve.wait_ge(s["state_done"], RH * (c + 1))
            dve.wait_ge(s["a_psum"], 4)
            for t in range(TT):
                dve.wait_ge(s["o_rstd"], t + 1)
                o_ps = psum[:, 4 + 2 * t:6 + 2 * t, :].rearrange("p b n -> p (b n)")
                for hd in range(RH):
                    d = slice(hd * RV, (hd + 1) * RV)
                    ins = dve.scalar_tensor_tensor(out=o_rows[:, t, d], in0=o_ps[:, d],
                                                   scalar=ostat[:, 1, t * RH + hd:t * RH + hd + 1],
                                                   in1=e_gate[:, t, d], op0=ALU.mult, op1=ALU.mult)
                    ins.then_inc(s["o_done"], 1)
            for b in range(4):
                dve.wait_ge(s["recT_high"], b + 1)
                part = (slice(None), slice(4 * (b % 2), 4 * (b % 2) + 4), slice(b // 2 * P, (b // 2 + 1) * P))
                dve.tensor_tensor(mix_lo[part], bank(b).rearrange("p (k t) -> p k t", k=4),
                                  mix_hi[part].bitcast(F32), ALU.subtract).then_inc(s["recT_low"], 1)
            add_mix(1, (4, 5, 6, 7))
            experts(1)

        @block.tensor
        def _(pe):
            def unit(u, n=0):
                pe.wait_ge(*arrival(u, n))
                return ring[:, RING_SLOT[u], :]

            def transposes(v, t):
                for half in range(2):
                    pe.wait_ge(s["xg_done"], TT * v + t + 1)
                    for k in range(4):
                        last = pe.transpose(bank(2 * t + half)[:, k * P:(k + 1) * P], xg[:, t, 4 * half + k::KD],
                                            ident[:, :])
                    last.then_inc(s["xT_psum"], 1)

            def keep_clock(n, b):
                for _ in range(n):
                    pe.matmul(bank(b)[:, 0:P], ident[:, :], ident[:, :], start=True, stop=True)

            pe.wait_ge(s["ident_done"], 1)
            keep_clock(START, 7)
            for t in range(TT):
                transposes(0, t)
            pe.wait_ge(s["xT_front"], 2)
            pe.wait_ge(s["xT_back"], 2)

            def w_cols(r, n):
                return r[:, 0:KD * n].rearrange("p (k n) -> p k n", k=KD)

            def tile_T(dst, lhs):
                for k in range(KD):
                    last = pe.matmul(dst, lhs(k), xT[:, k, :], start=(k == 0), stop=(k == KD - 1))
                return last

            def tile_rows(dst, t, rhs):
                for k in range(KD):
                    last = pe.matmul(dst, xT[:, k, t * P:(t + 1) * P], rhs(k), start=(k == 0), stop=(k == KD - 1))
                return last

            def three(dst, ready, a_hi, a_lo, b_hi, b_lo, a_first):
                for k in range(KD):
                    pe.matmul(dst, a_hi(k), b_hi(k), start=(k == 0), stop=False)
                    if a_first:
                        pe.matmul(dst, a_hi(k), b_lo(k), start=False, stop=False)
                    else:
                        pe.matmul(dst, a_lo(k), b_hi(k), start=False, stop=False)
                if ready is not None:
                    pe.wait_ge(*ready)
                for k in range(KD):
                    if a_first:
                        last = pe.matmul(dst, a_lo(k), b_hi(k), start=False, stop=(k == KD - 1))
                    else:
                        last = pe.matmul(dst, a_hi(k), b_lo(k), start=False, stop=(k == KD - 1))
                return last

            def proj(n):
                if n >= 2:
                    pe.wait_ge(s["proj_odd" if n % 2 else "proj_even"], (n - 2) // 2 + 1)
                b = bank(n % 2)
                if n < 4:
                    for i in range(2):
                        r = 2 * (n % 2) + i
                        pe.wait_ge(s["w_low_dve"], LOW_DVE["q" if n < 2 else "kv"] + r + 1)
                        last = three(b[:, i * T:(i + 1) * T], (s["x_lo_done"], TT) if n == 0 and i == 0 else None,
                                     lambda k: quarter_hi(r)[:, k, :],
                                     lambda k: (q_lo[:, r] if n < 2 else quarter_lo(U_KV, r))[:, k, :],
                                     lambda k: x_hi[:, k, :], lambda k: x_lo[:, :, k, :], False)
                elif n in (4, 5):
                    t = n - 4
                    pe.wait_ge(s["w_low_dve"], LOW_DVE["wg"] + 1)
                    last = three(b[:, 0:WG], None, lambda k: x_hi[:, k, t * P:(t + 1) * P],
                                 lambda k: x_lo[:, t, k, :], lambda k: wg_hi[:, k, :], lambda k: wg_lo[:, k, :], True)
                elif n in (6, 7, 8, 9):
                    for i in range(2):
                        r = 2 * (n - 6) + i
                        pe.wait_ge(s["w_low_pool"], LOW_POOL["att"] + r + 1)
                        last = three(b[:, i * T:(i + 1) * T], None,
                                     lambda k: quarter_hi(r)[:, k, :], lambda k: quarter_lo(U_QB, r)[:, k, :],
                                     lambda k: x_hi[:, k, :], lambda k: x_lo[:, :, k, :], False)
                else:
                    pe.wait_ge(s["w_low_pool"], LOW_POOL["att"] + 2 * (n - 6) + 2)
                    high, low = half_parts(U_QB, n - 6)
                    for t in range(TT):
                        last = three(b[:, t * 256:(t + 1) * 256], None, lambda k: x_hi[:, k, t * P:(t + 1) * P],
                                     lambda k: x_lo[:, t, k, :], lambda k: high[:, k, :],
                                     lambda k: low[:, k, :], True)
                last.then_inc(s["proj_psum"], 1)

            def free_units(k):
                pe.drain().then_inc(s["unit_used"], k)

            pe.wait_ge(s["x_lo_done"], 1)
            proj(0)
            proj(1)
            free_units(1)
            pe.wait_ge(s["cmp_small"], 64)
            for i in range(2):
                last = pe.transpose(bank(5)[:, i * LP:(i + 1) * LP], pe_rows[0:LP, i, :], ident[0:LP, 0:LP])
            last.then_inc(s["pe_psum"], 1)
            proj(2)
            proj(3)
            free_units(1)
            w1 = unit(U_CMP).rearrange("p (w j n) -> p w j n", w=2, n=P)
            pe.wait_ge(s["cmp_w1_rest"], 32)
            pe.wait_ge(s["kv2_done"], 7)
            pe.wait_ge(s["proj_even"], 2)
            pe.wait_ge(s["pe_done"], 1)
            for kv in range(2):
                for j in range(LP):
                    last = pe.matmul(bank(4)[:, 64 * kv:64 * kv + (NSA_G + 1) * NC]
                                     .rearrange("p (g c) -> p g c", g=NSA_G + 1),
                                     w1[:, kv, j, :],
                                     kv2[:, kv, :, 2 * j:2 * j + CMP_STRIDE * (NC - 1) + 1:CMP_STRIDE],
                                     start=(j == 0), stop=(j == LP - 1))
            last.then_inc(s["cmp_hidden"], 1)
            proj(4)
            pe.wait_ge(s["cmp_h_done"], 3)
            pe.matmul(bank(5)[0:DH, 0:2 * NC], w2[:, 0, :], cmp_h[:, 0, :], start=True, stop=True)
            for g in range(NSA_G):
                last = pe.matmul(bank(5)[:, 64 + g * DH:64 + (g + 1) * DH],
                                 hv4[:, g, :, :].rearrange("p a c -> p (a c)"), w2[:, 1, :], start=True, stop=True)
            last.then_inc(s["cmp_kv"], 1)
            proj(5)
            free_units(2)
            pe.wait_ge(s["cmp_kv_done"], 3)
            pe.wait_ge(s["proj_odd"], 1)

            def q_of(hd, t):
                g, i = divmod(hd, HPG)
                return qT[g * DH:(g + 1) * DH, i, t * P:(t + 1) * P]

            for t in range(TT):
                for hd in range(NSA_H):
                    g = hd // HPG
                    c = (t * HPG + hd % HPG) * NC
                    last = pe.matmul(bank(4 + g)[:, c:c + NC], q_of(hd, t), kcT[g * DH:(g + 1) * DH, :],
                                     start=True, stop=True)
            last.then_inc(s["cmp_scores"], 1)

            def nsa_scores(u):
                t, br, g, nk = u // 4, u // 2 % 2, u % 2, P * (u // 4 + 1)
                if u == 0:
                    pe.wait_ge(s["cmp_shifted"], 1)
                    pe.wait_ge(s["proj_odd"], 2)
                else:
                    pe.wait_ge(s["nsa_masked"], u)
                dst = psum[:, 4:6, :].rearrange("p b n -> p (b n)")
                for i in range(HPG):
                    last = pe.matmul(dst[:, i * nk:(i + 1) * nk], q_of(g * HPG + i, t),
                                     ksw[g * DH:(g + 1) * DH, br, 0:nk], start=True, stop=True)
                last.then_inc(s["nsa_scores"], 1)

            def nsa_T(u):
                pe.wait_ge(s["nsa_scaled"], u + 1)
                if u >= 1:
                    pe.wait_ge(s["nsa_pT_even"], u)
                if u >= 5:
                    pe.wait_ge(s["nsa_pT_odd"], u - 4)
                for kb in range(u // 4 + 1):
                    for i in range(HPG):
                        last = pe.transpose(bank(2 + kb)[:, i * P:(i + 1) * P],
                                            scores[:, u % 2, i, kb * P:(kb + 1) * P], ident[:, :])
                last.then_inc(s["nsa_pT"], 1)

            def nsa_pv(u):
                t, br, g = u // 4, u // 2 % 2, u % 2
                pe.wait_ge(s["nsa_pT_even"], u + 1)
                if u >= 4:
                    pe.wait_ge(s["nsa_pT_odd"], u - 3)
                acc = bank(6 + g).rearrange("p (a t) -> p a t", a=2)
                for kb in range(t + 1):
                    for par in range(2):
                        heads = probsT[:, u % 2, kb, :].rearrange("p (a two q) -> p a two q", two=2, q=P)
                        last = pe.matmul(acc[par * DH:(par + 1) * DH, :, t * P:(t + 1) * P],
                                         vsw[:, kb, br * P + g * DH:br * P + (g + 1) * DH], heads[:, :, par, :],
                                         start=False, stop=True, skip_group_check=True)
                last.then_inc(s["nsa_pv"], 1)

            nsa_scores(0)
            for u in range(8):
                if u + 1 < 8:
                    nsa_scores(u + 1)
                if u == 1:
                    pe.wait_ge(s["cmp_pT_done"], 1)
                    for i in range(HPG):
                        for g in range(NSA_G):
                            last = pe.matmul(bank(6 + g)[i % 2 * DH:(i % 2 + 1) * DH, i // 2 * T:(i // 2 + 1) * T],
                                             vc4[i * 32:(i + 1) * 32, g, :], pcT[i * 32:(i + 1) * 32, g, :],
                                             start=(i < 2), stop=True, skip_group_check=True)
                        if i % 2:
                            last.then_inc(s["cmp_pv"], 1)
                            pe.wait_ge(s["cmp_pv"], i // 2 + 1)
                if u >= 1:
                    nsa_pv(u - 1)
                if u in PROJ_AT:
                    proj(PROJ_AT[u])
                    if PROJ_AT[u] in (7, 9, 11):
                        free_units(1)
                if u == 0:
                    pe.wait_ge(s["cmp_p_done"], 2)
                    for g in range(NSA_G):
                        for t in range(TT):
                            last = pe.transpose(bank(5)[:, g * T + t * P:g * T + (t + 1) * P],
                                                cp[:, t, g * HPG:(g + 1) * HPG, :].rearrange("p h c -> p (h c)"),
                                                ident[:, :])
                    last.then_inc(s["cmp_pT"], 1)
                nsa_T(u)
            nsa_pv(7)

            def sb_z(hd):
                p0, j = hd % 2 * DH, hd // 2
                if hd == 0:
                    pe.wait_ge(s["nsa_masked"], 8)
                    pe.wait_ge(s["proj_odd"], 6)
                    pe.wait_ge(s["proj_even"], 6)
                if hd >= 4:
                    pe.wait_ge(s["sb_a"], hd - 3)
                z = bank(SB_BANKS[hd % 4])
                pe.matmul(z[:, 0:T], kbT[p0:p0 + DH, j, 0:P], qbT[p0:p0 + DH, j, :], start=True, stop=True,
                          skip_group_check=True)
                pe.matmul(z[:, T:T + P], kbT[p0:p0 + DH, j, P:T], qbT[p0:p0 + DH, j, P:T], start=False, stop=True,
                          skip_group_check=True).then_inc(s["sb_z_raw"], 1)

            def sb_mask(hd):
                z = bank(SB_BANKS[hd % 4])
                pe.wait_ge(s["sb_z_raw"], hd + 1)
                pe.matmul(z.rearrange("p (a n) -> p a n", a=2)[:, :, 0:P], ident_r[:, :], spread(before_r[:, :], 1, 2),
                          start=False, stop=True, skip_group_check=True).then_inc(s["sb_z"], 1)

            def sb_e(hd):
                pe.wait_ge(s["sb_t"], hd + 1)
                z, t = bank(SB_BANKS[hd % 4]), zt[:, hd % 3, :]
                pe.matmul(z[:, 0:T], later_own, t[:, 0:T], start=False, stop=True, skip_group_check=True)
                pe.matmul(z[:, P:T], later_all, t[:, T:T + P], start=False, stop=True, skip_group_check=True)
                pe.matmul(z[:, T:T + P], later_own, t[:, T:T + P], start=False, stop=True, skip_group_check=True)\
                    .then_inc(s["sb_e"], 1)

            def sb_pv(hd):
                pe.wait_ge(s["sb_a"], hd + 1)
                if hd == 0:
                    pe.wait_ge(s["nsa_pT_even"], 8)
                    pe.wait_ge(s["nsa_pT_odd"], 4)
                p0, j = hd % 2 * DH, hd // 2
                acc = bank(2 + j // 2)[p0:p0 + DH, j % 2 * T:(j % 2 + 1) * T]
                w, p = vb[:, :, hd * DH:(hd + 1) * DH], za[:, hd % 2, :]
                pe.matmul(acc, w[:, 0, :], p[:, 0:T], start=(hd % 4 < 2), stop=True, skip_group_check=True)
                pe.matmul(acc[:, P:T], w[:, 1, :], p[:, T:T + P], start=False, stop=True, skip_group_check=True)\
                    .then_inc(s["sb_pv"], 1)

            sb_z(0)
            sb_z(1)
            sb_mask(0)
            sb_mask(1)
            for hd in range(SB_H):
                if hd + 2 < SB_H:
                    sb_z(hd + 2)
                sb_e(hd)
                if hd + 2 < SB_H:
                    sb_mask(hd + 2)
                if hd >= 1:
                    sb_pv(hd - 1)
            sb_pv(SB_H - 1)

            def mix(l, base, banks, tile_ready=None):
                for m in range(4):
                    pe.wait_ge(s["w_low_pool"], LOW_POOL[f"mix{l}"] + 2 * m + 2)
                    high, low = half_parts(base, m)
                    for t in range(TT):
                        if m == 0 and tile_ready:
                            tile_ready(t)
                        if m >= 2:
                            pe.wait_ge(s["h_done"], 12 * l + 2 * (m - 2) + t + 1)
                        three(bank(banks[m % 2 * 2 + t])[:, 0:256], None,
                              lambda j: mix_hi[:, j, t * P:(t + 1) * P], lambda j: mix_lo[:, j, t * P:(t + 1) * P],
                              lambda j: high[:, j, :], lambda j: low[:, j, :], True).then_inc(s["mix_psum"], 1)
                    if m % 2:
                        free_units(1)
                for t in range(TT):
                    transposes(2 * l + 1, t)

            pe.wait_ge(s["oT_high"], 2)
            pe.wait_ge(s["oT_low"], 4)
            pe.wait_ge(s["sb_a"], SB_H)
            mix(0, U_WO, (0, 1, 4, 5))

            def route(l):
                pe.wait_ge(s["route_loaded"], 64 * (l + 1))
                for t in range(TT):
                    pe.wait_ge(s["xT_front"], TT * (2 * l + 1) + t + 1)
                    pe.wait_ge(s["xT_back"], TT * (2 * l + 1) + t + 1)
                    last = tile_rows(bank(4 + t)[:, 0:GR + NE], t, lambda k: w_route[:, k, :])
                last.then_inc(s["route_psum"], 1)
                keep_clock(ROUTE, 3)
                pe.wait_ge(s["member_done"], l + 1)
                both = member[:, :, :].rearrange("p t e -> p (t e)")
                pe.matmul(bank(6)[:, 0:2 * NE], earlier[:, :], both, start=True, stop=True, skip_group_check=True)
                pe.matmul(bank(6)[:, NE:2 * NE], ones[:, :], member[:, 0, :], start=False, stop=True,
                          skip_group_check=True).then_inc(s["slot_psum"], 1)
                pe.matmul(bank(7)[:, 0:NE], ones[:, :], member[:, 0, :], start=True, stop=False)
                pe.matmul(bank(7)[:, 0:NE], ones[:, :], member[:, 1, :], start=False, stop=True)\
                    .then_inc(s["total_psum"], 1)

            def combine(l, m):
                pe.wait_ge(s[f"shareT{l}"], m + 1)
                pe.wait_ge(s[f"y_rows{l}"], 2 * m + 2)
                for i, b in enumerate(COMBINE_BANKS):
                    t, half = divmod(i, 2)
                    pe.matmul(bank(b), shareT[:, t, :], y_rows[:, half * 512:(half + 1) * 512],
                              start=True, stop=True).then_inc(s[f"combined{l}"], 1)

            def quad(l, n, before):
                static = isinstance(n, int)
                pe.wait_ge(s[f"slots{l}"], n + 1)
                if not static:
                    pe.wait_ge(s[f"added{l}"], 4 * n - 4)
                for k in range(KD):
                    for t in range(TT):
                        last = pe.matmul(bank(k // 4)[:, k % 4 * P:(k % 4 + 1) * P], xg[:, t, k::KD],
                                         slots[:, t].rearrange("p e c -> p (e c)"), start=(t == 0), stop=(t == TT - 1))
                    if k % 4 == 3:
                        last.then_inc(s[f"gathered{l}"], 1)

                def weights(i):
                    if static and n == 1 and i < SPARE:
                        pe.wait_ge(s[f"spare{i}_loaded"], 32 * (l + 1))
                        return spare[:, i, :], False
                    if static:
                        return unit(BASE_MOE[l] + i + (NU - SPARE) * n, before), True
                    return unit(BASE_LOOP[l] + i, n - 2 + before), True

                pe.wait_ge(s[f"gatheredT{l}"], 2 * n + 2)
                for c in range(KD // 2):
                    w, in_ring = weights(c)
                    w = w.rearrange("p (w e r f) -> p w e r f", w=2, e=QE, r=2)
                    for r in range(2):
                        k = 2 * c + r
                        for e in range(QE):
                            last = pe.matmul(bank(3)[e * CAP:(e + 1) * CAP, :].rearrange("p (w f) -> p w f", w=2),
                                             gatheredT[:, k, e * CAP:(e + 1) * CAP], w[:, :, e, r, :],
                                             start=(k == 0), stop=(k == KD - 1))
                    if c < KD // 2 - 1 and in_ring:
                        last.then_inc(s["unit_used"], 1)
                last.then_inc(s[f"gate_up{l}"], 1)
                if in_ring:
                    pe.wait_ge(s[f"gate_up{l}"], n + 1)
                    pe.sem_inc(s["unit_used"], 1)
                if not (static and n == 0):
                    combine(l, n - 1)
                pe.wait_ge(s[f"slots_share{l}"], n + 1)
                for t in range(TT):
                    pe.transpose(bank(4)[:, FF + t * P:FF + (t + 1) * P],
                                 slots_share[:, t].rearrange("p e c -> p (e c)"), ident[:, :])
                pe.wait_ge(s[f"hid{l}"], 2 * n + 2)
                for j in range(KF):
                    last = pe.transpose(bank(4)[:, j * P:(j + 1) * P], hid[:, j::KF], ident[:, :])
                last.then_inc(s[f"hid_psum{l}"], 1)
                pe.wait_ge(s[f"hidT{l}"], n + 1)
                for j in range(KF):
                    w, in_ring = weights(KD // 2 + j)
                    w = w.rearrange("p (e n) -> p e n", e=QE)
                    for c in range(2):
                        for e in range(QE):
                            last = pe.matmul(bank(5 + c)[e * CAP:(e + 1) * CAP, :],
                                             hidT[:, j, e * CAP:(e + 1) * CAP], w[:, e, c * 512:(c + 1) * 512],
                                             start=(j == 0), stop=(j == KF - 1))
                    if j == 0:
                        last.then_inc(s["unit_used"], 1)
                last.then_inc(s[f"down{l}"], 1)
                pe.wait_ge(s[f"down{l}"], n + 1)
                pe.sem_inc(s["unit_used"], 1)

            def experts(l, before):
                route(l)
                for q in range(2):
                    quad(l, q, before)
                with pe.Fori(2, NQ) as q:
                    quad(l, q, before)
                pe.wait_ge(s["passes_ready"], l + 1)
                more = pe.value_load(passes[l][0:1, 0:1], min_val=0, max_val=PASS_MAX - 1)
                with pe.If(more > 0):
                    with pe.Fori(0, more) as r:
                        with pe.Fori(0, NQ) as q:
                            quad(l, q + NQ * (r + 1), before)
                combine(l, NQ * more + NQ - 1)
                if l == 0:
                    keep_clock(NORM, 3)
                return NQ * more

            before = experts(0, 0)

            for t in range(TT):
                transposes(2, t)
            pe.wait_ge(s["rec_small"], 32)
            pe.transpose(bank(7)[:, 0:2 * RH], lb_rows[0:2 * RH, :], ident[0:2 * RH, 0:2 * RH])\
                .then_inc(s["lb_psum"], 1)
            pe.wait_ge(s["xT_front"], 6)
            pe.wait_ge(s["xT_back"], 6)

            for m in range(8):
                if m == 3:
                    pe.wait_ge(s["lb_diff"], 1)
                b = bank(m + 4 if m < 4 else m - 4)
                for i in range(2):
                    r = 2 * m + i
                    if i:
                        pe.wait_ge(s["w_low_pool"], LOW_POOL["rec"] + m + 1)
                    else:
                        pe.wait_ge(s["w_low_dve"], LOW_DVE["rec"] + m + 1)
                    three(b[:, i * T:(i + 1) * T], (s["x_lo_done"], 2 * TT) if r == 0 else None,
                          lambda k: quarter_hi(r)[:, k, :], lambda k: quarter_lo(BASE_REC, r)[:, k, :],
                          lambda k: x_hi[:, k, :], lambda k: x_lo[:, :, k, :], False).then_inc(s["rec_psum"], 1)
                if m % 2:
                    free_units(1)
            for m in range(8, 16):
                if m == 8:
                    pe.wait_ge(s["rec_f"], 4)
                if m >= 12:
                    pe.wait_ge(s["rec_v"], m - 11)
                pe.wait_ge(s["w_low_dve"], LOW_DVE["rec"] + m + 1)
                pe.wait_ge(s["w_low_pool"], LOW_POOL["rec"] + m + 1)
                high, low = half_parts(BASE_REC, m)
                for t in range(TT):
                    three(bank(4 + m % 4)[:, t * 256:(t + 1) * 256], None,
                          lambda k: x_hi[:, k, t * P:(t + 1) * P], lambda k: x_lo[:, t, k, :],
                          lambda k: high[:, k, :], lambda k: low[:, k, :], True).then_inc(s["rec_psum"], 1)
                if m % 2:
                    free_units(1)

            pe.wait_ge(s["rec_kout"], 2)
            pe.wait_ge(s["rec_q"], 4)
            pe.wait_ge(s["rec_v"], 4)
            for b in range(4):
                t, half = b // 2, b % 2
                for i in range(4):
                    last = pe.transpose(bank(b)[:, i * P:(i + 1) * P], rD[:, 4 * half + i, t * P:(t + 1) * P],
                                        ident[:, :])
                last.then_inc(s["ko_psum"], 1)
            pe.wait_ge(s["rec_kin"], 2)
            pe.wait_ge(s["rec_qin"], 4)
            for b in range(4):
                t, half = b // 2, b % 2
                pe.wait_ge(s["rec_gate"], b + 1)
                for i in range(4):
                    hd = 4 * half + i
                    last = pe.matmul(bank(4 + b)[:, i * P:(i + 1) * P], r2[:, hd, t * P:(t + 1) * P],
                                     r1[:, hd, t * P:(t + 1) * P], start=True, stop=True)
                last.then_inc(s["a_psum"], 1)

            def state(c):
                if c == 2:
                    pe.wait_ge(s["state_done"], RH)
                p0, t = c % 2 * CH, c // 2
                kv = psum[:, 2 * (c % 2):2 * (c % 2) + 2, :].rearrange("p b n -> p (b n)")
                for hd in range(RH):
                    d = slice(hd * P, (hd + 1) * P)
                    last = pe.matmul(kv[:, d], koR[p0:p0 + CH, t, d], rv[p0:p0 + CH, t, d], start=True, stop=True)
                last.then_inc(s["state_psum"], 1)

            pe.wait_ge(s["a_psum"], 4)
            pe.nop().then_inc(s["rec_kin_used"], 1)
            pe.wait_ge(s["ko_done"], 4)
            for c in range(NCH - 1):
                state(c)
            aMv = aM.rearrange("p h t -> p (h t)").rearrange("p (g t) -> p g t", t=P)
            for t in range(TT):
                pe.wait_ge(s["rec_a_masked"], 4)
                acc = psum[:, 4 + 2 * t:6 + 2 * t, :].rearrange("p b n -> p (b n)")
                for hd in range(RH):
                    d = slice(hd * P, (hd + 1) * P)
                    pe.matmul(acc[:, d], aMv[:, t * RH + hd, :], rv[:, t, d], start=(hd % 4 == 0), stop=True,
                              skip_group_check=True)
                for c in (2 * t, 2 * t + 1):
                    if c == 0:
                        continue
                    pe.wait_ge(s["state_done"], RH * c)
                    for hd in range(RH):
                        d = slice(hd * P, (hd + 1) * P)
                        last = pe.matmul(acc[c % 2 * CH:(c % 2 + 1) * CH, d], r3[:, hd, c * CH:(c + 1) * CH],
                                         states[c - 1][:, d], start=False, stop=True, skip_group_check=True)
                last.then_inc(s["o_psum"], 1)
            pe.wait_ge(s["o_psum"], TT)
            pe.nop().then_inc(s["a_used"], 1)
            for b in range(4):
                t, half = b // 2, b % 2
                pe.wait_ge(s["o_done"], 4 * b + 4)
                for i in range(4):
                    d = (4 * half + i) * P
                    last = pe.transpose(bank(b)[:, i * P:(i + 1) * P], o_rows[:, t, d:d + P], ident[:, :])
                last.then_inc(s["recT_psum"], 1)
            mix(1, BASE_REC + 8, (4, 5, 6, 7), lambda t: pe.wait_ge(s["recT_low"], 2 * t + 2))
            experts(1, before)

        assert max(att_end, rec_end, moe_end) <= arena_t.shape[1], (att_end, rec_end, moe_end)


_INS = ["x", "norm_mix", "norm_ffn", "att_w_in", "att_w_out", "cmp_pe_k", "cmp_w1_k", "cmp_w2_k", "cmp_pe_v",
        "cmp_w1_v", "cmp_w2_v", "rec_w_in", "rec_lb_logits", "rec_gnorm", "rec_w_out", "moe_w_grp", "moe_b_grp",
        "moe_w_exp", "moe_b_exp", "moe_w_gate", "moe_w_up", "moe_w_down", "final_norm"]


def kernel(**inputs):
    import numpy as np
    import concourse.bacc as bacc
    from concourse.bass_utils import run_bass_kernel_spmd

    nc = bacc.Bacc("TRN2", target_bir_lowering=False, num_devices=1)
    arrays, args = {}, []
    for name in _INS:
        a = np.ascontiguousarray(inputs[name])
        arrays[f"in_{name}"] = a
        args.append(nc.dram_tensor(f"in_{name}", a.shape, mybir.dt.from_np(a.dtype), kind="ExternalInput").ap())
    args.append(nc.dram_tensor("out", (1, T, D), F32, kind="ExternalOutput").ap())
    hybrid_trunk(nc, *args)
    return run_bass_kernel_spmd(nc, [arrays], core_ids=[0]).results[0]["out"]
```
